# Optimizing a Trainium2 kernel written in Bass

```python
import math
import jax, jax.numpy as jnp
from jax import lax
import numpy as np

D_MODEL = 1024
BATCH = 1
SEQ = 2048
DEPTH = 1

MIX_WIDTH = D_MODEL
GROUP_WIDTH = MIX_WIDTH // 4
ATTN_HEADS = 4
ATTN_QK_DIM = GROUP_WIDTH // ATTN_HEADS // 2
ATTN_V_DIM = 2 * ATTN_QK_DIM
Q_BLOCK = 128
CONF_KERNEL = 31
SHORT_KERNEL = 3
POOL_WINDOWS = (2, 4, 8, 16)
POOL_GROUPS = len(POOL_WINDOWS)
POOL_GROUP_DIM = GROUP_WIDTH // POOL_GROUPS
D_FF = 4 * D_MODEL
EPS = 1e-6
N_MOD = 6

A_QK = ATTN_HEADS * 2 * ATTN_QK_DIM
A_V = ATTN_HEADS * ATTN_V_DIM
B_IN = 2 * GROUP_WIDTH
C_IN = 3 * GROUP_WIDTH
D_IN = GROUP_WIDTH
IN_WIDTH = 2 * A_QK + A_V + B_IN + C_IN + D_IN
IN_SPLITS = (A_QK, 2 * A_QK, 2 * A_QK + A_V, 2 * A_QK + A_V + B_IN, 2 * A_QK + A_V + B_IN + C_IN)

kernel_name = 'hybrid_parallel_headgroup_adaln_trunk'

def rms_norm(x, g):
    xf = x.astype(jnp.float32)
    y = xf * lax.rsqrt(jnp.mean(xf * xf, axis=-1, keepdims=True) + EPS)
    return (y * g.astype(jnp.float32)).astype(x.dtype)

def layer_norm(x, g, b):
    xf = x.astype(jnp.float32)
    mu = jnp.mean(xf, axis=-1, keepdims=True)
    var = jnp.mean(jnp.square(xf - mu), axis=-1, keepdims=True)
    y = (xf - mu) * lax.rsqrt(var + EPS)
    return (y * g.astype(jnp.float32) + b.astype(jnp.float32)).astype(x.dtype)

def causal_dwconv(x, w):
    k = w.shape[0]
    ch = x.shape[-1]
    return lax.conv_general_dilated(
        x, w[:, None, :].astype(x.dtype), window_strides=(1,), padding=[(k - 1, 0)],
        dimension_numbers=('NWC', 'WIO', 'NWC'), feature_group_count=ch)

def diff_attention(q, k, v, lam_p, q_g, k_g, sub_g, lam_init):
    b, s, _ = q.shape
    q = rms_norm(q.reshape(b, s, ATTN_HEADS, 2, ATTN_QK_DIM), q_g).transpose(0, 2, 3, 1, 4)
    k = rms_norm(k.reshape(b, s, ATTN_HEADS, 2, ATTN_QK_DIM), k_g).transpose(0, 2, 3, 1, 4)
    v = v.reshape(b, s, ATTN_HEADS, ATTN_V_DIM).transpose(0, 2, 1, 3)
    lp = lam_p.astype(jnp.float32)
    lam = jnp.exp(jnp.sum(lp[0] * lp[1])) - jnp.exp(jnp.sum(lp[2] * lp[3])) + lam_init
    scale = ATTN_QK_DIM ** -0.5
    nb = s // Q_BLOCK
    qb = jnp.moveaxis(q.reshape(b, ATTN_HEADS, 2, nb, Q_BLOCK, ATTN_QK_DIM), 3, 0)
    starts = jnp.arange(nb) * Q_BLOCK
    kpos = jnp.arange(s)

    def block(args):
        qi, st = args
        sc = jnp.einsum('bhmqd,bhmkd->bhmqk', qi, k).astype(jnp.float32) * scale
        mask = kpos[None, :] <= (st + jnp.arange(Q_BLOCK))[:, None]
        p = jax.nn.softmax(jnp.where(mask, sc, -jnp.inf), axis=-1)
        a = p[:, :, 0] - lam * p[:, :, 1]
        return jnp.einsum('bhqk,bhkd->bhqd', a.astype(v.dtype), v)

    out = lax.map(block, (qb, starts))
    out = jnp.moveaxis(out, 0, 2).reshape(b, ATTN_HEADS, s, ATTN_V_DIM)
    out = rms_norm(out, sub_g) * (1.0 - lam_init)
    return out.transpose(0, 2, 1, 3).reshape(b, s, ATTN_HEADS * ATTN_V_DIM)

def conformer_conv(u, dw_w, dw_b, ln_g, ln_b):
    val, gate = jnp.split(u, 2, axis=-1)
    h = val * jax.nn.sigmoid(gate)
    h = causal_dwconv(h, dw_w) + dw_b
    return jax.nn.silu(layer_norm(h, ln_g, ln_b))

def short_gated_conv(u, w):
    bg, cg, xc = jnp.split(u, 3, axis=-1)
    return bg * causal_dwconv(cg * xc, w)

def multiscale_pool(u, w_pool, scale):
    b, s, _ = u.shape
    xf = u.reshape(b, s, POOL_GROUPS, POOL_GROUP_DIM).astype(jnp.float32)
    cs = jnp.concatenate([jnp.zeros((b, 1, POOL_GROUPS, POOL_GROUP_DIM), jnp.float32),
                          jnp.cumsum(xf, axis=1)], axis=1)
    t = np.arange(s)
    pooled = []
    for g, w in enumerate(POOL_WINDOWS):
        lo = np.maximum(t + 1 - w, 0)
        cnt = jnp.asarray(np.minimum(t + 1, w).astype(np.float32))
        pooled.append((cs[:, 1:, g] - cs[:, lo, g]) / cnt[None, :, None])
    y = (jnp.stack(pooled, axis=2) - xf).astype(u.dtype)
    y = jnp.einsum('bsgc,gcd->bsgd', y, w_pool)
    return y.reshape(b, s, GROUP_WIDTH) * scale

def setup_inputs(seed: int = 0) -> dict:
    key = jax.random.key(seed)
    ks = jax.random.split(key, 24)
    f32 = jnp.float32
    nrm = lambda k, shape, sd: jax.random.normal(k, shape, f32) * sd
    L = DEPTH
    return {
        'x': nrm(ks[0], (BATCH, SEQ, D_MODEL), 1.0),
        'c': nrm(ks[1], (BATCH, D_MODEL), 1.0),
        'w_ada': nrm(ks[2], (L, D_MODEL, N_MOD * D_MODEL), D_MODEL ** -0.5),
        'b_ada': nrm(ks[3], (L, N_MOD * D_MODEL), 0.02),
        'norm1_g': 1.0 + nrm(ks[4], (L, D_MODEL), 0.02),
        'norm2_g': 1.0 + nrm(ks[5], (L, D_MODEL), 0.02),
        'w_in': nrm(ks[6], (L, D_MODEL, IN_WIDTH), D_MODEL ** -0.5),
        'w_out': nrm(ks[7], (L, MIX_WIDTH, D_MODEL), MIX_WIDTH ** -0.5),
        'q_norm_g': 1.0 + nrm(ks[8], (L, ATTN_QK_DIM), 0.02),
        'k_norm_g': 1.0 + nrm(ks[9], (L, ATTN_QK_DIM), 0.02),
        'lam_params': nrm(ks[10], (L, 4, ATTN_QK_DIM), 0.1),
        'attn_sub_g': 1.0 + nrm(ks[11], (L, ATTN_V_DIM), 0.02),
        'conf_dw_w': nrm(ks[12], (L, CONF_KERNEL, GROUP_WIDTH), CONF_KERNEL ** -0.5),
        'conf_dw_b': nrm(ks[13], (L, GROUP_WIDTH), 0.02),
        'conf_ln_g': 1.0 + nrm(ks[14], (L, GROUP_WIDTH), 0.02),
        'conf_ln_b': nrm(ks[15], (L, GROUP_WIDTH), 0.02),
        'short_conv_w': nrm(ks[16], (L, SHORT_KERNEL, GROUP_WIDTH), SHORT_KERNEL ** -0.5),
        'pool_w': nrm(ks[17], (L, POOL_GROUPS, POOL_GROUP_DIM, POOL_GROUP_DIM), POOL_GROUP_DIM ** -0.5),
        'pool_scale': 1.0 + nrm(ks[18], (L, GROUP_WIDTH), 0.1),
        'w_ff1': nrm(ks[19], (L, D_MODEL, D_FF), D_MODEL ** -0.5),
        'w_ff2': nrm(ks[20], (L, D_FF, D_MODEL), D_FF ** -0.5),
    }

def reference(x, c, w_ada, b_ada, norm1_g, norm2_g, w_in, w_out, q_norm_g, k_norm_g, lam_params,
              attn_sub_g, conf_dw_w, conf_dw_b, conf_ln_g, conf_ln_b, short_conv_w, pool_w, pool_scale,
              w_ff1, w_ff2):
    c_act = jax.nn.silu(c)
    for l in range(DEPTH):
        lam_init = 0.8 - 0.6 * math.exp(-0.3 * l)
        mod = (c_act @ w_ada[l] + b_ada[l])[:, None, :]
        sh1, sc1, g1, sh2, sc2, g2 = jnp.split(mod, N_MOD, axis=-1)
        h = rms_norm(x, norm1_g[l]) * (1.0 + sc1) + sh1
        proj = h @ w_in[l]
        qa, ka, va, ub, uc, ud = jnp.split(proj, IN_SPLITS, axis=-1)
        ya = diff_attention(qa, ka, va, lam_params[l], q_norm_g[l], k_norm_g[l], attn_sub_g[l], lam_init)
        yb = conformer_conv(ub, conf_dw_w[l], conf_dw_b[l], conf_ln_g[l], conf_ln_b[l])
        yc = short_gated_conv(uc, short_conv_w[l])
        yd = multiscale_pool(ud, pool_w[l], pool_scale[l])
        mix = jnp.concatenate([ya, yb, yc, yd], axis=-1) @ w_out[l]
        x = x + g1 * mix
        h = rms_norm(x, norm2_g[l]) * (1.0 + sc2) + sh2
        x = x + g2 * (jnp.square(jax.nn.relu(h @ w_ff1[l])) @ w_ff2[l])
    return x


_drawn_inputs = setup_inputs


def setup_inputs(seed=0):
    import zlib

    import numpy as np

    out = dict(_drawn_inputs(seed))
    spreads = {}
    factors = {'norm1_g': 3.268,
     'norm2_g': 14.17,
     'q_norm_g': 23.894,
     'k_norm_g': 22.683,
     'lam_params': 8.0,
     'attn_sub_g': 64.0,
     'conf_dw_b': 64.0,
     'conf_ln_g': 64.0,
     'conf_ln_b': 64.0,
     'pool_scale': 8.0}
    for name, (base, spread) in spreads.items():
        noise = np.random.default_rng([zlib.crc32(name.encode()), seed]).standard_normal(out[name].shape)
        drawn = base * np.exp(spread * noise) if base else spread * noise
        out[name] = __import__('jax').numpy.asarray(drawn.astype(out[name].dtype))
    for name, factor in factors.items():
        out[name] = (out[name] * factor).astype(out[name].dtype)
    return out
```

```python
from contextlib import ExitStack

import concourse.bass as bass
from concourse import mybir

F32 = mybir.dt.float32
F32R = mybir.dt.float32r
ALU = mybir.AluOpType
ACT = mybir.ActivationFunctionType
AX = mybir.AxisListType

P = 128
SEQ = 2048
D = 1024
DC = D // P
NT = SEQ // P
HALF = SEQ // 2
HT = HALF // P
BLK = 512
NB = HALF // BLK
GW = 256
GC = GW // P
D_FF = 4 * D
HEADS, QKD, VD = 4, 32, 64
MAPS = 2 * HEADS
SCALE = QKD ** -0.5
LAM_INIT = 0.2
EPS = 1e-6
TAPS = 31
STAPS = 3
POOL_HALO = 16
NEG = -1.0e30

Q0, K0, V0, VAL0, GATE0, BG0, CG0, XC0, UD0 = range(0, 9 * GW, GW)
ITEMS = [("q", Q0), ("k", K0), ("v", V0), ("ud", UD0), ("gate", GATE0), ("val", VAL0),
         ("cg", CG0), ("xc", XC0), ("bg", BG0)]
NI = len(ITEMS)
ITEM = DC * GW
KC_OUT = 4
FG = D_FF // GW
C_ITEMS = KC_OUT + 2 * FG
C_FOLDS = KC_OUT + FG
BROADCASTS = 10

R_C, R_B, R_N1, R_N2 = 0, 8, 56, 64
R_DWB, R_LNG, R_LNB, R_PSC, R_END1 = 72, 74, 76, 78, 80
R_DWW, R_SW, R_END2 = 0, 62, 68


def projections():
    chan = [(b, c) for b in range(NB) for c in range(GC)]
    ln = lambda h: [("ln", h, b, s) for b in range(NB) for s in (0, 1)]
    out = []
    for h in range(2):
        out += [("qk", h, t, 0) for t in range(HT)] + [("v", h, t, 0) for t in range(0, HT, 2)]
        out += ln(0) if h else []
        for kind in ("ud", "gate", "pool", "val", "cg", "xc", "bg"):
            out += [(kind, h, c, b) for b, c in chan]
    return out + ln(1)


UNITS = NT * HEADS
STEPS = UNITS + 7


def fills_of(u):
    out = [("stack", u // HEADS + 1, u % HEADS)] if u // HEADS + 1 < NT else []
    return out + [("att", j, f) for j in range(NT // 4) for f in range(GC) if u == 16 * j + 21 + f]


FILLS = [("stack", 0, f) for f in range(4)] + [x for u in range(STEPS) for x in fills_of(u)]
FILL_NO = {x: n for n, x in enumerate(FILLS)}


def fills_at(u):
    return [FILL_NO[x] for x in fills_of(u)]


def splits_at(u):
    return [(n, a) for n in range(1, NT) for a in range(2) if u == max(0, 4 * n - 6 + 2 * a)]


def sc_chunks(i):
    n = (i + 1) * P
    return [(c0, min(BLK, n - c0)) for c0 in range(0, n, BLK)]


def at_groups(u):
    n = u // HEADS + 1
    return [(k0, min(4, n - k0)) for k0 in range(0, n, 4)]


def running(counts):
    out = [0]
    for n in counts:
        out.append(out[-1] + n)
    return out


SC_NO = running(2 * len(sc_chunks(u // HEADS)) for u in range(UNITS))
AT_NO = running(len(at_groups(u)) for u in range(UNITS))


def trunk(nc, x, c, w_ada, b_ada, norm1_g, norm2_g, w_in, w_out, q_norm_g, k_norm_g, lam_params,
          attn_sub_g, conf_dw_w, conf_dw_b, conf_ln_g, conf_ln_b, short_conv_w, pool_w, pool_scale,
          w_ff1, w_ff2, out):
    ctx = ExitStack()
    with ctx:
        KB = 1024
        base = 16512

        def sb(name, kb, shape, dt=F32):
            return nc.alloc_sbuf_tensor_at("sb_" + name, shape, dt, offset=base + int(kb * KB))

        def sem(name):
            return ctx.enter_context(nc.semaphore(name))

        qkv_d = nc.dram_tensor("qkv_scratch", (SEQ, 3 * GW), F32).ap()
        mix_d = nc.dram_tensor("mix_scratch", (D, SEQ), F32).ap()

        ident = sb("ident", 0, [P, P])
        ident_r = sb("ident_r", 0.5, [P, P], F32R)
        mask_r = sb("mask_r", 1, [P, P], F32R)
        ones_mean = sb("ones_mean", 1.5, [P, P])
        pool_blk = sb("pool_blk", 2, [P, GC, P])
        col1 = sb("col1", 3, [P, R_END1])
        col2 = sb("col2", 3.375, [P, R_END2])
        gain_qk = sb("gain_qk", 3.75, [P, 2, QKD])
        gain_sub = sb("gain_sub", 4, [P, VD])
        lam_in = sb("lam_in", 4.25, [P, 4, QKD])
        small = sb("small", 4.75, [P, 96])
        silu_c = sb("silu_c", 5.125, [P, DC])
        gain1 = sb("gain1", 5.1875, [P, DC])
        shift1 = sb("shift1", 5.25, [P, DC])
        gain2 = sb("gain2", 5.3125, [P, DC])
        shift2 = sb("shift2", 5.375, [P, DC])
        inv_win = sb("inv_win", 5.4375, [P, GC])
        inv_first = sb("inv_first", 5.5, [P, GC, POOL_HALO])
        bn = sb("bn", 5.6875, [P, 2, 6])
        stat = sb("stat", 5.75, [P, 16])
        eps_col, lam_neg = small[:, 0:1], small[:, 1:2]
        gate_row = sb("gate_row", 6, [P, 2, D])
        h_hi = sb("h_hi", 14, [P, DC, HALF], F32R)
        h_lo = sb("h_lo", 46, [P, DC, HALF], F32R)
        w_hi = [sb(f"w_hi{s}", 78 + 16 * s, [P, ITEM], F32R) for s in range(4)]
        w_lo = [sb(f"w_lo{s}", 86 + 16 * s, [P, ITEM], F32R) for s in range(4)]
        w_raw = sb("w_raw", 142, [P, ITEM])
        gated = sb("gated", 126, [P, GC, HALF])
        acc = sb("acc", 134, [P, GC, HALF])
        at = 150
        x_in = [sb(f"x_in{s}", at + 4 * s, [P, D]) for s in range(2)]
        h_tmp = sb("h_tmp", 158, [P, DC, P])
        conf = sb("conf", 162, [P, GC, TAPS - 1 + HALF])
        halo2 = sb("halo2", 170.25, [P, GC, 2])
        prod = sb("prod", 170.5, [P, GC, 2 + HALF])
        pool_in = sb("pool_in", 170.5, [P, GC, HALF])
        ln_sq = sb("ln_sq", 170.5, [P, GC, BLK])
        ln_sig = sb("ln_sig", 174.5, [P, BLK])
        ln_rs = sb("ln_rs", 176.5, [P, BLK])
        stage = [sb(f"stage{s}", 179 + 2 * s, [P, BLK]) for s in range(2)]
        ud = sb("ud", 183, [P, GC, POOL_HALO + BLK])
        win_a = sb("win_a", 187.25, [P, POOL_HALO + BLK])
        win_b = sb("win_b", 189.5, [P, POOL_HALO + BLK])
        ada = sb("ada", 191.75, [P, 2 * D])
        qk_sq = sb("qk_sq", 199.75, [P, BLK])
        qkv_out = [sb(f"qkv_out{s}", 201.75 + 2 * s, [P, BLK]) for s in range(2)]
        ada_first = [sb(f"ada_first{s}", k, [P, 2 * D]) for s, k in enumerate((126, 134, 162, 171))]
        table1 = sb("table1", 183, [R_END1, P])
        table2 = sb("table2", 183.5, [R_END2, P])
        k_stack = sb("k_stack", 14, [P, MAPS, SEQ], F32R)
        scores = [sb(f"scores{s}", 94 + 16 * s, [P, 2, SEQ]) for s in range(3)]
        v_sb = sb("v_sb", 150, [P, NT, GW])
        att = sb("att", 166, [P, NT, GW])
        q_stack = [sb(f"q_stack{s}", 182 + 4 * s, [P, MAPS, P], F32R) for s in range(2)]
        q_split = sb("q_split", 190, [P, MAPS, 4, QKD], F32R)
        k_split = sb("k_split", 194, [P, MAPS, 4, QKD], F32R)
        qk_in = [sb(f"qk_in{s}", 198 + 2 * s, [P, 2, GW]) for s in range(2)]
        a_t = [sb(f"a_t{s}", 202 + 2 * s, [P, BLK]) for s in range(2)]
        att_sq = sb("att_sq", 78, [P, 4, GW])
        att_t = [sb(f"att_t{s}", 82 + 4 * s, [P, GC, BLK]) for s in range(2)]
        bst = sb("bst", 90, [P, 3, 24])
        inv_s = sb("inv_s", 90.5, [P, 4])
        ams = sb("ams", 91, [P, 48])
        x_new = sb("x_new", 150, [P, HT, D])
        u_hi = sb("u_hi", 182, [P, 2, HALF], F32R)
        u_lo = sb("u_lo", 190, [P, 2, HALF], F32R)
        mix_in = [sb(f"mix_in{s}", 182 + 4 * s, [P, DC, P]) for s in range(2)]
        relu_t = [sb(f"relu_t{s}", 198 + 2 * s, [P, BLK]) for s in range(4)]
        xn2 = sb("xn2", 198, [P, D])
        h_tmp2 = sb("h_tmp2", 202, [P, DC, P])

        psum = ctx.enter_context(nc.psum_tensor("ps", [P, 8, BLK], F32))
        ps_t = psum[:, 0:2, :].rearrange("p a b -> p (a b)").rearrange("p (k t) -> p k t", t=P)

        tab_ld, bc_ld, dve_chain, act_chain, pool_chain = [sem(n) for n in (
            "tab_ld", "bc_ld", "dve_chain", "act_chain", "pool_chain")]
        const_ready, tab_t, tab_col, sigc_ready, siluc_ready = [sem(n) for n in (
            "const_ready", "tab_t", "tab_col", "sigc_ready", "siluc_ready")]
        ada0_ld = [sem(f"ada0_ld{s}") for s in range(4)]
        ada0_used, mod1_mm, mod1_ready = sem("ada0_used"), sem("mod1_mm"), sem("mod1_ready")
        ada_ld, ada_used = sem("ada_ld"), sem("ada_used")
        lam_sums, lam_exp = sem("lam_sums"), sem("lam_exp")
        qk_ready = sem("qk_ready")
        x_ld = [sem(f"x_ld{s}") for s in range(2)]
        ms_ready, rms_ready, xn_ready, xt_ready = [sem(n) for n in (
            "ms_ready", "rms_ready", "xn_ready", "xt_ready")]
        hmod_ready, hhi_ready, h_ready = sem("hmod_ready"), sem("hhi_ready"), sem("h_ready")
        w_ld, w_folded, whi_ready, wlo_ready = [sem(n) for n in (
            "w_ld", "w_folded", "whi_ready", "wlo_ready")]
        proj_ready = sem("proj_ready")
        qsq_ready, qss_ready, qrms_ready, qn_ready = [sem(n) for n in (
            "qsq_ready", "qss_ready", "qrms_ready", "qn_ready")]
        qkv_ready, qkv_st = sem("qkv_ready"), [sem(f"qkv_st{s}") for s in range(2)]
        v_ready, gated_ready, conf_ready, conv_ready, prod_ready, short_ready = [sem(n) for n in (
            "v_ready", "gated_ready", "conf_ready", "conv_ready", "prod_ready", "short_ready")]
        lnd_ready, lnsq_ready, lnsd_ready, lnz_ready, lny_ready, lnsig_ready, lnout_ready = [sem(n) for n in (
            "lnd_ready", "lnsq_ready", "lnsd_ready", "lnz_ready", "lny_ready", "lnsig_ready", "lnout_ready")]
        ud_ready, win_ready, pool_y, halo_saved, poolout_ready = [sem(n) for n in (
            "ud_ready", "win_ready", "pool_y", "halo_saved", "poolout_ready")]
        stage_st, ln_st, mod2_ready = [sem("stage_st0"), sem("stage_st1")], sem("ln_st"), sem("mod2_ready")
        qk_ld, v_ld = [sem("qk_ld0"), sem("qk_ld1")], sem("v_ld")
        split_hi, split_lo, x_fill, x_read = [sem(n) for n in ("split_hi", "split_lo", "x_fill", "x_read")]
        sc_mm, sc_read, max_ready, exp_done, a_ready = [sem(n) for n in (
            "sc_mm", "sc_read", "max_ready", "exp_done", "a_ready")]
        at_mm, at_ready, pv_mm, pv_done, o_read = [sem(n) for n in (
            "at_mm", "at_ready", "pv_mm", "pv_done", "o_read")]
        asq_ready, ams_ready, arms_ready, att_ready = [sem(n) for n in (
            "asq_ready", "ams_ready", "arms_ready", "att_ready")]
        attt_st = [sem("attt_st0"), sem("attt_st1")]
        mix_ld = [sem("mix_ld0"), sem("mix_ld1")]
        mixhi_ready, mix_ready, xr_ld, wo_mm, wo_read = [sem(n) for n in (
            "mixhi_ready", "mix_ready", "xr_ld", "wo_mm", "wo_read")]
        ff1_mm, relu_ready, sq_ready, uhi_ready, u_ready = [sem(n) for n in (
            "ff1_mm", "relu_ready", "sq_ready", "uhi_ready", "u_ready")]
        ff2_mm, ff2_read, out_st = [sem(n) for n in ("ff2_mm", "ff2_read", "out_st")]

        OUTS = projections()
        OUT_NO = {o: n for n, o in enumerate(OUTS)}

        def bank(o):
            return psum[:, 2 + o % 3, :]

        def chan_no(h, cc, b):
            return (h * NB + b) * GC + cc

        def released(o):
            kind, h, a, b = OUTS[o]
            if kind == "qk":
                return qn_ready, h * HT + a + 1
            if kind == "v":
                return v_ready, h * HT // 2 + a // 2 + 1
            if kind == "ln":
                return (lnsd_ready if b else lnd_ready), h * NB + a + 1
            n = chan_no(h, a, b)
            if kind in ("gate", "cg"):
                return gated_ready, n + h * NB * GC + (NB * GC if kind == "cg" else 0) + 1
            return {"ud": ud_ready, "pool": poolout_ready, "val": conf_ready, "xc": prod_ready,
                    "bg": short_ready}[kind], n + 1

        w_in_v = w_in.rearrange("a (k p) n -> p (a k) n", p=P)
        w_out_v = w_out.rearrange("a (k p) n -> p (a k) n", p=P)
        w_ff1_v = w_ff1.rearrange("a (k p) n -> p (a k) n", p=P)
        w_ff2_v = w_ff2.rearrange("a (k p) n -> p (a k) n", p=P)
        w_ada_v = w_ada.rearrange("a (k p) n -> p (a k) n", p=P)
        x_v = x.rearrange("a (t p) d -> p (a t) d", p=P)
        out_v = out.rearrange("a (t p) d -> p (a t) d", p=P)
        qkv_v = qkv_d.rearrange("(t p) d -> p t d", p=P)
        mix_v = mix_d.rearrange("(k p) t -> p k t", p=P)

        def used(w):
            h, i = divmod(w, NI)
            if i < 3:
                last = ("v", h, HT - 2, 0) if i == 2 else ("qk", h, HT - 1, 0)
            else:
                last = (ITEMS[i][0], h, GC - 1, NB - 1)
            return proj_ready, OUT_NO[last] + 1

        def qk_turn(n):
            return (n // HT) * (HT + HT // 2) + n % HT

        def v_turn(h, t):
            return h * (HT + HT // 2) + HT + t // 2

        def slot_of_qk(n):
            return qk_turn(n) % 2

        def slot_of_v(h, t):
            return v_turn(h, t) % 2

        def stores_before_qk(n):
            return qk_turn(n) // 2

        def stores_before_v(h, t):
            return v_turn(h, t) // 2

        def stores_of_stage(n, short):
            return (2 * NB * GC * (n // (NB * GC)) + NB * GC * short + n % (NB * GC)) // 2

        def heads_tails(a):
            if a == 0:
                return q_split[:, :, 0:2, :], q_split[:, :, 2:4, :]
            return k_split[:, :, 0:4:2, :], k_split[:, :, 1:4:2, :]

        def by_k8(a):
            return a.rearrange("p (k n) -> p k n", k=DC)

        def by_k2(a):
            return a.rearrange("p (k n) -> p k n", k=2)

        def f32(ap):
            return ap.bitcast(F32)

        block = ctx.enter_context(nc.Block())

        @block.sync
        def _(sp):
            def rows(src):
                return src.rearrange("o (a p) -> (o a) p", p=P)
            for r0, r1, src in ((R_C, R_B, c), (R_B, R_N1, b_ada), (R_N1, R_N2, norm1_g), (R_N2, R_DWB, norm2_g),
                                (R_DWB, R_LNG, conf_dw_b), (R_LNG, R_LNB, conf_ln_g),
                                (R_LNB, R_PSC, conf_ln_b), (R_PSC, R_END1, pool_scale)):
                sp.dma_start(table1[r0:r1, :], rows(src)).then_inc(tab_ld, 16)
            for r0, r1, src in ((R_DWW, R_SW, conf_dw_w), (R_SW, R_END2, short_conv_w)):
                sp.dma_start(table2[r0:r1, :], src.rearrange("o j (a p) -> (o j a) p", p=P)).then_inc(tab_ld, 16)
            def load_small():
                sp.wait_ge(const_ready, 1)
                for g in range(4):
                    r = 64 * (g % 2)
                    sp.dma_start(pool_blk[r:r + 64, g // 2, r:r + 64], pool_w[0, g, :, :]).then_inc(bc_ld, 16)
                for dst, src in ((gain_qk[:, 0, :], q_norm_g[0, :]), (gain_qk[:, 1, :], k_norm_g[0, :]),
                                 (gain_sub[:, :], attn_sub_g[0, :]), (lam_in[:, :, :], lam_params[0, :, :]),
                                 (gate_row[:, 0, :], b_ada[0, 2 * D:3 * D]), (gate_row[:, 1, :], b_ada[0, 5 * D:6 * D])):
                    sp.dma_start(dst, src.partition_broadcast(P)).then_inc(bc_ld, 16)

            for k in range(DC):
                if k == 4:
                    load_small()
                if k >= 4:
                    sp.wait_ge(ada0_used, k - 3)
                sp.dma_start(ada_first[k % 4][:, :], w_ada_v[:, k, 0:2 * D]).then_inc(ada0_ld[k % 4], 16)
                if k < 2:
                    sp.dma_start(x_in[k][:, :], x_v[:, k, :]).then_inc(x_ld[k], 16)

            def raw_free(w):
                sp.wait_ge(whi_ready, w)
                sp.wait_ge(wlo_ready, w)

            def load_w_in(w):
                if w:
                    raw_free(w)
                c0 = ITEMS[w % NI][1]
                sp.dma_start(by_k8(w_raw[:, :]), w_in_v[:, :, c0:c0 + GW]).then_inc(w_ld, 16)

            def load_x(n):
                if n >= 2:
                    sp.wait_ge(xt_ready, n - 1)
                sp.dma_start(x_in[n % 2][:, :], x_v[:, n, :]).then_inc(x_ld[n % 2], 16)

            def load_ada(h, k):
                if h * DC + k:
                    sp.wait_ge(ada_used, h * DC + k)
                gate0, norm0 = (2 + 3 * h) * D, (3 + h) * D
                sp.dma_start(ada[:, 0:D], w_ada_v[:, k, gate0:gate0 + D]).then_inc(ada_ld, 16)
                sp.dma_start(ada[:, D:2 * D], w_ada_v[:, k, norm0:norm0 + D]).then_inc(ada_ld, 16)

            def store_qk(n):
                sp.wait_ge(qk_ready, n + 1)
                s = slot_of_qk(n)
                sp.dma_start(qkv_v[:, n, 0:2 * GW], qkv_out[s][:, :]).then_inc(qkv_st[s], 16)

            def store_v(h, t):
                s = slot_of_v(h, t)
                sp.wait_ge(v_ready, h * HT // 2 + t // 2 + 1)
                sp.dma_start(qkv_v[:, h * HT + t:h * HT + t + 2, 2 * GW:3 * GW],
                             qkv_out[s][:, :].rearrange("p (t d) -> p t d", t=2)).then_inc(qkv_st[s], 16)

            def store_mixer(h, chunk, ready):
                for b in range(NB):
                    for cc in range(GC):
                        n = chan_no(h, cc, b)
                        t0 = h * HALF + b * BLK
                        sp.wait_ge(ready, n + 1)
                        sp.dma_start(mix_v[:, chunk + cc, t0:t0 + BLK], stage[n % 2][:, :]).then_inc(stage_st[n % 2], 16)

            def store_ln(h):
                sp.wait_ge(lnout_ready, GC * NB * (h + 1))
                sp.dma_start(mix_v[:, 2:4, h * HALF:(h + 1) * HALF], acc[:, :, :]).then_inc(ln_st, 16)

            load_w_in(0)
            for h in range(2):
                w0 = h * NI
                for t in range(HT):
                    n = h * HT + t
                    if t == 0:
                        load_w_in(w0 + 1)
                    if t == 2:
                        load_w_in(w0 + 2)
                    if n + 2 < NT:
                        load_x(n + 2)
                    if t >= 1:
                        store_qk(n - 1)
                load_ada(h, 0)
                store_qk(h * HT + HT - 1)
                load_w_in(w0 + 3)
                for t in range(0, HT, 2):
                    store_v(h, t)
                load_ada(h, 1)
                load_w_in(w0 + 4)
                if h:
                    store_ln(0)
                load_ada(h, 2)
                load_w_in(w0 + 5)
                load_ada(h, 3)
                store_mixer(h, 6, poolout_ready)
                load_w_in(w0 + 6)
                load_ada(h, 4)
                load_w_in(w0 + 7)
                load_ada(h, 5)
                load_w_in(w0 + 8)
                load_ada(h, 6)
                if h == 0:
                    load_w_in(w0 + NI)
                load_ada(h, 7)
                store_mixer(h, 4, short_ready)
            store_ln(1)

            for s in range(2):
                sp.wait_ge(qkv_st[s], 16 * (NT + NT // 2) // 2)
                sp.wait_ge(stage_st[s], 16 * 4 * NB * GC // 2)
            sp.wait_ge(proj_ready, len(OUTS))
            sp.wait_ge(mod2_ready, 2)
            sp.wait_ge(h_ready, NT)
            for i in range(NT):
                if i >= 2:
                    sp.wait_ge(split_lo, 2 * (i - 1))
                sp.dma_start(qk_in[i % 2][:, :, :],
                             qkv_v[:, i, 0:2 * GW].rearrange("p (a d) -> p a d", a=2)).then_inc(qk_ld[i % 2], 16)
                if i == 1:
                    sp.wait_ge(ln_st, 32)
                    sp.dma_start(v_sb[:, :, :], qkv_v[:, :, 2 * GW:3 * GW]).then_inc(v_ld, 16)
            for j in range(NT // 4):
                sp.wait_ge(x_read, FILL_NO["att", j, 1] + 1)
                sp.dma_start(mix_v[:, 0:2, j * BLK:(j + 1) * BLK], att_t[j % 2][:, :, :]).then_inc(attt_st[j % 2], 16)

            def load_mix(n):
                if n % HT >= 2:
                    sp.wait_ge(mix_ready, n - 1)
                sp.dma_start(mix_in[n % 2][:, :, :], mix_v[:, :, n * P:(n + 1) * P]).then_inc(mix_ld[n % 2], 16)

            for s in range(2):
                sp.wait_ge(attt_st[s], 32)
            sp.wait_ge(pv_mm, AT_NO[UNITS])
            sp.wait_ge(x_read, len(FILLS))
            for hc in range(2):
                w0 = 2 * NI + hc * C_ITEMS
                if hc:
                    sp.wait_ge(ff2_read, FG * 2 * HT)
                    sp.wait_ge(out_st, 16 * HT)
                for n in (0, 1):
                    load_mix(hc * HT + n)
                for i in range(KC_OUT):
                    raw_free(w0 + i)
                    sp.dma_start(by_k2(w_raw[:, :]), w_out_v[:, 2 * i:2 * i + 2, :]).then_inc(w_ld, 16)
                for t in range(HT):
                    n = hc * HT + t
                    if n:
                        sp.wait_ge(xr_ld, 16 * n)
                    sp.dma_start(x_new[:, t, :], x_v[:, n, :]).then_inc(xr_ld, 16)
                    if t + 2 < HT:
                        load_mix(n + 2)

                def load_ff(g):
                    w = 2 * g + (w0 + KC_OUT)
                    raw_free(w)
                    sp.dma_start(by_k8(w_raw[:, :]), w_ff1_v[:, :, bass.ds(g * GW, GW)]).then_inc(w_ld, 16)
                    raw_free(w + 1)
                    sp.dma_start(by_k2(w_raw[:, :]), w_ff2_v[:, bass.ds(g * 2, 2), :]).then_inc(w_ld, 16)

                load_ff(0)
                load_ff(1)
                with sp.Fori(0, FG // 2 - 1) as it:
                    for q in range(2):
                        load_ff(it * 2 + (2 + q))
                for t in range(HT):
                    sp.wait_ge(ff2_read, (hc + 1) * FG * 2 * HT - 2 * (HT - 1 - t))
                    sp.dma_start(out_v[:, hc * HT + t, :], x_new[:, t, :]).then_inc(out_st, 16)
            sp.wait_ge(out_st, 16 * NT)

        @block.gpsimd
        def _(pool):
            links = [0]

            def link(ins):
                links[0] += 1
                ins.then_inc(pool_chain, 1)
                pool.wait_ge(pool_chain, links[0])

            link(pool.memset(pool_blk[:, :, :], 0.0))
            link(pool.memset(ident[:, :], 0.0))
            pool.affine_select(out=ident[:, :], in_=ident[:, :], compare_op=ALU.not_equal, fill=1.0,
                               base=0, pattern=[[-1, P]], channel_multiplier=1)
            link(pool.memset(h_tmp[:, 0, :], 0.0))
            pool.affine_select(out=h_tmp[:, 0, :], in_=h_tmp[:, 0, :], compare_op=ALU.is_ge, fill=NEG,
                               base=0, pattern=[[-1, P]], channel_multiplier=1)
            pool.memset(ones_mean[:, :], 1.0 / GW)
            pool.memset(eps_col, EPS).then_inc(const_ready, 1)

            def norm_gain(n):
                pool.wait_ge(qn_ready, n + 1)
                v = qkv_out[slot_of_qk(n)][:, :].rearrange("p (a m d) -> p a m d", a=2, d=QKD)
                if n == 0:
                    pool.wait_ge(bc_ld, 16 * BROADCASTS)
                pool.tensor_tensor(out=v[:, 0], in0=v[:, 0], op=ALU.mult,
                                   in1=gain_qk[:, 0:1, :].to_broadcast([P, MAPS, QKD]))
                pool.tensor_tensor(out=v[:, 1], in0=v[:, 1], op=ALU.mult,
                                   in1=gain_qk[:, 1:2, :].to_broadcast([P, MAPS, QKD])).then_inc(qk_ready, 1)

            def windows(n, cc):
                pool.wait_ge(ud_ready, n + 1)
                if n:
                    pool.wait_ge(pool_y, n)
                end = POOL_HALO + BLK
                u = ud[:, cc, :]
                link(pool.tensor_tensor(out=win_a[:, 1:end], in0=u[:, 1:end], in1=u[:, 0:end - 1], op=ALU.add))
                last = pool.tensor_tensor(out=win_b[:, 3:end], in0=win_a[:, 3:end], in1=win_a[:, 1:end - 2], op=ALU.add)
                if cc:
                    link(last)
                    link(pool.tensor_tensor(out=win_a[:, 7:end], in0=win_b[:, 7:end], in1=win_b[:, 3:end - 4], op=ALU.add))
                    last = pool.tensor_tensor(out=win_b[:, 15:end], in0=win_a[:, 15:end], in1=win_a[:, 7:end - 8], op=ALU.add)
                last.then_inc(win_ready, 1)

            def ln_out(h):
                for b in range(NB):
                    for cc in range(GC):
                        pool.wait_ge(lnsig_ready, chan_no(h, cc, b) + 1)
                        y = acc[:, cc, b * BLK:(b + 1) * BLK]
                        pool.tensor_tensor(out=y, in0=y, in1=ln_sig[:, :], op=ALU.mult).then_inc(lnout_ready, 1)

            for h in range(2):
                for t in range(HT):
                    norm_gain(h * HT + t)
                if h:
                    ln_out(0)
                for b in range(NB):
                    for cc in range(GC):
                        windows(chan_no(h, cc, b), cc)
            ln_out(1)

            def split_tail(n, a):
                pool.wait_ge(split_hi, 2 * n + a + 1)
                hi, lo = heads_tails(a)
                src = qk_in[n % 2][:, a, :].rearrange("p (m o d) -> p m o d", o=1, d=QKD).to_broadcast([P, MAPS, 2, QKD])
                pool.tensor_tensor(out=lo, in0=src, in1=f32(hi), op=ALU.subtract).then_inc(split_lo, 1)

            split_tail(0, 0)
            split_tail(0, 1)
            for u in range(STEPS):
                for n, a in splits_at(u):
                    split_tail(n, a)
                j = (u - 19) // 16
                if j >= 0 and u == 16 * j + 19:
                    pool.wait_ge(o_read, 16 * (j + 1))
                    y = att[:, 4 * j:4 * j + 4, :]
                    pool.tensor_tensor(out=att_sq[:, :, :], in0=y, in1=y, op=ALU.mult).then_inc(asq_ready, 1)

        @block.scalar
        def _(act):
            A = nc.scalar.activation

            def w_head(w, s, ready, before):
                act.wait_ge(*ready)
                if before is not None:
                    act.wait_ge(*before)
                A(w_hi[s][:, :], w_raw[:, :], ACT.Copy).then_inc(whi_ready, 1)

            def w_in_head(w):
                w_head(w, w % 3, (w_ld, 16 * (w + 1)), used(w - 3) if w >= 3 else None)

            def rms_root(n):
                act.wait_ge(ms_ready, n + 1)
                A(stat[:, 4 * (n % 2) + 3:4 * (n % 2) + 4], stat[:, 4 * (n % 2) + 2:4 * (n % 2) + 3],
                  ACT.Sqrt, bias=eps_col).then_inc(rms_ready, 1)

            def modulate(n, tmp, gain, shift):
                act.wait_ge(xt_ready, n + 1)
                if n:
                    act.wait_ge(h_ready, n)
                for k in range(DC):
                    last = A(tmp[:, k, :], ps_t[:, k, :], ACT.Identity, scale=gain[:, k:k + 1], bias=shift[:, k:k + 1])
                last.then_inc(hmod_ready, 1)

            def h_head(n, tmp):
                act.wait_ge(hmod_ready, n + 1)
                t = n % HT
                A(h_hi[:, :, t * P:(t + 1) * P], tmp[:, :, :], ACT.Copy).then_inc(hhi_ready, 1)

            act.wait_ge(const_ready, 1)
            A(ident_r[:, :], ident[:, :], ACT.Copy)
            A(mask_r[:, :], h_tmp[:, 0, :], ACT.Copy).then_inc(act_chain, 1)
            act.wait_ge(tab_t, 1)
            A(col1[:, :], psum[:, 0, 0:R_END1], ACT.Copy).then_inc(tab_col, 1)
            A(col2[:, :], psum[:, 1, 0:R_END2], ACT.Copy).then_inc(tab_col, 1)
            act.wait_ge(tab_col, 2)
            A(silu_c[:, :], col1[:, R_C:R_B], ACT.Sigmoid).then_inc(sigc_ready, 1)
            act.wait_ge(lam_sums, 1)
            A(small[:, 6:8], small[:, 4:6], ACT.Exp).then_inc(lam_exp, 1)
            act.wait_ge(act_chain, 1)
            rms_root(0)
            rms_root(1)
            w_in_head(0)
            w_in_head(1)
            act.wait_ge(mod1_ready, 1)
            modulate(0, h_tmp, gain1, shift1)
            h_head(0, h_tmp)

            def qk_square(n):
                o = OUT_NO["qk", n // HT, n % HT, 0]
                act.wait_ge(proj_ready, o + 1)
                if n:
                    act.wait_ge(qss_ready, n)
                A(qk_sq[:, :], bank(o), ACT.Square).then_inc(qsq_ready, 1)
                act.wait_ge(qss_ready, n + 1)
                if n:
                    act.wait_ge(qn_ready, n)
                A(small[:, 48:64], small[:, 32:48], ACT.Sqrt, bias=eps_col, scale=1.0 / QKD).then_inc(qrms_ready, 1)

            def layer_norm(h):
                for b in range(NB):
                    m, blk = h * NB + b, slice(b * BLK, (b + 1) * BLK)
                    act.wait_ge(lnd_ready, m + 1)
                    A(ln_sq[:, :, :], acc[:, :, blk], ACT.Square).then_inc(lnsq_ready, 1)
                    o = OUT_NO["ln", h, b, 1]
                    act.wait_ge(proj_ready, o + 1)
                    A(ln_rs[:, :], bank(o), ACT.Sqrt, bias=eps_col).then_inc(lnsd_ready, 1)
                    act.wait_ge(lnz_ready, m + 1)
                    for cc in range(GC):
                        y, n = acc[:, cc, blk], GC * m + cc
                        A(y, y, ACT.Identity, scale=col1[:, R_LNG + cc:R_LNG + cc + 1],
                          bias=col1[:, R_LNB + cc:R_LNB + cc + 1]).then_inc(lny_ready, 1)
                        act.wait_ge(lny_ready, n + 1)
                        if n:
                            act.wait_ge(lnout_ready, n)
                        A(ln_sig[:, :], y, ACT.Sigmoid).then_inc(lnsig_ready, 1)

            def each_block(kind, h, evacuate):
                for b in range(NB):
                    for cc in range(GC):
                        o = OUT_NO[kind, h, cc, b]
                        act.wait_ge(proj_ready, o + 1)
                        evacuate(o, cc, b, chan_no(h, cc, b))

            def to_ud(o, cc, b, n):
                if n >= GC:
                    act.wait_ge(halo_saved, n - GC + 1)
                A(ud[:, cc, POOL_HALO:], bank(o), ACT.Copy).then_inc(ud_ready, 1)

            def to_gated(func):
                def evacuate(o, cc, b, n):
                    A(gated[:, cc, b * BLK:(b + 1) * BLK], bank(o), func).then_inc(gated_ready, 1)
                return evacuate

            def to_pool_stage(o, cc, b, n):
                if n >= 2:
                    act.wait_ge(stage_st[n % 2], 16 * stores_of_stage(n, False))
                A(stage[n % 2][:, :], bank(o), ACT.Copy, scale=col1[:, R_PSC + cc:R_PSC + cc + 1]).then_inc(poolout_ready, 1)

            for h in range(2):
                w0 = h * NI
                for t in range(HT):
                    n = h * HT + t
                    if n + 2 < NT:
                        rms_root(n + 2)
                    if t:
                        qk_square(n - 1)
                    if t + 1 < HT:
                        modulate(n + 1, h_tmp, gain1, shift1)
                        h_head(n + 1, h_tmp)
                    if t == 2:
                        w_in_head(w0 + 2)
                qk_square(h * HT + HT - 1)
                w_in_head(w0 + 3)
                for t in range(0, HT, 2):
                    o, s = OUT_NO["v", h, t, 0], slot_of_v(h, t)
                    act.wait_ge(proj_ready, o + 1)
                    act.wait_ge(qkv_st[s], 16 * stores_before_v(h, t))
                    A(qkv_out[s][:, :], bank(o), ACT.Copy).then_inc(v_ready, 1)
                if h:
                    layer_norm(0)
                w_in_head(w0 + 4)
                each_block("ud", h, to_ud)
                w_in_head(w0 + 5)
                if h:
                    act.wait_ge(prod_ready, NB * GC * h)
                each_block("gate", h, to_gated(ACT.Sigmoid))
                each_block("pool", h, to_pool_stage)
                w_in_head(w0 + 6)
                act.wait_ge(conf_ready, NB * GC * (h + 1))
                w_in_head(w0 + 7)
                each_block("cg", h, to_gated(ACT.Copy))
                w_in_head(w0 + 8)
                if h == 0:
                    w_in_head(NI)
                    modulate(HT, h_tmp, gain1, shift1)
                    act.wait_ge(*used(NI - 1))
                    h_head(HT, h_tmp)
                    w_in_head(NI + 1)
            layer_norm(1)

            act.wait_ge(proj_ready, len(OUTS))

            def split_head(n, a):
                hi, lo = heads_tails(a)
                if a == 0:
                    act.wait_ge(qk_ld[n % 2], 16 * (n // 2 + 1))
                if n:
                    act.wait_ge(x_fill, FILL_NO["stack", n - 1, 2 * a + 1] + 1)
                src = qk_in[n % 2][:, a, :].rearrange("p (m o d) -> p m o d", o=1, d=QKD).to_broadcast([P, MAPS, 2, QKD])
                A(hi, src, ACT.Copy).then_inc(split_hi, 1)

            def read_fill(x):
                kind, i, f = FILLS[x]
                act.wait_ge(x_fill, x + 1)
                if kind == "stack":
                    m0, src = 4 * (f % 2), psum[:, 7, :].rearrange("p (m t) -> p m t", m=4)
                    dst = q_stack[i % 2][:, m0:m0 + 4, :] if f < 2 else k_stack[:, m0:m0 + 4, i * P:(i + 1) * P]
                else:
                    if i >= 2 and f == 0:
                        act.wait_ge(attt_st[i % 2], 16)
                    src, dst = psum[:, 7, :], att_t[i % 2][:, f, :]
                A(dst, src, ACT.Copy).then_inc(x_read, 1)

            def exps(u):
                i, s = u // HEADS, u % 3
                n = (i + 1) * P
                act.wait_ge(max_ready, u + 1)
                for m in range(2):
                    A(scores[s][:, m, 0:n], scores[s][:, m, 0:n], ACT.Exp, scale=SCALE, bias=bst[:, s, 10 + m:11 + m],
                      accum_out=bst[:, s, 12 + m:13 + m]).then_inc(exp_done, 1)

            def read_at(u):
                for g, (k0, nk) in enumerate(at_groups(u)):
                    gn = AT_NO[u] + g
                    act.wait_ge(at_mm, gn + 1)
                    if gn >= 2:
                        act.wait_ge(pv_mm, gn - 1)
                    A(a_t[gn % 2][:, 0:nk * P], psum[:, 4 + gn % 2, 0:nk * P], ACT.Copy).then_inc(at_ready, 1)

            split_head(0, 0)
            split_head(0, 1)
            for x in range(4):
                read_fill(x)
            for u in range(STEPS):
                for n, a in splits_at(u):
                    split_head(n, a)
                for x in fills_at(u):
                    read_fill(x)
                if 0 <= u - 1 < UNITS:
                    exps(u - 1)
                if 0 <= u - 2 < UNITS:
                    read_at(u - 2)
                j = (u - 19) // 16
                if j >= 0 and u == 16 * j + 19:
                    act.wait_ge(ams_ready, j + 1)
                    A(ams[:, 16:32], ams[:, 0:16], ACT.Sqrt, bias=eps_col, scale=1.0 / VD).then_inc(arms_ready, 1)

            act.wait_ge(pv_mm, AT_NO[UNITS])
            for s in range(2):
                act.wait_ge(attt_st[s], 32)
            for hc in range(2):
                w0 = 2 * NI + hc * C_ITEMS
                n0 = hc * HT

                def mix_head(t):
                    n = n0 + t
                    act.wait_ge(mix_ld[n % 2], 16 * (n // 2 + 1))
                    A(h_hi[:, :, t * P:(t + 1) * P], mix_in[n % 2][:, :, :], ACT.Copy).then_inc(mixhi_ready, 1)

                before = [(ff1_mm, 4 * FG - 4), (ff2_mm, 16 * FG - 16), (ff1_mm, 4 * FG), (ff2_mm, 16 * FG)]
                if hc:
                    act.wait_ge(ff1_mm, 4 * FG)
                mix_head(0)
                for i in range(KC_OUT):
                    w_head(w0 + i, i, (w_folded, hc * C_FOLDS + i + 1), before[i] if hc else None)
                for t in range(HT):
                    n = NT + n0 + t
                    if t + 1 < HT:
                        mix_head(t + 1)
                    rms_root(n)
                    if t:
                        modulate(n - 1, h_tmp2, gain2, shift2)
                        h_head(n - 1, h_tmp2)
                modulate(NT + n0 + HT - 1, h_tmp2, gain2, shift2)
                h_head(NT + n0 + HT - 1, h_tmp2)

                all_w_out = (wo_mm, 2 * (n0 + HT))

                def ff1_head(g, q, first=False):
                    w = 2 * g + (w0 + KC_OUT)
                    w_head(w, 2 * q, (w_ld, (w + 1) * 16),
                           all_w_out if first else (ff1_mm, 4 * g + (4 * FG * hc - 4)))

                def ff2_head(g, q, first=False):
                    w = 2 * g + (w0 + KC_OUT + 1)
                    w_head(w, 2 * q + 1, (w_folded, g + (hc * C_FOLDS + KC_OUT + 1)),
                           all_w_out if first else (ff2_mm, 16 * g + (16 * FG * hc - 16)))

                ff1_head(0, 0, True)
                ff2_head(0, 0, True)
                act.wait_ge(h_ready, NT + n0 + HT)

                def group(g, q, ahead, first=False):
                    def relu(f):
                        F = 4 * g + (4 * FG * hc + f)
                        act.wait_ge(ff1_mm, F + 1)
                        if not first:
                            act.wait_ge(u_ready, F - 3)
                        A(relu_t[f][:, :], psum[:, 2 + f % 2, :], ACT.Relu).then_inc(relu_ready, 1)

                    def u_head(f):
                        F = 4 * g + (4 * FG * hc + f)
                        b, j = f // 2, f % 2
                        act.wait_ge(sq_ready, F + 1)
                        if not first:
                            act.wait_ge(ff2_mm, 16 * g + (16 * FG * hc - 16 + 8 * b + 8))
                        A(u_hi[:, j, b * BLK:(b + 1) * BLK], relu_t[f][:, :], ACT.Copy).then_inc(uhi_ready, 1)

                    relu(0)
                    if ahead:
                        ff1_head(g + 1, 1 - q, first)
                    u_head(0)
                    relu(1)
                    u_head(1)
                    relu(2)
                    u_head(2)
                    if ahead:
                        ff2_head(g + 1, 1 - q, first)
                    relu(3)
                    u_head(3)

                group(0, 0, True, first=True)
                group(1, 1, True)
                with act.Fori(1, FG // 2 - 1) as it:
                    for q in range(2):
                        group(it * 2 + q, q, True)
                group(FG - 2, 0, True)
                group(FG - 1, 1, False)

        @block.vector
        def _(dve):
            V = nc.vector
            links = [0]

            def mark(ins):
                links[0] += 1
                ins.then_inc(dve_chain, 1)
                return links[0]

            def link(ins):
                dve.wait_ge(dve_chain, mark(ins))

            def mean_square(n, src):
                s = 4 * (n % 2)
                V.bn_stats(bn[:, 0, :], src[:, 0:BLK])
                link(V.bn_stats(bn[:, 1, :], src[:, BLK:D]))
                link(V.bn_aggr(stat[:, s:s + 2], bn[:, :, :].rearrange("p a b -> p (a b)")))
                V.scalar_tensor_tensor(out=stat[:, s + 2:s + 3], in0=stat[:, s:s + 1], scalar=stat[:, s:s + 1],
                                       in1=stat[:, s + 1:s + 2], op0=ALU.mult, op1=ALU.add).then_inc(ms_ready, 1)

            def normalise(n, src, dst):
                s = 4 * (n % 2)
                dve.wait_ge(rms_ready, n + 1)
                link(V.reciprocal(stat[:, 8:9], stat[:, s + 3:s + 4]))
                V.tensor_scalar(dst, src, stat[:, 8:9], None, ALU.mult).then_inc(xn_ready, 1)

            def h_tail(n, tmp):
                t = n % HT
                dve.wait_ge(hhi_ready, n + 1)
                tok = slice(t * P, (t + 1) * P)
                V.tensor_tensor(out=h_lo[:, :, tok], in0=tmp[:, :, :], in1=f32(h_hi[:, :, tok]),
                                op=ALU.subtract).then_inc(h_ready, 1)

            def w_tail(w, s):
                dve.wait_ge(whi_ready, w + 1)
                V.tensor_tensor(out=w_lo[s][:, :], in0=w_raw[:, :], in1=f32(w_hi[s][:, :]),
                                op=ALU.subtract).then_inc(wlo_ready, 1)

            def w_in_tail(w):
                w_tail(w, w % 3)

            def w_fold(w, j):
                dve.wait_ge(w_ld, (w + 1) * 16)
                V.tensor_tensor(out=by_k2(w_raw[:, :]), in0=by_k2(w_raw[:, :]), op=ALU.mult,
                                in1=gate_row[:, j:j + 1, :].to_broadcast([P, 2, D])).then_inc(w_folded, 1)

            groups = [(cc, slice(64 * s, 64 * s + 64), 2 << (2 * cc + s)) for cc in range(GC) for s in range(2)]
            for cc, part, win in groups:
                V.memset(inv_win[part, cc:cc + 1], 1.0 / win)
                ins = V.memset(inv_first[part, cc, :], 1.0 / win)
            link(ins)
            for cc, part, win in groups:
                for t in range(win - 1):
                    V.memset(inv_first[part, cc, t:t + 1], 1.0 / (t + 1))

            dve.wait_ge(bc_ld, 16 * BROADCASTS)
            pairs = small[:, 32:96].rearrange("p (a d) -> p a d", d=QKD)
            link(V.tensor_tensor(out=pairs, in0=lam_in[:, 0:4:2, :], in1=lam_in[:, 1:4:2, :], op=ALU.mult))
            V.tensor_reduce(out=small[:, 4:6], in_=pairs, axis=AX.X, op=ALU.add).then_inc(lam_sums, 1)
            dve.wait_ge(sigc_ready, 1)
            V.tensor_tensor(out=silu_c[:, :], in0=silu_c[:, :], in1=col1[:, R_C:R_B], op=ALU.mult).then_inc(siluc_ready, 1)
            dve.wait_ge(lam_exp, 1)
            V.scalar_tensor_tensor(out=lam_neg, in0=small[:, 7:8], scalar=-LAM_INIT, in1=small[:, 6:7],
                                   op0=ALU.add, op1=ALU.subtract)
            V.tensor_scalar(gain_sub[:, :], gain_sub[:, :], 1.0 - LAM_INIT, None, ALU.mult)
            for n in range(2):
                dve.wait_ge(x_ld[n], 16)
                mean_square(n, x_in[n])
                normalise(n, x_in[n][:, :], x_in[n][:, :])
            w_in_tail(0)
            w_in_tail(1)
            dve.wait_ge(mod1_mm, 1)
            V.tensor_tensor(out=shift1[:, :], in0=psum[:, 7, 0:8], in1=col1[:, R_B:R_B + 8], op=ALU.add)
            link(V.tensor_tensor(out=gain1[:, :], in0=psum[:, 7, 8:16], in1=col1[:, R_B + 8:R_B + 16], op=ALU.add))
            V.scalar_tensor_tensor(out=gain1[:, :], in0=gain1[:, :], scalar=1.0, in1=col1[:, R_N1:R_N2],
                                   op0=ALU.add, op1=ALU.mult).then_inc(mod1_ready, 1)
            V.memset(conf[:, :, 0:TAPS - 1], 0.0)
            V.memset(ud[:, :, 0:POOL_HALO], 0.0)
            link(V.memset(halo2[:, :, :], 0.0))
            h_tail(0, h_tmp)

            def qk_sums(n):
                dve.wait_ge(qsq_ready, n + 1)
                V.tensor_reduce(out=small[:, 32:48], in_=qk_sq[:, :].rearrange("p (a d) -> p a d", d=QKD),
                                axis=AX.X, op=ALU.add).then_inc(qss_ready, 1)

            def qk_normalise(n):
                s = slot_of_qk(n)
                dve.wait_ge(qrms_ready, n + 1)
                link(V.reciprocal(small[:, 64:80], small[:, 48:64]))
                if stores_before_qk(n):
                    dve.wait_ge(qkv_st[s], 16 * stores_before_qk(n))
                r = small[:, 64:80].rearrange("p (a o) -> p a o", o=1).to_broadcast([P, 2 * MAPS, QKD])
                V.tensor_tensor(out=qkv_out[s][:, :].rearrange("p (a d) -> p a d", d=QKD),
                                in0=bank(OUT_NO["qk", n // HT, n % HT, 0]).rearrange("p (a d) -> p a d", d=QKD),
                                in1=r, op=ALU.mult).then_inc(qn_ready, 1)

            def conv_taps(h):
                marks = []
                for j in range(TAPS):
                    for cc in range(GC):
                        w, src, dst = col2[:, R_DWW + GC * j + cc:R_DWW + GC * j + cc + 1], conf[:, cc, j:j + HALF], acc[:, cc, :]
                        if j == 0:
                            if h and cc == 0:
                                dve.wait_ge(ln_st, 16)
                            ins = V.tensor_scalar(dst, src, w, col1[:, R_DWB + cc:R_DWB + cc + 1], ALU.mult, ALU.add)
                        else:
                            dve.wait_ge(dve_chain, marks[-GC])
                            ins = V.scalar_tensor_tensor(out=dst, in0=src, scalar=w, in1=dst, op0=ALU.mult, op1=ALU.add)
                        if j == TAPS - 1 and cc == GC - 1:
                            ins.then_inc(conv_ready, 1)
                        else:
                            marks.append(mark(ins))
                        yield
                dve.wait_ge(conv_ready, h + 1)
                link(V.tensor_copy(conf[:, :, 0:TAPS - 1], conf[:, :, HALF:HALF + TAPS - 1]))

            def pump(taps, n):
                for _ in range(n):
                    next(taps, None)

            def layer_norm(h):
                for b in range(NB):
                    blk = slice(b * BLK, (b + 1) * BLK)
                    o = OUT_NO["ln", h, b, 0]
                    dve.wait_ge(proj_ready, o + 1)
                    V.tensor_tensor(out=acc[:, 0, blk], in0=acc[:, 0, blk], in1=bank(o), op=ALU.subtract)
                    V.tensor_tensor(out=acc[:, 1, blk], in0=acc[:, 1, blk], in1=bank(o), op=ALU.subtract).then_inc(lnd_ready, 1)
                    dve.wait_ge(lnsd_ready, h * NB + b + 1)
                    link(V.reciprocal(ln_rs[:, :], ln_rs[:, :]))
                    V.tensor_tensor(out=acc[:, 0, blk], in0=acc[:, 0, blk], in1=ln_rs[:, :], op=ALU.mult)
                    V.tensor_tensor(out=acc[:, 1, blk], in0=acc[:, 1, blk], in1=ln_rs[:, :], op=ALU.mult).then_inc(lnz_ready, 1)

            def pooled(h, cc, b):
                n = chan_no(h, cc, b)
                dve.wait_ge(win_ready, n + 1)
                y = pool_in[:, cc, b * BLK:(b + 1) * BLK]
                first = POOL_HALO if h == b == 0 else 0
                for part, win in ((slice(0, 64), win_a), (slice(64, P), win_b)):
                    if first:
                        link(V.tensor_tensor(out=win[part, POOL_HALO:2 * POOL_HALO], in0=win[part, POOL_HALO:2 * POOL_HALO],
                                             in1=inv_first[part, cc, :], op=ALU.mult))
                        V.tensor_tensor(out=y[part, 0:first], in0=win[part, POOL_HALO:2 * POOL_HALO],
                                        in1=ud[part, cc, POOL_HALO:2 * POOL_HALO], op=ALU.subtract)
                    last = V.scalar_tensor_tensor(out=y[part, first:BLK], in0=win[part, POOL_HALO + first:],
                                                  scalar=inv_win[part, cc:cc + 1], in1=ud[part, cc, POOL_HALO + first:],
                                                  op0=ALU.mult, op1=ALU.subtract)
                last.then_inc(pool_y, 1)
                dve.wait_ge(pool_y, n + 1)
                V.tensor_copy(ud[:, cc, 0:POOL_HALO], ud[:, cc, BLK:BLK + POOL_HALO]).then_inc(halo_saved, 1)

            taps = iter(())
            for h in range(2):
                w0 = h * NI
                for t in range(HT):
                    n = h * HT + t
                    if n + 2 < NT:
                        dve.wait_ge(x_ld[n % 2], 16 * ((n + 2) // 2 + 1))
                        mean_square(n + 2, x_in[n % 2])
                    if t:
                        qk_sums(n - 1)
                    if n + 2 < NT:
                        normalise(n + 2, x_in[n % 2][:, :], x_in[n % 2][:, :])
                    if t:
                        qk_normalise(n - 1)
                    if t + 1 < HT:
                        h_tail(n + 1, h_tmp)
                    if t == 2:
                        w_in_tail(w0 + 2)
                    pump(taps, 2)
                qk_sums(h * HT + HT - 1)
                qk_normalise(h * HT + HT - 1)
                w_in_tail(w0 + 3)
                pump(taps, 3 * TAPS)
                if h:
                    layer_norm(0)
                w_in_tail(w0 + 4)
                for b in range(NB):
                    for cc in range(GC):
                        pooled(h, cc, b)
                w_in_tail(w0 + 5)
                for b in range(NB):
                    if b == 1:
                        w_in_tail(w0 + 6)
                    for cc in range(GC):
                        blk = slice(b * BLK, (b + 1) * BLK)
                        o = OUT_NO["val", h, cc, b]
                        dve.wait_ge(proj_ready, o + 1)
                        dve.wait_ge(gated_ready, 2 * h * NB * GC + GC * b + cc + 1)
                        V.tensor_tensor(out=conf[:, cc, TAPS - 1 + b * BLK:TAPS - 1 + (b + 1) * BLK], in0=bank(o),
                                        in1=gated[:, cc, blk], op=ALU.mult).then_inc(conf_ready, 1)
                dve.wait_ge(conf_ready, NB * GC * (h + 1))
                taps = conv_taps(h)
                pump(taps, 2)
                w_in_tail(w0 + 7)
                pump(taps, 16)
                dve.wait_ge(proj_ready, OUT_NO["pool", h, GC - 1, NB - 1] + 1)
                link(V.tensor_copy(prod[:, :, 0:STAPS - 1], halo2[:, :, :]))
                w_in_tail(w0 + 8)
                for b in range(NB):
                    for cc in range(GC):
                        blk = slice(b * BLK, (b + 1) * BLK)
                        o = OUT_NO["xc", h, cc, b]
                        dve.wait_ge(proj_ready, o + 1)
                        dve.wait_ge(gated_ready, (2 * h + 1) * NB * GC + GC * b + cc + 1)
                        V.tensor_tensor(out=prod[:, cc, STAPS - 1 + b * BLK:STAPS - 1 + (b + 1) * BLK], in0=bank(o),
                                        in1=gated[:, cc, blk], op=ALU.mult).then_inc(prod_ready, 1)
                        pump(taps, 4)
                dve.wait_ge(prod_ready, NB * GC * (h + 1))
                if h == 0:
                    w_in_tail(NI)
                for b in range(NB):
                    for cc in range(GC):
                        n = chan_no(h, cc, b)
                        y = stage[n % 2][:, :]
                        dve.wait_ge(stage_st[n % 2], 16 * stores_of_stage(n, True))
                        for j in range(STAPS):
                            w = col2[:, R_SW + GC * j + cc:R_SW + GC * j + cc + 1]
                            src = prod[:, cc, b * BLK + j:b * BLK + j + BLK]
                            if j == 0:
                                link(V.tensor_scalar(y, src, w, None, ALU.mult))
                            else:
                                link(V.scalar_tensor_tensor(out=y, in0=src, scalar=w, in1=y, op0=ALU.mult, op1=ALU.add))
                        o = OUT_NO["bg", h, cc, b]
                        dve.wait_ge(proj_ready, o + 1)
                        V.tensor_tensor(out=y, in0=y, in1=bank(o), op=ALU.mult).then_inc(short_ready, 1)
                        pump(taps, 4)
                link(V.tensor_copy(halo2[:, :, :], prod[:, :, HALF:HALF + STAPS - 1]))
                dve.wait_ge(ada_used, DC * (h + 1))
                V.tensor_tensor(out=gate_row[:, h, :], in0=gate_row[:, h, :],
                                in1=psum[:, 5:7, :].rearrange("p a n -> p (a n)"), op=ALU.add)
                r = R_B + (3 + h) * DC
                if h == 0:
                    V.tensor_tensor(out=shift2[:, :], in0=psum[:, 7, 0:DC], in1=col1[:, r:r + DC], op=ALU.add).then_inc(mod2_ready, 1)
                    h_tail(HT, h_tmp)
                    w_in_tail(NI + 1)
                else:
                    link(V.tensor_tensor(out=gain2[:, :], in0=psum[:, 7, 0:DC], in1=col1[:, r:r + DC], op=ALU.add))
                    V.scalar_tensor_tensor(out=gain2[:, :], in0=gain2[:, :], scalar=1.0, in1=col1[:, R_N2:R_DWB],
                                           op0=ALU.add, op1=ALU.mult).then_inc(mod2_ready, 1)
            pump(taps, 3 * TAPS)
            layer_norm(1)

            dve.wait_ge(proj_ready, len(OUTS))
            dve.wait_ge(ln_st, 32)

            def read_scores(u):
                i, s = u // HEADS, u % 3
                nch = len(sc_chunks(i))
                if u >= 3:
                    dve.wait_ge(at_mm, AT_NO[u - 2])
                for m in range(2):
                    for ch, (c0, n) in enumerate(sc_chunks(i)):
                        r = SC_NO[u] + m * nch + ch
                        dve.wait_ge(sc_mm, r + 1)
                        V.tensor_scalar(scores[s][:, m, c0:c0 + n], psum[:, r % 4, 0:n], 1.0, None, ALU.mult, ALU.max,
                                        accum_out=bst[:, s, 4 * m + ch:4 * m + ch + 1]).then_inc(sc_read, 1)
                dve.wait_ge(sc_read, SC_NO[u + 1])
                link(V.tensor_reduce(out=bst[:, s, 8:10], axis=AX.X, op=ALU.max,
                                     in_=bst[:, s, 0:8].rearrange("p (m c) -> p m c", m=2)[:, :, 0:nch]))
                V.tensor_scalar(bst[:, s, 10:12], bst[:, s, 8:10], -SCALE, None, ALU.mult).then_inc(max_ready, 1)

            def combine(u):
                i, s = u // HEADS, u % 3
                n = (i + 1) * P
                dve.wait_ge(exp_done, 2 * (u + 1))
                link(V.reciprocal(bst[:, s, 14:16], bst[:, s, 12:14]))
                link(V.scalar_tensor_tensor(out=bst[:, s, 16:17], in0=bst[:, s, 12:13], scalar=bst[:, s, 15:16],
                                            in1=lam_neg, op0=ALU.mult, op1=ALU.mult))
                V.scalar_tensor_tensor(out=scores[s][:, 0, 0:n], in0=scores[s][:, 1, 0:n], scalar=bst[:, s, 16:17],
                                       in1=scores[s][:, 0, 0:n], op0=ALU.mult, op1=ALU.add).then_inc(a_ready, 1)
                link(V.tensor_copy(inv_s[:, u % 4:u % 4 + 1], bst[:, s, 14:15]))

            def read_o(u):
                i, hd = u // HEADS, u % HEADS
                dve.wait_ge(pv_mm, AT_NO[u + 1])
                V.tensor_scalar(att[:, i, hd * VD:(hd + 1) * VD], psum[:, 6, 0:VD],
                                inv_s[:, u % 4:u % 4 + 1], None, ALU.mult).then_inc(o_read, 1)

            for u in range(STEPS):
                if 0 <= u - 3 < UNITS:
                    read_o(u - 3)
                if u < UNITS:
                    read_scores(u)
                if 0 <= u - 1 < UNITS:
                    combine(u - 1)
                j = (u - 19) // 16
                if j >= 0 and u == 16 * j + 19:
                    dve.wait_ge(asq_ready, j + 1)
                    V.tensor_reduce(out=ams[:, 0:16], in_=att_sq[:, :, :].rearrange("p i (a d) -> p (i a) d", d=VD),
                                    axis=AX.X, op=ALU.add).then_inc(ams_ready, 1)
                j = (u - 20) // 16
                if j >= 0 and u == 16 * j + 20:
                    y = att[:, 4 * j:4 * j + 4, :].rearrange("p i (a d) -> p (i a) d", d=VD)
                    dve.wait_ge(arms_ready, j + 1)
                    link(V.reciprocal(ams[:, 32:48], ams[:, 16:32]))
                    link(V.tensor_tensor(out=y, in0=y, op=ALU.mult,
                                         in1=ams[:, 32:48].rearrange("p (a o) -> p a o", o=1).to_broadcast([P, 16, VD])))
                    V.tensor_tensor(out=y, in0=y, op=ALU.mult,
                                    in1=gain_sub[:, :].rearrange("p (o d) -> p o d", o=1).to_broadcast([P, 16, VD])).then_inc(att_ready, 1)

            for hc in range(2):
                w0 = 2 * NI + hc * C_ITEMS
                n0 = hc * HT

                def mix_tail(t):
                    n, tok = n0 + t, slice(t * P, (t + 1) * P)
                    dve.wait_ge(mixhi_ready, n + 1)
                    V.tensor_tensor(out=h_lo[:, :, tok], in0=mix_in[n % 2][:, :, :], in1=f32(h_hi[:, :, tok]),
                                    op=ALU.subtract).then_inc(mix_ready, 1)

                mix_tail(0)
                for i in range(KC_OUT):
                    w_fold(w0 + i, 0)
                    w_tail(w0 + i, i)
                for t in range(HT):
                    n = n0 + t
                    if t + 1 < HT:
                        mix_tail(t + 1)
                    dve.wait_ge(xr_ld, 16 * (n + 1))
                    for cb in range(2):
                        o = 2 * n + cb
                        y = x_new[:, t, cb * BLK:(cb + 1) * BLK]
                        dve.wait_ge(wo_mm, o + 1)
                        V.tensor_tensor(out=y, in0=y, in1=psum[:, 4 + o % 4, :], op=ALU.add).then_inc(wo_read, 1)
                    dve.wait_ge(wo_read, 2 * (n + 1))
                    mean_square(NT + n, x_new[:, t, :])
                    if t:
                        dve.wait_ge(xt_ready, NT + n)
                    normalise(NT + n, x_new[:, t, :], xn2[:, :])
                    if t:
                        h_tail(NT + n - 1, h_tmp2)
                h_tail(NT + n0 + HT - 1, h_tmp2)

                def ff1_tail(g, q):
                    w_tail(2 * g + (w0 + KC_OUT), 2 * q)

                def ff2_fold(g):
                    w_fold(2 * g + (w0 + KC_OUT + 1), 1)

                def ff2_tail(g, q):
                    w_tail(2 * g + (w0 + KC_OUT + 1), 2 * q + 1)

                ff1_tail(0, 0)
                ff2_fold(0)
                ff2_tail(0, 0)

                def group(g, q, ahead):
                    def square(f):
                        dve.wait_ge(relu_ready, 4 * g + (4 * FG * hc + f + 1))
                        V.tensor_tensor(out=relu_t[f][:, :], in0=relu_t[f][:, :], in1=relu_t[f][:, :],
                                        op=ALU.mult).then_inc(sq_ready, 1)

                    def u_tail(f):
                        b, j = f // 2, f % 2
                        blk = slice(b * BLK, (b + 1) * BLK)
                        dve.wait_ge(uhi_ready, 4 * g + (4 * FG * hc + f + 1))
                        V.tensor_tensor(out=u_lo[:, j, blk], in0=relu_t[f][:, :], in1=f32(u_hi[:, j, blk]),
                                        op=ALU.subtract).then_inc(u_ready, 1)

                    def accumulate(q0):
                        for o in range(q0, q0 + 8):
                            t, cb = o // 2, o % 2
                            y = x_new[:, t, cb * BLK:(cb + 1) * BLK]
                            dve.wait_ge(ff2_mm, 16 * g + (16 * FG * hc + o + 1))
                            V.tensor_tensor(out=y, in0=y, in1=psum[:, 4 + o % 4, :], op=ALU.add).then_inc(ff2_read, 1)

                    square(0)
                    if ahead:
                        ff1_tail(g + 1, 1 - q)
                    u_tail(0)
                    square(1)
                    u_tail(1)
                    square(2)
                    if ahead:
                        ff2_fold(g + 1)
                    u_tail(2)
                    square(3)
                    u_tail(3)
                    accumulate(0)
                    if ahead:
                        ff2_tail(g + 1, 1 - q)
                    accumulate(8)

                with dve.Fori(0, FG // 2 - 1) as it:
                    for q in range(2):
                        group(it * 2 + q, q, True)
                group(FG - 2, 0, True)
                group(FG - 1, 1, False)

        @block.tensor
        def _(pe):
            M = nc.tensor.matmul

            def mm3(dst, terms):
                last = len(terms) - 1
                for n, (ah, al, bh, bl) in enumerate(terms):
                    M(dst, ah, bh, start=(n == 0), stop=False)
                    M(dst, ah, bl, start=False, stop=False)
                    ins = M(dst, al, bh, start=False, stop=(n == last))
                return ins

            def transposes(n, src):
                pe.wait_ge(xn_ready, n + 1)
                if n:
                    pe.wait_ge(hmod_ready, n)
                for k in range(DC):
                    ins = nc.tensor.transpose(ps_t[:, k, :], src[:, k * P:(k + 1) * P], ident[:, :])
                ins.then_inc(xt_ready, 1)

            pe.wait_ge(const_ready, 1)
            pe.wait_ge(tab_ld, 16 * 10)
            nc.tensor.transpose(psum[:, 0, 0:R_END1], table1[:, :], ident[0:R_END1, 0:R_END1])
            nc.tensor.transpose(psum[:, 1, 0:R_END2], table2[:, :], ident[0:R_END2, 0:R_END2]).then_inc(tab_t, 1)
            pe.wait_ge(siluc_ready, 1)
            for k in range(DC):
                pe.wait_ge(ada0_ld[k % 4], 16 * (k // 4 + 1))
                for m in range(2 * DC):
                    ins = M(psum[:, 7, m:m + 1], ada_first[k % 4][:, m * P:(m + 1) * P], silu_c[:, k:k + 1],
                            start=(k == 0 and m == 0), stop=(k == DC - 1), skip_group_check=True)
                ins.then_inc(ada0_used if k < DC - 1 else mod1_mm, 1)
            pe.wait_ge(tab_col, 2)
            transposes(0, x_in[0])

            def free(o):
                if o >= 3:
                    pe.wait_ge(*released(o - 3))

            def item_ready(w):
                pe.wait_ge(wlo_ready, w + 1)

            def w8(w, part):
                return by_k8(part[w % 3][:, :])

            def project_rows(h, t, w, dst):
                tok = slice(t * P, (t + 1) * P)
                wh, wl = w8(w, w_hi), w8(w, w_lo)
                return mm3(dst, [(h_hi[:, k, tok], h_lo[:, k, tok], wh[:, k, :], wl[:, k, :]) for k in range(DC)])

            def project_cols(kind, h, w):
                item_ready(w)
                wh, wl = w8(w, w_hi), w8(w, w_lo)
                for b in range(NB):
                    for cc in range(GC):
                        o = OUT_NO[kind, h, cc, b]
                        free(o)
                        col, tok = slice(cc * P, (cc + 1) * P), slice(b * BLK, (b + 1) * BLK)
                        ins = mm3(bank(o), [(wh[:, k, col], wl[:, k, col], h_hi[:, k, tok], h_lo[:, k, tok])
                                            for k in range(DC)])
                        ins.then_inc(proj_ready, 1)

            def modulation(h, k):
                pe.wait_ge(ada_ld, 32 * (h * DC + k + 1))
                if h and k == 0:
                    pe.wait_ge(mod2_ready, 1)
                for n in range(2):
                    M(psum[:, 5 + n, :], silu_c[:, k:k + 1].to_broadcast([P, P]), ada[:, n * BLK:(n + 1) * BLK],
                      start=(k == 0), stop=(k == DC - 1), skip_group_check=True)
                for m in range(DC):
                    ins = M(psum[:, 7, m:m + 1], ada[:, D + m * P:D + (m + 1) * P], silu_c[:, k:k + 1],
                            start=(k == 0 and m == 0), stop=(k == DC - 1), skip_group_check=True)
                ins.then_inc(ada_used, 1)

            def layer_norm(h):
                pe.wait_ge(conv_ready, h + 1)
                for b in range(NB):
                    for s in (0, 1):
                        o = OUT_NO["ln", h, b, s]
                        free(o)
                        if s:
                            pe.wait_ge(lnsq_ready, h * NB + b + 1)
                        for cc in range(GC):
                            src = ln_sq[:, cc, :] if s else acc[:, cc, b * BLK:(b + 1) * BLK]
                            ins = M(bank(o), ones_mean[:, :], src, start=(cc == 0), stop=(cc == GC - 1))
                        ins.then_inc(proj_ready, 1)

            for h in range(2):
                w0 = h * NI
                for t in range(HT):
                    n = h * HT + t
                    if n + 1 < NT:
                        transposes(n + 1, x_in[(n + 1) % 2])
                    o = OUT_NO["qk", h, t, 0]
                    pe.wait_ge(h_ready, n + 1)
                    free(o)
                    item_ready(w0)
                    project_rows(h, t, w0, bank(o)[:, 0:GW])
                    item_ready(w0 + 1)
                    project_rows(h, t, w0 + 1, bank(o)[:, GW:2 * GW]).then_inc(proj_ready, 1)
                item_ready(w0 + 2)
                for t in range(0, HT, 2):
                    o = OUT_NO["v", h, t, 0]
                    free(o)
                    project_rows(h, t, w0 + 2, bank(o)[:, 0:GW])
                    project_rows(h, t + 1, w0 + 2, bank(o)[:, GW:2 * GW]).then_inc(proj_ready, 1)
                modulation(h, 0)
                if h:
                    layer_norm(0)
                project_cols("ud", h, w0 + 3)
                modulation(h, 1)
                project_cols("gate", h, w0 + 4)
                modulation(h, 2)
                for b in range(NB):
                    for cc in range(GC):
                        o = OUT_NO["pool", h, cc, b]
                        free(o)
                        pe.wait_ge(pool_y, chan_no(h, cc, b) + 1)
                        if h == 0 and b == 0 and cc == 0:
                            pe.wait_ge(bc_ld, 16 * BROADCASTS)
                        M(bank(o), pool_blk[:, cc, :], pool_in[:, cc, b * BLK:(b + 1) * BLK],
                          start=True, stop=True).then_inc(proj_ready, 1)
                modulation(h, 3)
                for k, (kind, i) in enumerate((("val", 5), ("cg", 6), ("xc", 7), ("bg", 8))):
                    project_cols(kind, h, w0 + i)
                    modulation(h, 4 + k)
            layer_norm(1)

            for o in range(len(OUTS) - 3, len(OUTS)):
                pe.wait_ge(*released(o))
            pe.wait_ge(mod2_ready, 2)
            pe.wait_ge(hmod_ready, NT)

            def fill(x):
                kind, i, f = FILLS[x]
                if x:
                    pe.wait_ge(x_read, x)
                if kind == "stack":
                    a = f // 2
                    pe.wait_ge(split_lo, 2 * i + a + 1)
                    src = f32((k_split if a else q_split)[:, :, :, :]).rearrange("p m s d -> p m (s d)")
                    srcs = [src[:, 4 * (f % 2) + m, :] for m in range(4)]
                else:
                    pe.wait_ge(att_ready, i + 1)
                    srcs = [att[:, 4 * i + t, f * P:(f + 1) * P] for t in range(4)]
                for m, s in enumerate(srcs):
                    ins = nc.tensor.transpose(psum[:, 7, m * P:(m + 1) * P], s, ident[:, :])
                ins.then_inc(x_fill, 1)

            def score(u):
                i, hd = u // HEADS, u % HEADS
                if hd == 0:
                    pe.wait_ge(x_read, FILL_NO["stack", i, 3] + 1)
                r = SC_NO[u]
                for m in range(2):
                    for c0, n in sc_chunks(i):
                        if r >= 4:
                            pe.wait_ge(sc_read, r - 3)
                        diag = c0 + n == (i + 1) * P
                        ins = M(psum[:, r % 4, 0:n], q_stack[i % 2][:, 2 * hd + m, :], k_stack[:, 2 * hd + m, c0:c0 + n],
                                start=True, stop=not diag, skip_group_check=diag)
                        if diag:
                            ins = M(psum[:, r % 4, n - P:n], ident_r[:, :], mask_r[:, :], start=False, stop=True,
                                    skip_group_check=True)
                        ins.then_inc(sc_mm, 1)
                        r += 1

            def attend(u):
                i, hd = u // HEADS, u % HEADS
                s = u % 3
                pe.wait_ge(a_ready, u + 1)
                groups = at_groups(u)
                if u == 0:
                    pe.wait_ge(v_ld, 16)

                def turn(g):
                    gn, (k0, nk) = AT_NO[u] + g, groups[g]
                    if gn >= 2:
                        pe.wait_ge(at_ready, gn - 1)
                    for k in range(nk):
                        ins = nc.tensor.transpose(psum[:, 4 + gn % 2, k * P:(k + 1) * P],
                                                  scores[s][:, 0, (k0 + k) * P:(k0 + k + 1) * P], ident[:, :])
                    ins.then_inc(at_mm, 1)

                def product(g):
                    gn, (k0, nk) = AT_NO[u] + g, groups[g]
                    pe.wait_ge(at_ready, gn + 1)
                    if g == 0 and u:
                        pe.wait_ge(o_read, u)
                    for k in range(nk):
                        ins = M(psum[:, 6, 0:VD], a_t[gn % 2][:, k * P:(k + 1) * P],
                                v_sb[:, k0 + k, hd * VD:(hd + 1) * VD], start=(k0 + k == 0), stop=(k0 + k == i))
                    ins.then_inc(pv_mm, 1)

                turn(0)
                for g in range(1, len(groups)):
                    turn(g)
                    product(g - 1)
                product(len(groups) - 1)

            for x in range(4):
                fill(x)
            for u in range(STEPS):
                for x in fills_at(u):
                    fill(x)
                if u < UNITS:
                    score(u)
                if 0 <= u - 2 < UNITS:
                    attend(u - 2)

            pe.wait_ge(x_read, len(FILLS))
            pe.wait_ge(o_read, UNITS)
            pe.wait_ge(sc_read, SC_NO[UNITS])
            pe.wait_ge(at_ready, AT_NO[UNITS])
            for hc in range(2):
                w0 = 2 * NI + hc * C_ITEMS
                n0 = hc * HT
                for t in range(HT):
                    n, tok = n0 + t, slice(t * P, (t + 1) * P)
                    pe.wait_ge(mix_ready, n + 1)
                    for cb in range(2):
                        o, col = 2 * n + cb, slice(cb * BLK, (cb + 1) * BLK)
                        if t >= 2:
                            pe.wait_ge(wo_read, o - 3)
                        elif hc:
                            pe.wait_ge(ff2_read, FG * 2 * HT - 3 + 2 * t + cb)
                        for i in range(KC_OUT):
                            if t == 0 and cb == 0:
                                item_ready(w0 + i)
                            for kk in range(2):
                                k = 2 * i + kk
                                wh, wl = by_k2(w_hi[i][:, :])[:, kk, col], by_k2(w_lo[i][:, :])[:, kk, col]
                                M(psum[:, 4 + o % 4, :], h_hi[:, k, tok], wh, start=(k == 0), stop=False)
                                M(psum[:, 4 + o % 4, :], h_hi[:, k, tok], wl, start=False, stop=False)
                                ins = M(psum[:, 4 + o % 4, :], h_lo[:, k, tok], wh, start=False, stop=(k == DC - 1))
                        ins.then_inc(wo_mm, 1)
                    if t:
                        transposes(NT + n - 1, xn2)
                transposes(NT + n0 + HT - 1, xn2)

                def group(g, q, first=False):
                    w = 2 * g + (w0 + KC_OUT)
                    s1, s2 = 2 * q, 2 * q + 1
                    pe.wait_ge(wlo_ready, w + 1)
                    for b in range(NB):
                        for j in range(2):
                            f = 2 * b + j
                            if not (first and b == 0):
                                pe.wait_ge(relu_ready, 4 * g + (4 * FG * hc + f - 1))
                            if first:
                                pe.wait_ge(h_ready, NT + n0 + 4 * (b + 1))
                            col, tok = slice(j * P, (j + 1) * P), slice(b * BLK, (b + 1) * BLK)
                            wh, wl = by_k8(w_hi[s1][:, :]), by_k8(w_lo[s1][:, :])
                            ins = mm3(psum[:, 2 + f % 2, :], [(wh[:, k, col], wl[:, k, col], h_hi[:, k, tok], h_lo[:, k, tok])
                                                              for k in range(DC)])
                            ins.then_inc(ff1_mm, 1)
                    pe.wait_ge(wlo_ready, w + 2)
                    wh, wl = by_k2(w_hi[s2][:, :]), by_k2(w_lo[s2][:, :])
                    for o in range(2 * HT):
                        t, cb = o // 2, o % 2
                        tok, col = slice(t * P, (t + 1) * P), slice(cb * BLK, (cb + 1) * BLK)
                        if o % 8 == 0:
                            pe.wait_ge(u_ready, 4 * g + (4 * FG * hc + o // 4 + 2))
                        if first and o < 4:
                            pe.wait_ge(wo_read, 2 * (n0 + HT) - 3 + o)
                        else:
                            pe.wait_ge(ff2_read, 16 * g + (16 * FG * hc + o - 3))
                        ins = mm3(psum[:, 4 + o % 4, :], [(u_hi[:, j, tok], u_lo[:, j, tok], wh[:, j, col], wl[:, j, col])
                                                          for j in range(2)])
                        ins.then_inc(ff2_mm, 1)

                group(0, 0, first=True)
                group(1, 1)
                with pe.Fori(1, FG // 2) as it:
                    for q in range(2):
                        group(it * 2 + q, q)


INPUTS = ["x", "c", "w_ada", "b_ada", "norm1_g", "norm2_g", "w_in", "w_out", "q_norm_g", "k_norm_g",
          "lam_params", "attn_sub_g", "conf_dw_w", "conf_dw_b", "conf_ln_g", "conf_ln_b", "short_conv_w",
          "pool_w", "pool_scale", "w_ff1", "w_ff2"]


def kernel(**inputs):
    import numpy as np
    import concourse.bacc as bacc
    from concourse.bass_utils import run_bass_kernel_spmd

    nc = bacc.Bacc("TRN2", target_bir_lowering=False, num_devices=1)
    arrays, args = {}, []
    for name in INPUTS:
        a = np.ascontiguousarray(inputs[name])
        arrays["in_" + name] = a
        args.append(nc.dram_tensor("in_" + name, a.shape, mybir.dt.from_np(a.dtype), kind="ExternalInput").ap())
    out = nc.dram_tensor("out", (1, SEQ, D), F32, kind="ExternalOutput").ap()
    trunk(nc, *args, out)
    r = run_bass_kernel_spmd(nc, [arrays], core_ids=[0])
    return r.results[0]["out"]
```

```python
from contextlib import ExitStack

import concourse.bass as bass
from concourse import mybir

F32 = mybir.dt.float32
F32R = mybir.dt.float32r
ALU = mybir.AluOpType
ACT = mybir.ActivationFunctionType
AX = mybir.AxisListType

P = 128
SEQ = 2048
D = 1024
DC = D // P
NT = SEQ // P
HALF = SEQ // 2
HT = HALF // P
BLK = 512
NB = HALF // BLK
GW = 256
GC = GW // P
D_FF = 4 * D
HEADS, QKD, VD = 4, 32, 64
MAPS = 2 * HEADS
SCALE = QKD ** -0.5
LAM_INIT = 0.2
EPS = 1e-6
TAPS = 31
STAPS = 3
POOL_HALO = 16
NEG = -1.0e30

Q0, K0, V0, VAL0, GATE0, BG0, CG0, XC0, UD0 = range(0, 9 * GW, GW)
ITEMS = [("q", Q0), ("k", K0), ("v", V0), ("gate", GATE0), ("val", VAL0), ("ud", UD0),
         ("cg", CG0), ("xc", XC0), ("bg", BG0)]
NI = len(ITEMS)
ITEM = DC * GW
KC_OUT = 4
FG = D_FF // GW
C_ITEMS = KC_OUT + 2 * FG
BROADCASTS = 10

R_C, R_B, R_N1, R_N2 = 0, 8, 56, 64
R_DWB, R_LNG, R_LNB, R_PSC, R_END1 = 72, 74, 76, 78, 80
R_DWW, R_SW, R_END2 = 0, 62, 68


def projections():
    chan = [(b, c) for b in range(NB) for c in range(GC)]
    out = []

    def ln(h, b):
        return [("ln", h, b, s) for s in (0, 1)]

    for h in range(2):
        for t in range(0, HT, 2):
            out += [("qk", h, t, 0), ("qk", h, t + 1, 0), ("v", h, t, 0)]
        for kind in ("gate", "val", "ud", "cg", "pool", "xc", "bg"):
            if h and kind in ("gate", "val", "bg"):
                out += {"gate": ln(0, 0), "val": ln(0, 1), "bg": ln(1, 0)}[kind]
            out += [(kind, h, c, b) for b, c in chan]
    return out + ln(1, 1)


UNITS = NT * HEADS
STEPS = UNITS + 7


def fills_of(u):
    out = [("stack", u // HEADS + 1, u % HEADS)] if u // HEADS + 1 < NT else []
    return out + [("att", j, f) for j in range(NT // 4) for f in range(GC) if u == 16 * j + 21 + f]


FILLS = [("stack", 0, f) for f in range(4)] + [x for u in range(STEPS) for x in fills_of(u)]
FILL_NO = {x: n for n, x in enumerate(FILLS)}


def fills_at(u):
    return [FILL_NO[x] for x in fills_of(u)]


def splits_at(u):
    return [(n, a) for n in range(1, NT) for a in range(2) if u == max(0, 4 * n - 6 + 2 * a)]


def sc_chunks(i):
    n = (i + 1) * P
    return [(c0, min(BLK, n - c0)) for c0 in range(0, n, BLK)]


def at_groups(u):
    n = u // HEADS + 1
    return [(k0, min(4, n - k0)) for k0 in range(0, n, 4)]


def running(counts):
    out = [0]
    for n in counts:
        out.append(out[-1] + n)
    return out


SC_NO = running(2 * len(sc_chunks(u // HEADS)) for u in range(UNITS))
AT_NO = running(len(at_groups(u)) for u in range(UNITS))


def trunk(nc, x, c, w_ada, b_ada, norm1_g, norm2_g, w_in, w_out, q_norm_g, k_norm_g, lam_params,
          attn_sub_g, conf_dw_w, conf_dw_b, conf_ln_g, conf_ln_b, short_conv_w, pool_w, pool_scale,
          w_ff1, w_ff2, out):
    ctx = ExitStack()
    with ctx:
        KB = 1024
        base = 16512

        def sb(name, kb, shape, dt=F32):
            return nc.alloc_sbuf_tensor_at("sb_" + name, shape, dt, offset=base + int(kb * KB))

        def sem(name):
            return ctx.enter_context(nc.semaphore(name))

        qkv_d = nc.dram_tensor("qkv_scratch", (SEQ, 3 * GW), F32).ap()
        mix_d = nc.dram_tensor("mix_scratch", (D, SEQ), F32).ap()

        ident = sb("ident", 0, [P, P])
        ident_r = sb("ident_r", 0.5, [P, P], F32R)
        mask_r = sb("mask_r", 1, [P, P], F32R)
        ones_mean = sb("ones_mean", 1.5, [P, P])
        pool_blk = sb("pool_blk", 2, [P, GC, P])
        col1 = sb("col1", 3, [P, R_END1])
        col2 = sb("col2", 3.375, [P, R_END2])
        gain_qk = sb("gain_qk", 3.75, [P, 2, QKD])
        gain_sub = sb("gain_sub", 4, [P, VD])
        lam_in = sb("lam_in", 4.25, [P, 4, QKD])
        small = sb("small", 4.75, [P, 96])
        silu_c = sb("silu_c", 5.125, [P, DC])
        gain1 = sb("gain1", 5.1875, [P, DC])
        shift1 = sb("shift1", 5.25, [P, DC])
        gain2 = sb("gain2", 5.3125, [P, DC])
        shift2 = sb("shift2", 5.375, [P, DC])
        inv_win = sb("inv_win", 5.4375, [P, GC])
        inv_first = sb("inv_first", 5.5, [P, GC, POOL_HALO])
        bn = sb("bn", 5.6875, [P, 2, 6])
        stat = sb("stat", 5.75, [P, 16])
        diag_sum = sb("diag_sum", 5.8125, [P, 2 * DC])
        eps_col, lam_neg = small[:, 0:1], small[:, 1:2]
        gate_row = sb("gate_row", 6, [P, 2, D])
        h_hi = sb("h_hi", 14, [P, DC, HALF], F32R)
        h_lo = sb("h_lo", 46, [P, DC, HALF], F32R)
        w_hi = [sb(f"w_hi{s}", 78 + 16 * s, [P, ITEM], F32R) for s in range(4)]
        w_lo = [sb(f"w_lo{s}", 86 + 16 * s, [P, ITEM], F32R) for s in range(4)]
        w_raw = sb("w_raw", 142, [P, ITEM])
        gated = sb("gated", 126, [P, GC, HALF])
        acc = sb("acc", 134, [P, GC, HALF])
        at = 150
        x_in = [sb(f"x_in{s}", at + 4 * s, [P, D]) for s in range(2)]
        h_tmp = sb("h_tmp", 158, [P, DC, P])
        conf = sb("conf", 162, [P, GC, TAPS - 1 + HALF])
        halo2 = sb("halo2", 170.25, [P, GC, 2])
        prod = sb("prod", 170.5, [P, GC, 2 + HALF])
        pool_in = sb("pool_in", 170.5, [P, GC, HALF])
        ln_sq = [sb(f"ln_sq{h}", k, [P, GC, BLK]) for h, k in enumerate((170.5, 191.75))]
        ln_sig = [sb(f"ln_sig{h}", k, [P, BLK]) for h, k in enumerate((174.5, 195.75))]
        ln_rs = [sb(f"ln_rs{h}", k, [P, BLK]) for h, k in enumerate((176.5, 197.75))]
        stage = [sb(f"stage{s}", 179 + 2 * s, [P, BLK]) for s in range(2)]
        ud = sb("ud", 183, [P, GC, POOL_HALO + BLK])
        win_a = sb("win_a", 187.25, [P, POOL_HALO + BLK])
        win_b = sb("win_b", 189.5, [P, POOL_HALO + BLK])
        ada = sb("ada", 191.75, [P, 2 * D])
        qk_sq = sb("qk_sq", 199.75, [P, BLK])
        qkv_out = [sb(f"qkv_out{s}", 201.75 + 2 * s, [P, BLK]) for s in range(2)]
        ada_first = [sb(f"ada_first{s}", k, [P, 2 * D]) for s, k in enumerate((126, 134, 162, 171))]
        table1 = sb("table1", 183, [R_END1, P])
        table2 = sb("table2", 183.5, [R_END2, P])
        k_stack = sb("k_stack", 14, [P, MAPS, SEQ], F32R)
        scores = [sb(f"scores{s}", 94 + 16 * s, [P, 2, SEQ]) for s in range(3)]
        v_sb = sb("v_sb", 150, [P, NT, GW])
        att = sb("att", 166, [P, NT, GW])
        q_stack = [sb(f"q_stack{s}", 182 + 4 * s, [P, MAPS, P], F32R) for s in range(2)]
        q_split = sb("q_split", 190, [P, MAPS, 4, QKD], F32R)
        k_split = sb("k_split", 194, [P, MAPS, 4, QKD], F32R)
        qk_in = [sb(f"qk_in{s}", 198 + 2 * s, [P, 2, GW]) for s in range(2)]
        a_t = [sb(f"a_t{s}", 202 + 2 * s, [P, BLK]) for s in range(2)]
        att_sq = sb("att_sq", 78, [P, 4, GW])
        att_t = [sb(f"att_t{s}", 82 + 4 * s, [P, GC, BLK]) for s in range(2)]
        bst = sb("bst", 90, [P, 3, 24])
        inv_s = sb("inv_s", 90.5, [P, 4])
        ams = sb("ams", 91, [P, 48])
        x_new = sb("x_new", 150, [P, HT, D])
        u_hi = sb("u_hi", 182, [P, 2, HALF], F32R)
        u_lo = sb("u_lo", 190, [P, 2, HALF], F32R)
        mix_in = [sb(f"mix_in{s}", 182 + 4 * s, [P, DC, P]) for s in range(2)]
        mix_early = [sb(f"mix_early{s}", 198 + 4 * s, [P, DC, P]) for s in range(2)]
        w_raw_x = [sb(f"w_raw_x{s}", 166 + 8 * s, [P, ITEM]) for s in range(2)]
        wo_gated = sb("wo_gated", 194, [P, BLK])
        relu_t = [sb(f"relu_t{s}", 198 + 2 * s, [P, BLK]) for s in range(4)]
        xn2 = sb("xn2", 198, [P, D])
        h_tmp2 = sb("h_tmp2", 202, [P, DC, P])

        psum = ctx.enter_context(nc.psum_tensor("ps", [P, 8, BLK], F32))
        ps_t = psum[:, 0:2, :].rearrange("p a b -> p (a b)").rearrange("p (k t) -> p k t", t=P)

        tab_ld, bc_ld, dve_chain, act_chain, pool_chain = [sem(n) for n in (
            "tab_ld", "bc_ld", "dve_chain", "act_chain", "pool_chain")]
        const_ready, tab_t, tab_col, sigc_ready, siluc_ready = [sem(n) for n in (
            "const_ready", "tab_t", "tab_col", "sigc_ready", "siluc_ready")]
        ada0_ld = [sem(f"ada0_ld{s}") for s in range(4)]
        ada0_used, mod1_mm, mod1_ready = sem("ada0_used"), sem("mod1_mm"), sem("mod1_ready")
        ada_ld, ada_used = sem("ada_ld"), sem("ada_used")
        lam_sums, lam_exp = sem("lam_sums"), sem("lam_exp")
        qk_ready = sem("qk_ready")
        x_ld = [sem(f"x_ld{s}") for s in range(2)]
        ms_ready, rms_ready, xn_ready, xt_ready = [sem(n) for n in (
            "ms_ready", "rms_ready", "xn_ready", "xt_ready")]
        hmod_ready, hhi_ready, h_ready = sem("hmod_ready"), sem("hhi_ready"), sem("h_ready")
        w_ld, w_folded, whi_ready, wlo_ready = [sem(n) for n in (
            "w_ld", "w_folded", "whi_ready", "wlo_ready")]
        proj_ready = sem("proj_ready")
        qsq_ready, qss_ready, qrms_ready, qn_ready = [sem(n) for n in (
            "qsq_ready", "qss_ready", "qrms_ready", "qn_ready")]
        qkv_ready, qkv_st = sem("qkv_ready"), [sem(f"qkv_st{s}") for s in range(2)]
        v_ready, gated_ready, conf_ready, conv_ready, prod_ready, short_ready = [sem(n) for n in (
            "v_ready", "gated_ready", "conf_ready", "conv_ready", "prod_ready", "short_ready")]
        lnd_ready, lnsq_ready, lnsd_ready, lnz_ready, lny_ready, lnsig_ready, lnout_ready = [sem(n) for n in (
            "lnd_ready", "lnsq_ready", "lnsd_ready", "lnz_ready", "lny_ready", "lnsig_ready", "lnout_ready")]
        ud_ready, win_ready, pool_y, halo_saved, poolout_ready = [sem(n) for n in (
            "ud_ready", "win_ready", "pool_y", "halo_saved", "poolout_ready")]
        stage_st, ln_st, mod2_ready = [sem("stage_st0"), sem("stage_st1")], sem("ln_st"), sem("mod2_ready")
        qk_ld, v_ld = [sem("qk_ld0"), sem("qk_ld1")], sem("v_ld")
        split_hi, split_lo, x_fill, x_read = [sem(n) for n in ("split_hi", "split_lo", "x_fill", "x_read")]
        sc_mm, sc_read, max_ready, exp_done, a_ready = [sem(n) for n in (
            "sc_mm", "sc_read", "max_ready", "exp_done", "a_ready")]
        at_mm, at_ready, pv_mm, pv_done, o_read = [sem(n) for n in (
            "at_mm", "at_ready", "pv_mm", "pv_done", "o_read")]
        asq_ready, ams_ready, arms_ready, att_ready = [sem(n) for n in (
            "asq_ready", "ams_ready", "arms_ready", "att_ready")]
        attt_st = [sem("attt_st0"), sem("attt_st1")]
        mix_ld = [sem("mix_ld0"), sem("mix_ld1")]
        wx_ld = [sem("wx_ld0"), sem("wx_ld1")]
        mixhi_ready, mix_ready, xr_ld, wo_mm, wo_read = [sem(n) for n in (
            "mixhi_ready", "mix_ready", "xr_ld", "wo_mm", "wo_read")]
        ff1_mm, relu_ready, sq_ready, uhi_ready, u_ready = [sem(n) for n in (
            "ff1_mm", "relu_ready", "sq_ready", "uhi_ready", "u_ready")]
        ff2_mm, ff2_read, out_st = [sem(n) for n in ("ff2_mm", "ff2_read", "out_st")]

        OUTS = projections()
        OUT_NO = {o: n for n, o in enumerate(OUTS)}

        def bank(o):
            return psum[:, (2, 3, 4, 7)[o % 4], :]

        def chan_no(h, cc, b):
            return (h * NB + b) * GC + cc

        def released(o):
            kind, h, a, b = OUTS[o]
            if kind == "qk":
                return qn_ready, h * HT + a + 1
            if kind == "v":
                return v_ready, h * HT // 2 + a // 2 + 1
            if kind == "ln":
                return (lnsd_ready if b else lnd_ready), h * NB + a + 1
            n = chan_no(h, a, b)
            if kind in ("gate", "cg"):
                return gated_ready, n + h * NB * GC + (NB * GC if kind == "cg" else 0) + 1
            return {"ud": ud_ready, "pool": poolout_ready, "val": conf_ready, "xc": prod_ready,
                    "bg": short_ready}[kind], n + 1

        w_in_v = w_in.rearrange("a (k p) n -> p (a k) n", p=P)
        w_out_v = w_out.rearrange("a (k p) n -> p (a k) n", p=P)
        w_ff1_v = w_ff1.rearrange("a (k p) n -> p (a k) n", p=P)
        w_ff2_v = w_ff2.rearrange("a (k p) n -> p (a k) n", p=P)
        w_ada_v = w_ada.rearrange("a (k p) n -> p (a k) n", p=P)
        x_v = x.rearrange("a (t p) d -> p (a t) d", p=P)
        out_v = out.rearrange("a (t p) d -> p (a t) d", p=P)
        qkv_v = qkv_d.rearrange("(t p) d -> p t d", p=P)
        mix_v = mix_d.rearrange("(k p) t -> p k t", p=P)

        def used(w):
            h, i = divmod(w, NI)
            if i < 3:
                last = ("v", h, HT - 2, 0) if i == 2 else ("qk", h, HT - 1, 0)
            else:
                last = (ITEMS[i][0], h, GC - 1, NB - 1)
            return proj_ready, OUT_NO[last] + 1

        def qk_turn(n):
            return n // 2 * 3 + n % 2

        def v_turn(h, t):
            return (h * HT + t) // 2 * 3 + 2

        def slot_of_qk(n):
            return qk_turn(n) % 2

        def slot_of_v(h, t):
            return v_turn(h, t) % 2

        def stores_before_qk(n):
            return qk_turn(n) // 2

        def stores_before_v(h, t):
            return v_turn(h, t) // 2

        def stores_of_stage(n, short):
            return (2 * NB * GC * (n // (NB * GC)) + NB * GC * short + n % (NB * GC)) // 2

        def heads_tails(a):
            if a == 0:
                return q_split[:, :, 0:2, :], q_split[:, :, 2:4, :]
            return k_split[:, :, 0:4:2, :], k_split[:, :, 1:4:2, :]

        def mix_buf(n):
            return mix_early[n % 2] if n in (HT, HT + 1) else mix_in[n % 2]

        def wo_slot(hc, i):
            return i if hc else (i + 1) % 4

        def wo_raw(hc, i):
            return w_raw_x[i - 1] if hc == 0 and i in (1, 2) else w_raw

        def loaded(w):
            return w_ld, (w - 1) * 16

        def wo_loaded(hc, i):
            if hc == 0 and i < 3:
                return (wx_ld[i - 1], 16) if i else (w_ld, (2 * NI + 1) * 16)
            return loaded(2 * NI + hc * C_ITEMS + i)

        def by_k8(a):
            return a.rearrange("p (k n) -> p k n", k=DC)

        def by_k2(a):
            return a.rearrange("p (k n) -> p k n", k=2)

        def f32(ap):
            return ap.bitcast(F32)

        block = ctx.enter_context(nc.Block())

        @block.sync
        def _(sp):
            def rows(src):
                return src.rearrange("o (a p) -> (o a) p", p=P)
            for r0, r1, src in ((R_C, R_B, c), (R_B, R_N1, b_ada), (R_N1, R_N2, norm1_g), (R_N2, R_DWB, norm2_g),
                                (R_DWB, R_LNG, conf_dw_b), (R_LNG, R_LNB, conf_ln_g),
                                (R_LNB, R_PSC, conf_ln_b), (R_PSC, R_END1, pool_scale)):
                sp.dma_start(table1[r0:r1, :], rows(src)).then_inc(tab_ld, 16)
            for r0, r1, src in ((R_DWW, R_SW, conf_dw_w), (R_SW, R_END2, short_conv_w)):
                sp.dma_start(table2[r0:r1, :], src.rearrange("o j (a p) -> (o j a) p", p=P)).then_inc(tab_ld, 16)
            def load_small():
                sp.wait_ge(const_ready, 1)
                for g in range(4):
                    r = 64 * (g % 2)
                    sp.dma_start(pool_blk[r:r + 64, g // 2, r:r + 64], pool_w[0, g, :, :]).then_inc(bc_ld, 16)
                for dst, src in ((gain_qk[:, 0, :], q_norm_g[0, :]), (gain_qk[:, 1, :], k_norm_g[0, :]),
                                 (gain_sub[:, :], attn_sub_g[0, :]), (lam_in[:, :, :], lam_params[0, :, :]),
                                 (gate_row[:, 0, :], b_ada[0, 2 * D:3 * D]), (gate_row[:, 1, :], b_ada[0, 5 * D:6 * D])):
                    sp.dma_start(dst, src.partition_broadcast(P)).then_inc(bc_ld, 16)

            def raw_free(w):
                sp.wait_ge(whi_ready, w)
                sp.wait_ge(wlo_ready, w)

            def load_w_in(w):
                if w:
                    raw_free(w)
                c0 = ITEMS[w % NI][1]
                sp.dma_start(by_k8(w_raw[:, :]), w_in_v[:, :, c0:c0 + GW]).then_inc(w_ld, 16)

            for k in range(DC):
                if k == 4:
                    load_small()
                if k >= 4:
                    sp.wait_ge(ada0_used, k - 3)
                sp.dma_start(ada_first[k % 4][:, :], w_ada_v[:, k, 0:2 * D]).then_inc(ada0_ld[k % 4], 16)
                if k == 3:
                    for n in range(2):
                        sp.dma_start(x_in[n][:, :], x_v[:, n, :]).then_inc(x_ld[n], 16)
                    load_w_in(0)

            def load_x(n):
                if n >= 2:
                    sp.wait_ge(xt_ready, n - 1)
                sp.dma_start(x_in[n % 2][:, :], x_v[:, n, :]).then_inc(x_ld[n % 2], 16)

            def load_ada(h, k):
                if h * DC + k:
                    sp.wait_ge(ada_used, h * DC + k)
                gate0, norm0 = (2 + 3 * h) * D, (3 + h) * D
                sp.dma_start(ada[:, 0:D], w_ada_v[:, k, gate0:gate0 + D]).then_inc(ada_ld, 16)
                sp.dma_start(ada[:, D:2 * D], w_ada_v[:, k, norm0:norm0 + D]).then_inc(ada_ld, 16)

            def store_qk(n):
                sp.wait_ge(qk_ready, n + 1)
                s = slot_of_qk(n)
                sp.dma_start(qkv_v[:, n, 0:2 * GW], qkv_out[s][:, :]).then_inc(qkv_st[s], 16)

            def store_v(h, t):
                s = slot_of_v(h, t)
                sp.wait_ge(v_ready, h * HT // 2 + t // 2 + 1)
                sp.dma_start(qkv_v[:, h * HT + t:h * HT + t + 2, 2 * GW:3 * GW],
                             qkv_out[s][:, :].rearrange("p (t d) -> p t d", t=2)).then_inc(qkv_st[s], 16)

            def store_mixer(h, chunk, ready):
                for b in range(NB):
                    for cc in range(GC):
                        n = chan_no(h, cc, b)
                        t0 = h * HALF + b * BLK
                        sp.wait_ge(ready, n + 1)
                        sp.dma_start(mix_v[:, chunk + cc, t0:t0 + BLK], stage[n % 2][:, :]).then_inc(stage_st[n % 2], 16)

            def store_ln(h):
                sp.wait_ge(lnout_ready, GC * NB * (h + 1))
                sp.dma_start(mix_v[:, 2:4, h * HALF:(h + 1) * HALF], acc[:, :, :]).then_inc(ln_st, 16)

            def store_turn(n):
                store_qk(n)
                if n % 2:
                    store_v(n // HT, n % HT - 1)

            load_w_in(1)
            for h in range(2):
                w0 = h * NI
                for t in range(HT):
                    n = h * HT + t
                    if t == 0:
                        load_w_in(w0 + 2)
                    if n + 2 < NT:
                        load_x(n + 2)
                    if t >= 2:
                        store_turn(n - 2)
                    if t == 2:
                        load_w_in(w0 + 3)
                    if t == 3:
                        load_ada(h, 0)
                store_turn(h * HT + HT - 2)
                load_w_in(w0 + 4)
                store_turn(h * HT + HT - 1)
                load_ada(h, 1)
                load_w_in(w0 + 5)
                load_w_in(w0 + 6)
                load_ada(h, 2)
                load_ada(h, 3)
                if h:
                    store_ln(0)
                load_w_in(w0 + 7)
                load_ada(h, 4)
                load_w_in(w0 + 8)
                load_ada(h, 5)
                if h == 0:
                    load_w_in(NI)
                load_ada(h, 6)
                store_mixer(h, 6, poolout_ready)
                load_ada(h, 7)
                if h == 0:
                    load_w_in(NI + 1)
                store_mixer(h, 4, short_ready)
            store_ln(1)

            for s in range(2):
                sp.wait_ge(qkv_st[s], 16 * (NT + NT // 2) // 2)
                sp.wait_ge(stage_st[s], 16 * 4 * NB * GC // 2)
            sp.wait_ge(proj_ready, len(OUTS))
            sp.wait_ge(mod2_ready, 2)
            sp.wait_ge(h_ready, NT)
            def load_w_out(hc, i):
                w = 2 * NI + hc * C_ITEMS + i
                raw = wo_raw(hc, i)
                if raw is w_raw:
                    raw_free(w if hc or i == 0 else w - 2)
                sp.dma_start(by_k2(raw[:, :]), w_out_v[:, 2 * i:2 * i + 2, :]).then_inc(wo_loaded(hc, i)[0], 16)

            def load_mix(n):
                if n % HT >= 2:
                    sp.wait_ge(mix_ready, n - 1)
                sp.dma_start(mix_buf(n)[:, :, :], mix_v[:, :, n * P:(n + 1) * P]).then_inc(mix_ld[n % 2], 16)

            for i in range(NT):
                if i >= 2:
                    sp.wait_ge(split_lo, 2 * (i - 1))
                sp.dma_start(qk_in[i % 2][:, :, :],
                             qkv_v[:, i, 0:2 * GW].rearrange("p (a d) -> p a d", a=2)).then_inc(qk_ld[i % 2], 16)
                if i == 1:
                    load_w_out(0, 0)
                    sp.wait_ge(ln_st, 32)
                    sp.dma_start(v_sb[:, :, :], qkv_v[:, :, 2 * GW:3 * GW]).then_inc(v_ld, 16)
            def store_out(hc, t):
                sp.wait_ge(ff2_read, (hc + 1) * FG * 2 * HT - 2 * (HT - 1 - t))
                sp.dma_start(out_v[:, hc * HT + t, :], x_new[:, t, :]).then_inc(out_st, 16)

            def store_att(j):
                sp.wait_ge(x_read, FILL_NO["att", j, 1] + 1)
                sp.dma_start(mix_v[:, 0:2, j * BLK:(j + 1) * BLK], att_t[j % 2][:, :, :]).then_inc(attt_st[j % 2], 16)

            for j in range(NT // 4 - 1):
                store_att(j)

            for s in range(2):
                sp.wait_ge(attt_st[s], 16)
            sp.wait_ge(sc_mm, SC_NO[UNITS])
            for n in (0, 1):
                load_mix(n)
            store_att(NT // 4 - 1)
            sp.wait_ge(pv_mm, AT_NO[UNITS])
            load_w_out(0, 1)
            load_w_out(0, 2)
            load_w_out(0, 3)
            for hc in range(2):
                w0 = 2 * NI + hc * C_ITEMS
                if hc:
                    for s in range(2):
                        sp.wait_ge(attt_st[s], 32)
                    load_w_out(1, 0)
                    load_w_out(1, 1)
                    sp.wait_ge(u_ready, 4 * FG)
                    for n in (0, 1):
                        load_mix(HT + n)
                    load_w_out(1, 2)
                    for t in range(HT):
                        store_out(0, t)
                    load_w_out(1, 3)
                    sp.wait_ge(ff2_mm, 16 * FG)
                    sp.wait_ge(out_st, 16 * HT)
                for t in range(HT):
                    n = hc * HT + t
                    if n:
                        sp.wait_ge(xr_ld, 16 * n)
                    if n == HT // 2:
                        sp.wait_ge(wlo_ready, w0 + 3)
                    sp.dma_start(x_new[:, t, :], x_v[:, n, :]).then_inc(xr_ld, 16)
                    if t + 2 < HT:
                        load_mix(n + 2)

                def load_ff(g):
                    w = 2 * g + (w0 + KC_OUT)
                    raw_free(w)
                    sp.dma_start(by_k8(w_raw[:, :]), w_ff1_v[:, :, bass.ds(g * GW, GW)]).then_inc(w_ld, 16)
                    raw_free(w + 1)
                    sp.dma_start(by_k2(w_raw[:, :]), w_ff2_v[:, bass.ds(g * 2, 2), :]).then_inc(w_ld, 16)

                load_ff(0)
                load_ff(1)
                with sp.Fori(0, FG // 2 - 1) as it:
                    for q in range(2):
                        load_ff(it * 2 + (2 + q))
            for t in range(HT):
                store_out(1, t)
            sp.wait_ge(out_st, 16 * NT)

        @block.gpsimd
        def _(pool):
            links = [0]

            def link(ins):
                links[0] += 1
                ins.then_inc(pool_chain, 1)
                pool.wait_ge(pool_chain, links[0])

            link(pool.memset(pool_blk[:, :, :], 0.0))
            link(pool.memset(ident[:, :], 0.0))
            pool.affine_select(out=ident[:, :], in_=ident[:, :], compare_op=ALU.not_equal, fill=1.0,
                               base=0, pattern=[[-1, P]], channel_multiplier=1)
            link(pool.memset(h_tmp[:, 0, :], 0.0))
            pool.affine_select(out=h_tmp[:, 0, :], in_=h_tmp[:, 0, :], compare_op=ALU.is_ge, fill=NEG,
                               base=0, pattern=[[-1, P]], channel_multiplier=1)
            pool.memset(ones_mean[:, :], 1.0 / GW)
            pool.memset(eps_col, EPS).then_inc(const_ready, 1)

            def norm_gain(n):
                pool.wait_ge(qn_ready, n + 1)
                v = qkv_out[slot_of_qk(n)][:, :].rearrange("p (a m d) -> p a m d", a=2, d=QKD)
                if n == 0:
                    pool.wait_ge(bc_ld, 16 * BROADCASTS)
                pool.tensor_tensor(out=v[:, 0], in0=v[:, 0], op=ALU.mult,
                                   in1=gain_qk[:, 0:1, :].to_broadcast([P, MAPS, QKD]))
                pool.tensor_tensor(out=v[:, 1], in0=v[:, 1], op=ALU.mult,
                                   in1=gain_qk[:, 1:2, :].to_broadcast([P, MAPS, QKD])).then_inc(qk_ready, 1)

            def windows(n, cc):
                pool.wait_ge(ud_ready, n + 1)
                if n:
                    pool.wait_ge(pool_y, n)
                end = POOL_HALO + BLK
                u = ud[:, cc, :]
                link(pool.tensor_tensor(out=win_a[:, 1:end], in0=u[:, 1:end], in1=u[:, 0:end - 1], op=ALU.add))
                last = pool.tensor_tensor(out=win_b[:, 3:end], in0=win_a[:, 3:end], in1=win_a[:, 1:end - 2], op=ALU.add)
                if cc:
                    link(last)
                    link(pool.tensor_tensor(out=win_a[:, 7:end], in0=win_b[:, 7:end], in1=win_b[:, 3:end - 4], op=ALU.add))
                    last = pool.tensor_tensor(out=win_b[:, 15:end], in0=win_a[:, 15:end], in1=win_a[:, 7:end - 8], op=ALU.add)
                last.then_inc(win_ready, 1)

            def ln_out(h):
                for b in range(NB):
                    for cc in range(GC):
                        pool.wait_ge(lnsig_ready, chan_no(h, cc, b) + 1)
                        y = acc[:, cc, b * BLK:(b + 1) * BLK]
                        pool.tensor_tensor(out=y, in0=y, in1=ln_sig[h][:, :], op=ALU.mult).then_inc(lnout_ready, 1)

            for h in range(2):
                for t in range(HT):
                    norm_gain(h * HT + t)
                if h:
                    ln_out(0)
                for b in range(NB):
                    for cc in range(GC):
                        windows(chan_no(h, cc, b), cc)
            ln_out(1)

            def split_tail(n, a):
                pool.wait_ge(split_hi, 2 * n + a + 1)
                hi, lo = heads_tails(a)
                src = qk_in[n % 2][:, a, :].rearrange("p (m o d) -> p m o d", o=1, d=QKD).to_broadcast([P, MAPS, 2, QKD])
                pool.tensor_tensor(out=lo, in0=src, in1=f32(hi), op=ALU.subtract).then_inc(split_lo, 1)

            split_tail(0, 0)
            split_tail(0, 1)
            for u in range(STEPS):
                for n, a in splits_at(u):
                    split_tail(n, a)
                j = (u - 19) // 16
                if j >= 0 and u == 16 * j + 19:
                    pool.wait_ge(o_read, 16 * (j + 1))
                    y = att[:, 4 * j:4 * j + 4, :]
                    pool.tensor_tensor(out=att_sq[:, :, :], in0=y, in1=y, op=ALU.mult).then_inc(asq_ready, 1)

        @block.scalar
        def _(act):
            A = nc.scalar.activation

            def w_head(w, s, ready, before, raw=w_raw):
                act.wait_ge(*ready)
                if before is not None:
                    act.wait_ge(*before)
                A(w_hi[s][:, :], raw[:, :], ACT.Copy).then_inc(whi_ready, 1)

            def w_in_head(w):
                w_head(w, w % 3, (w_ld, 16 * (w + 1)), used(w - 3) if w >= 3 else None)

            def rms_root(n):
                act.wait_ge(ms_ready, n + 1)
                A(stat[:, 4 * (n % 2) + 3:4 * (n % 2) + 4], stat[:, 4 * (n % 2) + 2:4 * (n % 2) + 3],
                  ACT.Sqrt, bias=eps_col).then_inc(rms_ready, 1)

            def modulate(n, tmp, gain, shift):
                act.wait_ge(xt_ready, n + 1)
                if n:
                    act.wait_ge(h_ready, n)
                for k in range(DC):
                    last = A(tmp[:, k, :], ps_t[:, k, :], ACT.Identity, scale=gain[:, k:k + 1], bias=shift[:, k:k + 1])
                last.then_inc(hmod_ready, 1)

            def h_head(n, tmp):
                act.wait_ge(hmod_ready, n + 1)
                t = n % HT
                A(h_hi[:, :, t * P:(t + 1) * P], tmp[:, :, :], ACT.Copy).then_inc(hhi_ready, 1)

            act.wait_ge(const_ready, 1)
            A(ident_r[:, :], ident[:, :], ACT.Copy)
            A(mask_r[:, :], h_tmp[:, 0, :], ACT.Copy).then_inc(act_chain, 1)
            act.wait_ge(tab_t, 1)
            A(col1[:, :], psum[:, 0, 0:R_END1], ACT.Copy).then_inc(tab_col, 1)
            A(col2[:, :], psum[:, 1, 0:R_END2], ACT.Copy).then_inc(tab_col, 1)
            act.wait_ge(tab_col, 2)
            A(silu_c[:, :], col1[:, R_C:R_B], ACT.Sigmoid).then_inc(sigc_ready, 1)
            act.wait_ge(lam_sums, 1)
            A(small[:, 6:8], small[:, 4:6], ACT.Exp).then_inc(lam_exp, 1)
            act.wait_ge(act_chain, 1)
            rms_root(0)
            rms_root(1)
            w_in_head(0)
            w_in_head(1)
            act.wait_ge(mod1_ready, 1)
            modulate(0, h_tmp, gain1, shift1)
            h_head(0, h_tmp)

            def qk_square(n):
                o = OUT_NO["qk", n // HT, n % HT, 0]
                act.wait_ge(proj_ready, o + 1)
                if n:
                    act.wait_ge(qss_ready, n)
                A(qk_sq[:, :], bank(o), ACT.Square).then_inc(qsq_ready, 1)
                act.wait_ge(qss_ready, n + 1)
                if n:
                    act.wait_ge(qn_ready, n)
                A(small[:, 48:64], small[:, 32:48], ACT.Sqrt, bias=eps_col, scale=1.0 / QKD).then_inc(qrms_ready, 1)

            def layer_norm(h, b):
                m, blk = h * NB + b, slice(b * BLK, (b + 1) * BLK)
                act.wait_ge(lnd_ready, m + 1)
                A(ln_sq[h][:, :, :], acc[:, :, blk], ACT.Square).then_inc(lnsq_ready, 1)
                o = OUT_NO["ln", h, b, 1]
                act.wait_ge(proj_ready, o + 1)
                A(ln_rs[h][:, :], bank(o), ACT.Sqrt, bias=eps_col).then_inc(lnsd_ready, 1)
                act.wait_ge(lnz_ready, m + 1)
                for cc in range(GC):
                    y, n = acc[:, cc, blk], GC * m + cc
                    A(y, y, ACT.Identity, scale=col1[:, R_LNG + cc:R_LNG + cc + 1],
                      bias=col1[:, R_LNB + cc:R_LNB + cc + 1]).then_inc(lny_ready, 1)
                    act.wait_ge(lny_ready, n + 1)
                    if n:
                        act.wait_ge(lnout_ready, n)
                    A(ln_sig[h][:, :], y, ACT.Sigmoid).then_inc(lnsig_ready, 1)

            def each_block(kind, h, evacuate):
                for b in range(NB):
                    for cc in range(GC):
                        o = OUT_NO[kind, h, cc, b]
                        act.wait_ge(proj_ready, o + 1)
                        evacuate(o, cc, b, chan_no(h, cc, b))

            def to_ud(o, cc, b, n):
                if n >= GC:
                    act.wait_ge(halo_saved, n - GC + 1)
                A(ud[:, cc, POOL_HALO:], bank(o), ACT.Copy).then_inc(ud_ready, 1)

            def to_gated(func):
                def evacuate(o, cc, b, n):
                    A(gated[:, cc, b * BLK:(b + 1) * BLK], bank(o), func).then_inc(gated_ready, 1)
                return evacuate

            def to_pool_stage(o, cc, b, n):
                if n >= 2:
                    act.wait_ge(stage_st[n % 2], 16 * stores_of_stage(n, False))
                A(stage[n % 2][:, :], bank(o), ACT.Copy, scale=col1[:, R_PSC + cc:R_PSC + cc + 1]).then_inc(poolout_ready, 1)

            def copy_v(h, t):
                o, s = OUT_NO["v", h, t, 0], slot_of_v(h, t)
                act.wait_ge(proj_ready, o + 1)
                if stores_before_v(h, t):
                    act.wait_ge(qkv_st[s], 16 * stores_before_v(h, t))
                A(qkv_out[s][:, :], bank(o), ACT.Copy).then_inc(v_ready, 1)

            for h in range(2):
                w0 = h * NI
                for t in range(HT):
                    n = h * HT + t
                    if t + 1 < HT:
                        modulate(n + 1, h_tmp, gain1, shift1)
                        h_head(n + 1, h_tmp)
                    if n + 2 < NT:
                        rms_root(n + 2)
                    if t:
                        qk_square(n - 1)
                    if t >= 2 and t % 2 == 0:
                        copy_v(h, t - 2)
                    if t == 0:
                        w_in_head(w0 + 2)
                w_in_head(w0 + 3)
                qk_square(h * HT + HT - 1)
                copy_v(h, HT - 2)
                w_in_head(w0 + 4)
                if h:
                    layer_norm(0, 0)
                w_in_head(w0 + 5)
                if h:
                    act.wait_ge(prod_ready, NB * GC * h)
                each_block("gate", h, to_gated(ACT.Sigmoid))
                w_in_head(w0 + 6)
                if h:
                    layer_norm(0, 1)
                w_in_head(w0 + 7)
                each_block("ud", h, to_ud)
                w_in_head(w0 + 8)
                act.wait_ge(conf_ready, NB * GC * (h + 1))
                each_block("cg", h, to_gated(ACT.Copy))
                each_block("pool", h, to_pool_stage)
                if h == 0:
                    w_in_head(NI)
                    w_in_head(NI + 1)
                    modulate(HT, h_tmp, gain1, shift1)
                    act.wait_ge(*used(NI - 1))
                    h_head(HT, h_tmp)
                else:
                    layer_norm(1, 0)
            layer_norm(1, 1)

            act.wait_ge(proj_ready, len(OUTS))

            def split_head(n, a):
                hi, lo = heads_tails(a)
                if a == 0:
                    act.wait_ge(qk_ld[n % 2], 16 * (n // 2 + 1))
                if n:
                    act.wait_ge(x_fill, FILL_NO["stack", n - 1, 2 * a + 1] + 1)
                src = qk_in[n % 2][:, a, :].rearrange("p (m o d) -> p m o d", o=1, d=QKD).to_broadcast([P, MAPS, 2, QKD])
                A(hi, src, ACT.Copy).then_inc(split_hi, 1)

            def read_fill(x):
                kind, i, f = FILLS[x]
                act.wait_ge(x_fill, x + 1)
                if kind == "stack":
                    m0, src = 4 * (f % 2), psum[:, 7, :].rearrange("p (m t) -> p m t", m=4)
                    dst = q_stack[i % 2][:, m0:m0 + 4, :] if f < 2 else k_stack[:, m0:m0 + 4, i * P:(i + 1) * P]
                else:
                    if i >= 2 and f == 0:
                        act.wait_ge(attt_st[i % 2], 16)
                    src, dst = psum[:, 7, :], att_t[i % 2][:, f, :]
                A(dst, src, ACT.Copy).then_inc(x_read, 1)

            def exps(u):
                i, s = u // HEADS, u % 3
                n = (i + 1) * P
                act.wait_ge(max_ready, u + 1)
                for m in range(2):
                    A(scores[s][:, m, 0:n], scores[s][:, m, 0:n], ACT.Exp, scale=SCALE, bias=bst[:, s, 10 + m:11 + m],
                      accum_out=bst[:, s, 12 + m:13 + m]).then_inc(exp_done, 1)

            def read_at(u, part):
                if not 0 <= u < UNITS:
                    return
                for g, (k0, nk) in list(enumerate(at_groups(u)))[part]:
                    gn = AT_NO[u] + g
                    act.wait_ge(at_mm, gn + 1)
                    if gn >= 2:
                        act.wait_ge(pv_mm, gn - 1)
                    A(a_t[gn % 2][:, 0:nk * P], psum[:, 4 + gn % 2, 0:nk * P], ACT.Copy).then_inc(at_ready, 1)

            def wo_head(hc, i, before):
                w_head(2 * NI + hc * C_ITEMS + i, wo_slot(hc, i), wo_loaded(hc, i), before, wo_raw(hc, i))

            def mix_head(n):
                act.wait_ge(mix_ld[n % 2], 16 * (n // 2 + 1))
                t = n % HT
                A(h_hi[:, :, t * P:(t + 1) * P], mix_buf(n)[:, :, :], ACT.Copy).then_inc(mixhi_ready, 1)

            split_head(0, 0)
            split_head(0, 1)
            for x in range(4):
                read_fill(x)
            for u in range(STEPS):
                for n, a in splits_at(u):
                    split_head(n, a)
                for x in fills_at(u):
                    read_fill(x)
                read_at(u - 2, slice(0, 2))
                if 0 <= u - 1 < UNITS:
                    exps(u - 1)
                read_at(u - 2, slice(2, 4))
                j = (u - 19) // 16
                if j >= 0 and u == 16 * j + 19:
                    act.wait_ge(ams_ready, j + 1)
                    A(ams[:, 16:32], ams[:, 0:16], ACT.Sqrt, bias=eps_col, scale=1.0 / VD).then_inc(arms_ready, 1)
                if u == UNITS + 1:
                    act.wait_ge(sc_mm, SC_NO[UNITS])
                    mix_head(0)
                    mix_head(1)
                if u == UNITS + 4:
                    wo_head(0, 0, (at_mm, AT_NO[UNITS]))

            for hc in range(2):
                w0 = 2 * NI + hc * C_ITEMS
                n0 = hc * HT
                if hc == 0:
                    for i in (1, 2):
                        wo_head(0, i, (at_mm, AT_NO[UNITS]))
                    for q in range(2):
                        act.wait_ge(attt_st[q], 32)
                    wo_head(0, 3, None)
                else:
                    wo_head(1, 2, (ff1_mm, 4 * FG))
                    act.wait_ge(ff1_mm, 4 * FG)
                    mix_head(HT)
                    mix_head(HT + 1)
                    wo_head(1, 3, (ff2_mm, 16 * FG))
                for t in range(HT):
                    n = NT + n0 + t
                    if 2 <= t + 1 < HT:
                        mix_head(n0 + t + 1)
                    rms_root(n)
                    if t:
                        modulate(n - 1, h_tmp2, gain2, shift2)
                        h_head(n - 1, h_tmp2)

                all_w_out = (wo_mm, 2 * (n0 + HT))

                def ff1_head(g, q, first=False):
                    w = 2 * g + (w0 + KC_OUT)
                    w_head(w, 2 * q, loaded(w),
                           all_w_out if first else (ff1_mm, 4 * g + (4 * FG * hc - 4)))

                def ff2_head(g, q, first=False):
                    w = 2 * g + (w0 + KC_OUT + 1)
                    w_head(w, 2 * q + 1, (w_folded, g + (hc * FG + 1)),
                           all_w_out if first else (ff2_mm, 16 * g + (16 * FG * hc - 16)))

                ff1_head(0, 0, True)
                modulate(NT + n0 + HT - 1, h_tmp2, gain2, shift2)
                h_head(NT + n0 + HT - 1, h_tmp2)
                ff2_head(0, 0, True)
                act.wait_ge(h_ready, NT + n0 + HT)

                def group(g, q, first=False, ahead=None):
                    if ahead is None:
                        ahead = (lambda: ff1_head(g + 1, 1 - q, first), lambda: ff2_head(g + 1, 1 - q, first))

                    def relu(f):
                        F = 4 * g + (4 * FG * hc + f)
                        act.wait_ge(ff1_mm, F + 1)
                        if not first:
                            act.wait_ge(u_ready, F - 3)
                        A(relu_t[f][:, :], psum[:, 2 + f % 2, :], ACT.Relu).then_inc(relu_ready, 1)

                    def u_head(f):
                        F = 4 * g + (4 * FG * hc + f)
                        b, j = f // 2, f % 2
                        act.wait_ge(sq_ready, F + 1)
                        if not first:
                            act.wait_ge(ff2_mm, 16 * g + (16 * FG * hc - 16 + 8 * b + 8))
                        A(u_hi[:, j, b * BLK:(b + 1) * BLK], relu_t[f][:, :], ACT.Copy).then_inc(uhi_ready, 1)

                    relu(0)
                    ahead[0]()
                    u_head(0)
                    relu(1)
                    u_head(1)
                    relu(2)
                    u_head(2)
                    ahead[1]()
                    relu(3)
                    u_head(3)

                group(0, 0, first=True)
                group(1, 1)
                with act.Fori(1, FG // 2 - 1) as it:
                    for q in range(2):
                        group(it * 2 + q, q)
                group(FG - 2, 0)
                before = (ff1_mm, 4 * FG - 4), (ff2_mm, 16 * FG - 16)
                group(FG - 1, 1, ahead=(lambda: hc or wo_head(1, 0, before[0]), lambda: hc or wo_head(1, 1, before[1])))

        @block.vector
        def _(dve):
            V = nc.vector
            links = [0]

            def mark(ins):
                links[0] += 1
                ins.then_inc(dve_chain, 1)
                return links[0]

            def link(ins):
                dve.wait_ge(dve_chain, mark(ins))

            def mean_square(n, src):
                s = 4 * (n % 2)
                V.bn_stats(bn[:, 0, :], src[:, 0:BLK])
                link(V.bn_stats(bn[:, 1, :], src[:, BLK:D]))
                link(V.bn_aggr(stat[:, s:s + 2], bn[:, :, :].rearrange("p a b -> p (a b)")))
                V.scalar_tensor_tensor(out=stat[:, s + 2:s + 3], in0=stat[:, s:s + 1], scalar=stat[:, s:s + 1],
                                       in1=stat[:, s + 1:s + 2], op0=ALU.mult, op1=ALU.add).then_inc(ms_ready, 1)

            def normalise(n, src, dst):
                s = 4 * (n % 2)
                dve.wait_ge(rms_ready, n + 1)
                link(V.reciprocal(stat[:, 8:9], stat[:, s + 3:s + 4]))
                V.tensor_scalar(dst, src, stat[:, 8:9], None, ALU.mult).then_inc(xn_ready, 1)

            def h_tail(n, tmp):
                t = n % HT
                dve.wait_ge(hhi_ready, n + 1)
                tok = slice(t * P, (t + 1) * P)
                V.tensor_tensor(out=h_lo[:, :, tok], in0=tmp[:, :, :], in1=f32(h_hi[:, :, tok]),
                                op=ALU.subtract).then_inc(h_ready, 1)

            def w_tail(w, s, raw=w_raw):
                dve.wait_ge(whi_ready, w + 1)
                V.tensor_tensor(out=w_lo[s][:, :], in0=raw[:, :], in1=f32(w_hi[s][:, :]),
                                op=ALU.subtract).then_inc(wlo_ready, 1)

            def w_in_tail(w):
                w_tail(w, w % 3)

            def w_fold(w):
                dve.wait_ge(*loaded(w))
                V.tensor_tensor(out=by_k2(w_raw[:, :]), in0=by_k2(w_raw[:, :]), op=ALU.mult,
                                in1=gate_row[:, 1:2, :].to_broadcast([P, 2, D])).then_inc(w_folded, 1)

            def columns(rows, n, tmp):
                blocks = tmp.rearrange("p (m c) -> p m c", c=P)
                link(V.tensor_tensor(out=blocks, in0=rows.rearrange("p a n -> p (a n)").rearrange("p (m c) -> p m c", c=P),
                                     in1=ident[:, :].rearrange("p (o c) -> p o c", o=1).to_broadcast([P, n, P]), op=ALU.mult))
                link(V.tensor_reduce(out=diag_sum[:, 0:n], in_=blocks, axis=AX.X, op=ALU.add))

            groups = [(cc, slice(64 * s, 64 * s + 64), 2 << (2 * cc + s)) for cc in range(GC) for s in range(2)]
            for cc, part, win in groups:
                V.memset(inv_win[part, cc:cc + 1], 1.0 / win)
                ins = V.memset(inv_first[part, cc, :], 1.0 / win)
            link(ins)
            for cc, part, win in groups:
                for t in range(win - 1):
                    V.memset(inv_first[part, cc, t:t + 1], 1.0 / (t + 1))

            dve.wait_ge(sigc_ready, 1)
            V.tensor_tensor(out=silu_c[:, :], in0=silu_c[:, :], in1=col1[:, R_C:R_B], op=ALU.mult).then_inc(siluc_ready, 1)
            dve.wait_ge(bc_ld, 16 * BROADCASTS)
            pairs = small[:, 32:96].rearrange("p (a d) -> p a d", d=QKD)
            link(V.tensor_tensor(out=pairs, in0=lam_in[:, 0:4:2, :], in1=lam_in[:, 1:4:2, :], op=ALU.mult))
            V.tensor_reduce(out=small[:, 4:6], in_=pairs, axis=AX.X, op=ALU.add).then_inc(lam_sums, 1)
            dve.wait_ge(lam_exp, 1)
            V.scalar_tensor_tensor(out=lam_neg, in0=small[:, 7:8], scalar=-LAM_INIT, in1=small[:, 6:7],
                                   op0=ALU.add, op1=ALU.subtract)
            V.tensor_scalar(gain_sub[:, :], gain_sub[:, :], 1.0 - LAM_INIT, None, ALU.mult)
            for n in range(2):
                dve.wait_ge(x_ld[n], 16)
                mean_square(n, x_in[n])
                normalise(n, x_in[n][:, :], x_in[n][:, :])
            w_in_tail(0)
            w_in_tail(1)
            dve.wait_ge(mod1_mm, 1)
            columns(psum[:, 2:6, :], 2 * DC, ada_first[0][:, :])
            V.tensor_tensor(out=shift1[:, :], in0=diag_sum[:, 0:DC], in1=col1[:, R_B:R_B + 8], op=ALU.add)
            link(V.tensor_tensor(out=gain1[:, :], in0=diag_sum[:, DC:2 * DC], in1=col1[:, R_B + 8:R_B + 16], op=ALU.add))
            V.scalar_tensor_tensor(out=gain1[:, :], in0=gain1[:, :], scalar=1.0, in1=col1[:, R_N1:R_N2],
                                   op0=ALU.add, op1=ALU.mult).then_inc(mod1_ready, 1)
            V.memset(conf[:, :, 0:TAPS - 1], 0.0)
            V.memset(ud[:, :, 0:POOL_HALO], 0.0)
            link(V.memset(halo2[:, :, :], 0.0))
            h_tail(0, h_tmp)

            def qk_sums(n):
                dve.wait_ge(qsq_ready, n + 1)
                V.tensor_reduce(out=small[:, 32:48], in_=qk_sq[:, :].rearrange("p (a d) -> p a d", d=QKD),
                                axis=AX.X, op=ALU.add).then_inc(qss_ready, 1)

            def qk_normalise(n):
                s = slot_of_qk(n)
                dve.wait_ge(qrms_ready, n + 1)
                link(V.reciprocal(small[:, 64:80], small[:, 48:64]))
                if stores_before_qk(n):
                    dve.wait_ge(qkv_st[s], 16 * stores_before_qk(n))
                r = small[:, 64:80].rearrange("p (a o) -> p a o", o=1).to_broadcast([P, 2 * MAPS, QKD])
                V.tensor_tensor(out=qkv_out[s][:, :].rearrange("p (a d) -> p a d", d=QKD),
                                in0=bank(OUT_NO["qk", n // HT, n % HT, 0]).rearrange("p (a d) -> p a d", d=QKD),
                                in1=r, op=ALU.mult).then_inc(qn_ready, 1)

            def conv_taps(h):
                for b in range(NB):
                    marks = []
                    dve.wait_ge(conf_ready, NB * GC * h + GC * (b + 1))
                    for j in range(TAPS):
                        for cc in range(GC):
                            w = col2[:, R_DWW + GC * j + cc:R_DWW + GC * j + cc + 1]
                            src, dst = conf[:, cc, b * BLK + j:b * BLK + j + BLK], acc[:, cc, b * BLK:(b + 1) * BLK]
                            if j == 0:
                                if h and b == 0 and cc == 0:
                                    dve.wait_ge(ln_st, 16)
                                ins = V.tensor_scalar(dst, src, w, col1[:, R_DWB + cc:R_DWB + cc + 1], ALU.mult, ALU.add)
                            else:
                                dve.wait_ge(dve_chain, marks[-GC])
                                ins = V.scalar_tensor_tensor(out=dst, in0=src, scalar=w, in1=dst, op0=ALU.mult, op1=ALU.add)
                            if j == TAPS - 1 and cc == GC - 1:
                                ins.then_inc(conv_ready, 1)
                            else:
                                marks.append(mark(ins))
                            yield
                dve.wait_ge(conv_ready, NB * (h + 1))
                link(V.tensor_copy(conf[:, :, 0:TAPS - 1], conf[:, :, HALF:HALF + TAPS - 1]))

            def pump(taps, n):
                for _ in range(n):
                    next(taps, None)

            def layer_norm(h, b):
                blk = slice(b * BLK, (b + 1) * BLK)
                o = OUT_NO["ln", h, b, 0]
                dve.wait_ge(proj_ready, o + 1)
                V.tensor_tensor(out=acc[:, 0, blk], in0=acc[:, 0, blk], in1=bank(o), op=ALU.subtract)
                V.tensor_tensor(out=acc[:, 1, blk], in0=acc[:, 1, blk], in1=bank(o), op=ALU.subtract).then_inc(lnd_ready, 1)
                dve.wait_ge(lnsd_ready, h * NB + b + 1)
                link(V.reciprocal(ln_rs[h][:, :], ln_rs[h][:, :]))
                V.tensor_tensor(out=acc[:, 0, blk], in0=acc[:, 0, blk], in1=ln_rs[h][:, :], op=ALU.mult)
                V.tensor_tensor(out=acc[:, 1, blk], in0=acc[:, 1, blk], in1=ln_rs[h][:, :], op=ALU.mult).then_inc(lnz_ready, 1)

            def pooled(h, cc, b):
                n = chan_no(h, cc, b)
                dve.wait_ge(win_ready, n + 1)
                y = pool_in[:, cc, b * BLK:(b + 1) * BLK]
                first = POOL_HALO if h == b == 0 else 0
                for part, win in ((slice(0, 64), win_a), (slice(64, P), win_b)):
                    if first:
                        link(V.tensor_tensor(out=win[part, POOL_HALO:2 * POOL_HALO], in0=win[part, POOL_HALO:2 * POOL_HALO],
                                             in1=inv_first[part, cc, :], op=ALU.mult))
                        V.tensor_tensor(out=y[part, 0:first], in0=win[part, POOL_HALO:2 * POOL_HALO],
                                        in1=ud[part, cc, POOL_HALO:2 * POOL_HALO], op=ALU.subtract)
                    last = V.scalar_tensor_tensor(out=y[part, first:BLK], in0=win[part, POOL_HALO + first:],
                                                  scalar=inv_win[part, cc:cc + 1], in1=ud[part, cc, POOL_HALO + first:],
                                                  op0=ALU.mult, op1=ALU.subtract)
                last.then_inc(pool_y, 1)
                dve.wait_ge(pool_y, n + 1)
                V.tensor_copy(ud[:, cc, 0:POOL_HALO], ud[:, cc, BLK:BLK + POOL_HALO]).then_inc(halo_saved, 1)

            def in_prod(h, cc, b):
                o = OUT_NO["xc", h, cc, b]
                dve.wait_ge(proj_ready, o + 1)
                dve.wait_ge(gated_ready, (2 * h + 1) * NB * GC + GC * b + cc + 1)
                V.tensor_tensor(out=prod[:, cc, STAPS - 1 + b * BLK:STAPS - 1 + (b + 1) * BLK], in0=bank(o),
                                in1=gated[:, cc, b * BLK:(b + 1) * BLK], op=ALU.mult).then_inc(prod_ready, 1)

            def short(h, cc, b):
                n = chan_no(h, cc, b)
                y = stage[n % 2][:, :]
                dve.wait_ge(stage_st[n % 2], 16 * stores_of_stage(n, True))
                for j in range(STAPS):
                    w = col2[:, R_SW + GC * j + cc:R_SW + GC * j + cc + 1]
                    src = prod[:, cc, b * BLK + j:b * BLK + j + BLK]
                    if j == 0:
                        link(V.tensor_scalar(y, src, w, None, ALU.mult))
                    else:
                        link(V.scalar_tensor_tensor(out=y, in0=src, scalar=w, in1=y, op0=ALU.mult, op1=ALU.add))
                o = OUT_NO["bg", h, cc, b]
                dve.wait_ge(proj_ready, o + 1)
                V.tensor_tensor(out=y, in0=y, in1=bank(o), op=ALU.mult).then_inc(short_ready, 1)

            def read_modulation(h):
                dve.wait_ge(ada_used, DC * (h + 1))
                V.tensor_tensor(out=gate_row[:, h, :], in0=gate_row[:, h, :],
                                in1=psum[:, 5:7, :].rearrange("p a n -> p (a n)"), op=ALU.add)
                columns(psum[:, 0:2, :], DC, h_tmp[:, :, :].rearrange("p k t -> p (k t)"))
                r = R_B + (3 + h) * DC
                if h == 0:
                    V.tensor_tensor(out=shift2[:, :], in0=diag_sum[:, 0:DC], in1=col1[:, r:r + DC], op=ALU.add).then_inc(mod2_ready, 1)
                else:
                    link(V.tensor_tensor(out=gain2[:, :], in0=diag_sum[:, 0:DC], in1=col1[:, r:r + DC], op=ALU.add))
                    V.scalar_tensor_tensor(out=gain2[:, :], in0=gain2[:, :], scalar=1.0, in1=col1[:, R_N2:R_DWB],
                                           op0=ALU.add, op1=ALU.mult).then_inc(mod2_ready, 1)

            taps = iter(())
            blocks = [(cc, b) for b in range(NB) for cc in range(GC)]
            for h in range(2):
                w0 = h * NI
                for t in range(HT):
                    n = h * HT + t
                    if n + 2 < NT:
                        dve.wait_ge(x_ld[n % 2], 16 * ((n + 2) // 2 + 1))
                        mean_square(n + 2, x_in[n % 2])
                    if t + 1 < HT:
                        h_tail(n + 1, h_tmp)
                    if n + 2 < NT:
                        normalise(n + 2, x_in[n % 2][:, :], x_in[n % 2][:, :])
                    if t:
                        qk_sums(n - 1)
                        qk_normalise(n - 1)
                    if t == 0:
                        w_in_tail(w0 + 2)
                    pump(taps, 2)
                w_in_tail(w0 + 3)
                qk_sums(h * HT + HT - 1)
                qk_normalise(h * HT + HT - 1)
                w_in_tail(w0 + 4)
                pump(taps, 9 * TAPS)
                if h:
                    layer_norm(0, 0)
                w_in_tail(w0 + 5)
                w_in_tail(w0 + 6)
                if h:
                    layer_norm(0, 1)
                for cc, b in blocks:
                    blk = slice(b * BLK, (b + 1) * BLK)
                    o = OUT_NO["val", h, cc, b]
                    dve.wait_ge(proj_ready, o + 1)
                    dve.wait_ge(gated_ready, 2 * h * NB * GC + GC * b + cc + 1)
                    V.tensor_tensor(out=conf[:, cc, TAPS - 1 + b * BLK:TAPS - 1 + (b + 1) * BLK], in0=bank(o),
                                    in1=gated[:, cc, blk], op=ALU.mult).then_inc(conf_ready, 1)
                    if (cc, b) == (GC - 1, 0):
                        taps = conv_taps(h)
                    if b or cc == GC - 1:
                        pump(taps, 6)
                w_in_tail(w0 + 7)
                pump(taps, 16)
                for cc, b in blocks:
                    if (cc, b) == (0, 1):
                        w_in_tail(w0 + 8)
                    pooled(h, cc, b)
                    pump(taps, 7)
                dve.wait_ge(proj_ready, OUT_NO["pool", h, GC - 1, NB - 1] + 1)
                link(V.tensor_copy(prod[:, :, 0:STAPS - 1], halo2[:, :, :]))
                for cc, b in blocks:
                    in_prod(h, cc, b)
                    if h == 0 and cc == b == 0:
                        w_in_tail(NI)
                    pump(taps, 7)
                dve.wait_ge(prod_ready, NB * GC * (h + 1))
                read_modulation(h)
                if h:
                    layer_norm(1, 0)
                for cc, b in blocks:
                    short(h, cc, b)
                    if h == 0 and cc == b == 0:
                        w_in_tail(NI + 1)
                    if h or (cc, b) != blocks[-1]:
                        pump(taps, 5)
                if h == 0:
                    h_tail(HT, h_tmp)
                    link(V.tensor_copy(halo2[:, :, :], prod[:, :, HALF:HALF + STAPS - 1]))
            pump(taps, 9 * TAPS)
            layer_norm(1, 1)

            dve.wait_ge(proj_ready, len(OUTS))
            dve.wait_ge(ln_st, 32)

            def read_scores(u):
                i, s = u // HEADS, u % 3
                nch = len(sc_chunks(i))
                if u >= 3:
                    dve.wait_ge(at_mm, AT_NO[u - 2])
                for m in range(2):
                    for ch, (c0, n) in enumerate(sc_chunks(i)):
                        r = SC_NO[u] + m * nch + ch
                        dve.wait_ge(sc_mm, r + 1)
                        V.tensor_scalar(scores[s][:, m, c0:c0 + n], psum[:, r % 4, 0:n], 1.0, None, ALU.mult, ALU.max,
                                        accum_out=bst[:, s, 4 * m + ch:4 * m + ch + 1]).then_inc(sc_read, 1)
                dve.wait_ge(sc_read, SC_NO[u + 1])
                link(V.tensor_reduce(out=bst[:, s, 8:10], axis=AX.X, op=ALU.max,
                                     in_=bst[:, s, 0:8].rearrange("p (m c) -> p m c", m=2)[:, :, 0:nch]))
                V.tensor_scalar(bst[:, s, 10:12], bst[:, s, 8:10], -SCALE, None, ALU.mult).then_inc(max_ready, 1)

            def combine(u):
                i, s = u // HEADS, u % 3
                n = (i + 1) * P
                dve.wait_ge(exp_done, 2 * (u + 1))
                link(V.reciprocal(bst[:, s, 14:16], bst[:, s, 12:14]))
                link(V.scalar_tensor_tensor(out=bst[:, s, 16:17], in0=bst[:, s, 12:13], scalar=bst[:, s, 15:16],
                                            in1=lam_neg, op0=ALU.mult, op1=ALU.mult))
                V.scalar_tensor_tensor(out=scores[s][:, 0, 0:n], in0=scores[s][:, 1, 0:n], scalar=bst[:, s, 16:17],
                                       in1=scores[s][:, 0, 0:n], op0=ALU.mult, op1=ALU.add).then_inc(a_ready, 1)
                link(V.tensor_copy(inv_s[:, u % 4:u % 4 + 1], bst[:, s, 14:15]))

            def read_o(u):
                i, hd = u // HEADS, u % HEADS
                dve.wait_ge(pv_mm, AT_NO[u + 1])
                V.tensor_scalar(att[:, i, hd * VD:(hd + 1) * VD], psum[:, 6, 0:VD],
                                inv_s[:, u % 4:u % 4 + 1], None, ALU.mult).then_inc(o_read, 1)

            def mix_tail(n):
                tok = slice(n % HT * P, (n % HT + 1) * P)
                dve.wait_ge(mixhi_ready, n + 1)
                V.tensor_tensor(out=h_lo[:, :, tok], in0=mix_buf(n)[:, :, :], in1=f32(h_hi[:, :, tok]),
                                op=ALU.subtract).then_inc(mix_ready, 1)

            def wo_tail(hc, i):
                w_tail(2 * NI + hc * C_ITEMS + i, wo_slot(hc, i), wo_raw(hc, i))

            for u in range(STEPS):
                if 0 <= u - 3 < UNITS:
                    read_o(u - 3)
                if u < UNITS:
                    read_scores(u)
                if 0 <= u - 1 < UNITS:
                    combine(u - 1)
                j = (u - 19) // 16
                if j >= 0 and u == 16 * j + 19:
                    dve.wait_ge(asq_ready, j + 1)
                    V.tensor_reduce(out=ams[:, 0:16], in_=att_sq[:, :, :].rearrange("p i (a d) -> p (i a) d", d=VD),
                                    axis=AX.X, op=ALU.add).then_inc(ams_ready, 1)
                j = (u - 20) // 16
                if j >= 0 and u == 16 * j + 20:
                    y = att[:, 4 * j:4 * j + 4, :].rearrange("p i (a d) -> p (i a) d", d=VD)
                    dve.wait_ge(arms_ready, j + 1)
                    link(V.reciprocal(ams[:, 32:48], ams[:, 16:32]))
                    link(V.tensor_tensor(out=y, in0=y, op=ALU.mult,
                                         in1=ams[:, 32:48].rearrange("p (a o) -> p a o", o=1).to_broadcast([P, 16, VD])))
                    V.tensor_tensor(out=y, in0=y, op=ALU.mult,
                                    in1=gain_sub[:, :].rearrange("p (o d) -> p o d", o=1).to_broadcast([P, 16, VD])).then_inc(att_ready, 1)
                if u == UNITS + 1:
                    mix_tail(0)
                    mix_tail(1)
                if u == UNITS + 4:
                    wo_tail(0, 0)

            for hc in range(2):
                w0 = 2 * NI + hc * C_ITEMS
                n0 = hc * HT

                if hc == 0:
                    for i in (1, 2, 3):
                        wo_tail(0, i)
                for t in range(HT):
                    n = n0 + t
                    if 2 <= t + 1 < HT:
                        mix_tail(n + 1)
                    dve.wait_ge(xr_ld, 16 * (n + 1))
                    for cb in range(2):
                        o, col = 2 * n + cb, slice(cb * BLK, (cb + 1) * BLK)
                        y = x_new[:, t, col]
                        dve.wait_ge(wo_mm, o + 1)
                        V.tensor_tensor(out=wo_gated[:, :], in0=psum[:, 4 + o % 4, :], in1=gate_row[:, 0, col],
                                        op=ALU.mult).then_inc(wo_read, 1)
                        dve.wait_ge(wo_read, o + 1)
                        link(V.tensor_tensor(out=y, in0=y, in1=wo_gated[:, :], op=ALU.add))
                    mean_square(NT + n, x_new[:, t, :])
                    if t:
                        dve.wait_ge(xt_ready, NT + n)
                    normalise(NT + n, x_new[:, t, :], xn2[:, :])
                    if t:
                        h_tail(NT + n - 1, h_tmp2)

                def ff1_tail(g, q):
                    w_tail(2 * g + (w0 + KC_OUT), 2 * q)

                def ff2_fold(g):
                    w_fold(2 * g + (w0 + KC_OUT + 1))

                def ff2_tail(g, q):
                    w_tail(2 * g + (w0 + KC_OUT + 1), 2 * q + 1)

                ff1_tail(0, 0)
                h_tail(NT + n0 + HT - 1, h_tmp2)
                ff2_fold(0)
                ff2_tail(0, 0)

                def group(g, q, last=False):
                    def square(f):
                        dve.wait_ge(relu_ready, 4 * g + (4 * FG * hc + f + 1))
                        V.tensor_tensor(out=relu_t[f][:, :], in0=relu_t[f][:, :], in1=relu_t[f][:, :],
                                        op=ALU.mult).then_inc(sq_ready, 1)

                    def u_tail(f):
                        b, j = f // 2, f % 2
                        blk = slice(b * BLK, (b + 1) * BLK)
                        dve.wait_ge(uhi_ready, 4 * g + (4 * FG * hc + f + 1))
                        V.tensor_tensor(out=u_lo[:, j, blk], in0=relu_t[f][:, :], in1=f32(u_hi[:, j, blk]),
                                        op=ALU.subtract).then_inc(u_ready, 1)

                    def accumulate(q0):
                        for o in range(q0, q0 + 8):
                            t, cb = o // 2, o % 2
                            y = x_new[:, t, cb * BLK:(cb + 1) * BLK]
                            dve.wait_ge(ff2_mm, 16 * g + (16 * FG * hc + o + 1))
                            V.tensor_tensor(out=y, in0=y, in1=psum[:, 4 + o % 4, :], op=ALU.add).then_inc(ff2_read, 1)

                    square(0)
                    if not last:
                        ff1_tail(g + 1, 1 - q)
                    elif hc == 0:
                        wo_tail(1, 0)
                    u_tail(0)
                    square(1)
                    u_tail(1)
                    square(2)
                    if not last:
                        ff2_fold(g + 1)
                    u_tail(2)
                    square(3)
                    u_tail(3)
                    if last and hc == 0:
                        wo_tail(1, 1)
                    accumulate(0)
                    if not last:
                        ff2_tail(g + 1, 1 - q)
                    elif hc == 0:
                        wo_tail(1, 2)
                        mix_tail(HT)
                        mix_tail(HT + 1)
                    accumulate(8)
                    if last and hc == 0:
                        wo_tail(1, 3)

                with dve.Fori(0, FG // 2 - 1) as it:
                    for q in range(2):
                        group(it * 2 + q, q)
                group(FG - 2, 0)
                group(FG - 1, 1, last=True)

        @block.tensor
        def _(pe):
            M = nc.tensor.matmul

            def mm3(dst, terms):
                last = len(terms) - 1
                for n, (ah, al, bh, bl) in enumerate(terms):
                    M(dst, ah, bh, start=(n == 0), stop=False)
                    M(dst, ah, bl, start=False, stop=False)
                    ins = M(dst, al, bh, start=False, stop=(n == last))
                return ins

            def transposes(n, src):
                pe.wait_ge(xn_ready, n + 1)
                if n:
                    pe.wait_ge(hmod_ready, n)
                for k in range(DC):
                    ins = nc.tensor.transpose(ps_t[:, k, :], src[:, k * P:(k + 1) * P], ident[:, :])
                ins.then_inc(xt_ready, 1)

            pe.wait_ge(const_ready, 1)
            pe.wait_ge(tab_ld, 16 * 10)
            nc.tensor.transpose(psum[:, 0, 0:R_END1], table1[:, :], ident[0:R_END1, 0:R_END1])
            nc.tensor.transpose(psum[:, 1, 0:R_END2], table2[:, :], ident[0:R_END2, 0:R_END2]).then_inc(tab_t, 1)
            pe.wait_ge(siluc_ready, 1)
            for k in range(DC):
                pe.wait_ge(ada0_ld[k % 4], 16 * (k // 4 + 1))
                for m in range(4):
                    ins = M(psum[:, 2 + m, :], silu_c[:, k:k + 1].to_broadcast([P, P]), ada_first[k % 4][:, m * BLK:(m + 1) * BLK],
                            start=(k == 0), stop=(k == DC - 1), skip_group_check=True)
                ins.then_inc(ada0_used if k < DC - 1 else mod1_mm, 1)
            pe.wait_ge(tab_col, 2)
            transposes(0, x_in[0])

            def free(o):
                if o >= 4:
                    pe.wait_ge(*released(o - 4))

            def item_ready(w):
                pe.wait_ge(wlo_ready, w + 1)

            def w8(w, part):
                return by_k8(part[w % 3][:, :])

            def project_rows(h, t, w, dst):
                tok = slice(t * P, (t + 1) * P)
                wh, wl = w8(w, w_hi), w8(w, w_lo)
                return mm3(dst, [(h_hi[:, k, tok], h_lo[:, k, tok], wh[:, k, :], wl[:, k, :]) for k in range(DC)])

            def project_cols(kind, h, w, middle=lambda: None):
                item_ready(w)
                wh, wl = w8(w, w_hi), w8(w, w_lo)
                for b in range(NB):
                    if b:
                        middle()
                    for cc in range(GC):
                        o = OUT_NO[kind, h, cc, b]
                        free(o)
                        col, tok = slice(cc * P, (cc + 1) * P), slice(b * BLK, (b + 1) * BLK)
                        ins = mm3(bank(o), [(wh[:, k, col], wl[:, k, col], h_hi[:, k, tok], h_lo[:, k, tok])
                                            for k in range(DC)])
                        ins.then_inc(proj_ready, 1)

            def modulation(h, k):
                pe.wait_ge(ada_ld, 32 * (h * DC + k + 1))
                if h and k == 0:
                    pe.wait_ge(mod2_ready, 1)
                for n, to in enumerate((5, 6, 0, 1)):
                    ins = M(psum[:, to, :], silu_c[:, k:k + 1].to_broadcast([P, P]), ada[:, n * BLK:(n + 1) * BLK],
                            start=(k == 0), stop=(k == DC - 1), skip_group_check=True)
                ins.then_inc(ada_used, 1)

            def layer_norm(h, b):
                pe.wait_ge(conv_ready, h * NB + b + 1)
                for s in (0, 1):
                    o = OUT_NO["ln", h, b, s]
                    free(o)
                    if s:
                        pe.wait_ge(lnsq_ready, h * NB + b + 1)
                    for cc in range(GC):
                        src = ln_sq[h][:, cc, :] if s else acc[:, cc, b * BLK:(b + 1) * BLK]
                        ins = M(bank(o), ones_mean[:, :], src, start=(cc == 0), stop=(cc == GC - 1))
                    ins.then_inc(proj_ready, 1)

            def project_v(h, t):
                o = OUT_NO["v", h, t // 2 * 2, 0]
                if t % 2 == 0:
                    free(o)
                return project_rows(h, t, h * NI + 2, bank(o)[:, t % 2 * GW:(t % 2 + 1) * GW])

            def next_tile():
                pe.wait_ge(mod2_ready, 1)
                transposes(HT, x_in[HT % 2])

            for h in range(2):
                w0 = h * NI
                for t in range(HT):
                    n = h * HT + t
                    if t + 1 < HT:
                        transposes(n + 1, x_in[(n + 1) % 2])
                    o = OUT_NO["qk", h, t, 0]
                    pe.wait_ge(h_ready, n + 1)
                    free(o)
                    item_ready(w0)
                    project_rows(h, t, w0, bank(o)[:, 0:GW])
                    item_ready(w0 + 1)
                    project_rows(h, t, w0 + 1, bank(o)[:, GW:2 * GW]).then_inc(proj_ready, 1)
                    if t == 1:
                        item_ready(w0 + 2)
                        project_v(h, 0)
                    if t:
                        ins = project_v(h, t)
                        if t % 2:
                            ins.then_inc(proj_ready, 1)
                modulation(h, 0)
                if h:
                    layer_norm(0, 0)
                project_cols("gate", h, w0 + 3, lambda: modulation(h, 1))
                modulation(h, 2)
                if h:
                    layer_norm(0, 1)
                project_cols("val", h, w0 + 4)
                modulation(h, 3)
                project_cols("ud", h, w0 + 5)
                modulation(h, 4)
                project_cols("cg", h, w0 + 6)
                modulation(h, 5)
                for b in range(NB):
                    for cc in range(GC):
                        o = OUT_NO["pool", h, cc, b]
                        free(o)
                        pe.wait_ge(pool_y, chan_no(h, cc, b) + 1)
                        if h == 0 and b == 0 and cc == 0:
                            pe.wait_ge(bc_ld, 16 * BROADCASTS)
                        M(bank(o), pool_blk[:, cc, :], pool_in[:, cc, b * BLK:(b + 1) * BLK],
                          start=True, stop=True).then_inc(proj_ready, 1)
                project_cols("xc", h, w0 + 7, lambda: modulation(h, 6))
                modulation(h, 7)
                if h:
                    layer_norm(1, 0)
                project_cols("bg", h, w0 + 8, (lambda: None) if h else next_tile)
            layer_norm(1, 1)

            for o in range(len(OUTS) - 4, len(OUTS)):
                pe.wait_ge(*released(o))
            pe.wait_ge(mod2_ready, 2)
            pe.wait_ge(hmod_ready, NT)

            def fill(x):
                kind, i, f = FILLS[x]
                if x:
                    pe.wait_ge(x_read, x)
                if kind == "stack":
                    a = f // 2
                    pe.wait_ge(split_lo, 2 * i + a + 1)
                    src = f32((k_split if a else q_split)[:, :, :, :]).rearrange("p m s d -> p m (s d)")
                    srcs = [src[:, 4 * (f % 2) + m, :] for m in range(4)]
                else:
                    pe.wait_ge(att_ready, i + 1)
                    srcs = [att[:, 4 * i + t, f * P:(f + 1) * P] for t in range(4)]
                for m, s in enumerate(srcs):
                    ins = nc.tensor.transpose(psum[:, 7, m * P:(m + 1) * P], s, ident[:, :])
                ins.then_inc(x_fill, 1)

            def score(u, between):
                i, hd = u // HEADS, u % HEADS
                if hd == 0:
                    pe.wait_ge(x_read, FILL_NO["stack", i, 3] + 1)
                r = SC_NO[u]
                for m in range(2):
                    for c0, n in sc_chunks(i):
                        if r >= 4:
                            pe.wait_ge(sc_read, r - 3)
                        diag = c0 + n == (i + 1) * P
                        ins = M(psum[:, r % 4, 0:n], q_stack[i % 2][:, 2 * hd + m, :], k_stack[:, 2 * hd + m, c0:c0 + n],
                                start=True, stop=not diag, skip_group_check=diag)
                        if diag:
                            ins = M(psum[:, r % 4, n - P:n], ident_r[:, :], mask_r[:, :], start=False, stop=True,
                                    skip_group_check=True)
                        ins.then_inc(sc_mm, 1)
                        r += 1

            def attend(u):
                if not 0 <= u < UNITS:
                    return
                i, hd = u // HEADS, u % HEADS
                s = u % 3
                pe.wait_ge(a_ready, u + 1)
                groups = at_groups(u)
                if u == 0:
                    pe.wait_ge(v_ld, 16)

                def turn(g):
                    gn, (k0, nk) = AT_NO[u] + g, groups[g]
                    if gn >= 2:
                        pe.wait_ge(at_ready, gn - 1)
                    for k in range(nk):
                        ins = nc.tensor.transpose(psum[:, 4 + gn % 2, k * P:(k + 1) * P],
                                                  scores[s][:, 0, (k0 + k) * P:(k0 + k + 1) * P], ident[:, :])
                    ins.then_inc(at_mm, 1)

                def product(g):
                    gn, (k0, nk) = AT_NO[u] + g, groups[g]
                    pe.wait_ge(at_ready, gn + 1)
                    if g == 0 and u:
                        pe.wait_ge(o_read, u)
                    for k in range(nk):
                        ins = M(psum[:, 6, 0:VD], a_t[gn % 2][:, k * P:(k + 1) * P],
                                v_sb[:, k0 + k, hd * VD:(hd + 1) * VD], start=(k0 + k == 0), stop=(k0 + k == i))
                    ins.then_inc(pv_mm, 1)

                last = len(groups) - 1
                turn(0)
                if last:
                    turn(1)
                yield
                for g in range(last + 1):
                    product(g)
                    if g + 2 <= last:
                        turn(g + 2)
                    yield

            for x in range(4):
                fill(x)
            for u in range(STEPS):
                for x in fills_at(u):
                    fill(x)
                pieces = attend(u - 2)
                next(pieces, None)
                if u < UNITS:
                    score(u, pieces)
                for _ in pieces:
                    pass

            pe.wait_ge(x_read, len(FILLS))
            pe.wait_ge(o_read, UNITS)
            pe.wait_ge(sc_read, SC_NO[UNITS])
            pe.wait_ge(at_ready, AT_NO[UNITS])
            for hc in range(2):
                w0 = 2 * NI + hc * C_ITEMS
                n0 = hc * HT
                for t in range(HT):
                    n, tok = n0 + t, slice(t * P, (t + 1) * P)
                    pe.wait_ge(mix_ready, n + 1)
                    for cb in range(2):
                        o, col = 2 * n + cb, slice(cb * BLK, (cb + 1) * BLK)
                        if t >= 2:
                            pe.wait_ge(wo_read, o - 3)
                        elif hc:
                            pe.wait_ge(ff2_read, FG * 2 * HT - 3 + 2 * t + cb)
                        for i in range(KC_OUT):
                            if t == 0 and cb == 0:
                                item_ready(w0 + i)
                            slot = wo_slot(hc, i)
                            for kk in range(2):
                                k = 2 * i + kk
                                wh, wl = by_k2(w_hi[slot][:, :])[:, kk, col], by_k2(w_lo[slot][:, :])[:, kk, col]
                                M(psum[:, 4 + o % 4, :], h_hi[:, k, tok], wh, start=(k == 0), stop=False)
                                M(psum[:, 4 + o % 4, :], h_hi[:, k, tok], wl, start=False, stop=False)
                                ins = M(psum[:, 4 + o % 4, :], h_lo[:, k, tok], wh, start=False, stop=(k == DC - 1))
                        ins.then_inc(wo_mm, 1)
                    if t:
                        transposes(NT + n - 1, xn2)

                def group(g, q, first=False):
                    w = 2 * g + (w0 + KC_OUT)
                    s1, s2 = 2 * q, 2 * q + 1
                    pe.wait_ge(wlo_ready, w + 1)
                    for b in range(NB):
                        if first and b:
                            transposes(NT + n0 + HT - 1, xn2)
                        for j in range(2):
                            f = 2 * b + j
                            if not (first and b == 0):
                                pe.wait_ge(relu_ready, 4 * g + (4 * FG * hc + f - 1))
                            if first:
                                pe.wait_ge(h_ready, NT + n0 + 4 * (b + 1))
                            col, tok = slice(j * P, (j + 1) * P), slice(b * BLK, (b + 1) * BLK)
                            wh, wl = by_k8(w_hi[s1][:, :]), by_k8(w_lo[s1][:, :])
                            ins = mm3(psum[:, 2 + f % 2, :], [(wh[:, k, col], wl[:, k, col], h_hi[:, k, tok], h_lo[:, k, tok])
                                                              for k in range(DC)])
                            ins.then_inc(ff1_mm, 1)
                    pe.wait_ge(wlo_ready, w + 2)
                    wh, wl = by_k2(w_hi[s2][:, :]), by_k2(w_lo[s2][:, :])
                    for o in range(2 * HT):
                        t, cb = o // 2, o % 2
                        tok, col = slice(t * P, (t + 1) * P), slice(cb * BLK, (cb + 1) * BLK)
                        if o % 8 == 0:
                            pe.wait_ge(u_ready, 4 * g + (4 * FG * hc + o // 4 + 2))
                        if first and o < 4:
                            pe.wait_ge(wo_read, 2 * (n0 + HT) - 3 + o)
                        else:
                            pe.wait_ge(ff2_read, 16 * g + (16 * FG * hc + o - 3))
                        ins = mm3(psum[:, 4 + o % 4, :], [(u_hi[:, j, tok], u_lo[:, j, tok], wh[:, j, col], wl[:, j, col])
                                                          for j in range(2)])
                        ins.then_inc(ff2_mm, 1)

                group(0, 0, first=True)
                group(1, 1)
                with pe.Fori(1, FG // 2) as it:
                    for q in range(2):
                        group(it * 2 + q, q)


INPUTS = ["x", "c", "w_ada", "b_ada", "norm1_g", "norm2_g", "w_in", "w_out", "q_norm_g", "k_norm_g",
          "lam_params", "attn_sub_g", "conf_dw_w", "conf_dw_b", "conf_ln_g", "conf_ln_b", "short_conv_w",
          "pool_w", "pool_scale", "w_ff1", "w_ff2"]


def kernel(**inputs):
    import numpy as np
    import concourse.bacc as bacc
    from concourse.bass_utils import run_bass_kernel_spmd

    nc = bacc.Bacc("TRN2", target_bir_lowering=False, num_devices=1)
    arrays, args = {}, []
    for name in INPUTS:
        a = np.ascontiguousarray(inputs[name])
        arrays["in_" + name] = a
        args.append(nc.dram_tensor("in_" + name, a.shape, mybir.dt.from_np(a.dtype), kind="ExternalInput").ap())
    out = nc.dram_tensor("out", (1, SEQ, D), F32, kind="ExternalOutput").ap()
    trunk(nc, *args, out)
    r = run_bass_kernel_spmd(nc, [arrays], core_ids=[0])
    return r.results[0]["out"]
```

```python
from contextlib import ExitStack

import concourse.bass as bass
from concourse import mybir

F32 = mybir.dt.float32
F32R = mybir.dt.float32r
ALU = mybir.AluOpType
ACT = mybir.ActivationFunctionType
AX = mybir.AxisListType

P = 128
SEQ = 2048
D = 1024
DC = D // P
NT = SEQ // P
HALF = SEQ // 2
HT = HALF // P
BLK = 512
NB = HALF // BLK
GW = 256
GC = GW // P
D_FF = 4 * D
HEADS, QKD, VD = 4, 32, 64
MAPS = 2 * HEADS
SCALE = QKD ** -0.5
LAM_INIT = 0.2
EPS = 1e-6
TAPS = 31
STAPS = 3
POOL_HALO = 16
NEG = -1.0e30

Q0, K0, V0, VAL0, GATE0, BG0, CG0, XC0, UD0 = range(0, 9 * GW, GW)
ITEMS = [("q", Q0), ("k", K0), ("v", V0), ("gate", GATE0), ("val", VAL0), ("ud", UD0),
         ("cg", CG0), ("xc", XC0), ("bg", BG0)]
NI = len(ITEMS)
ITEM = DC * GW
KC_OUT = 4
FG = D_FF // GW
C_ITEMS = KC_OUT + 2 * FG
BROADCASTS = 8

R_C, R_B, R_N1, R_N2 = 0, 8, 56, 64
R_DWB, R_LNG, R_LNB, R_PSC, R_END1 = 72, 74, 76, 78, 80
R_DWW, R_SW, R_END2 = 0, 62, 68


def projections():
    out = []

    for h in range(2):
        for t in range(0, HT, 2):
            out += [("qk", h, t, 0), ("qk", h, t + 1, 0), ("v", h, t, 0)]
        for kind in ("gate", "val", "ud", "cg", "pool", "xc", "bg"):
            for b in range(NB):
                if h and kind in LN_AT:
                    out.append(("ln",) + LN_AT[kind] + (b,))
                out += [(kind, h, c, b) for c in range(GC)]
    return out


LN_AT = {"gate": (0, 0), "val": (0, 1), "bg": (1, 0)}


UNITS = NT * HEADS
RING = 6
LN_STEP = 7
STEPS = UNITS + 7


def att_stage(u, k):
    for j in range(NT // 4):
        if u == 4 * HEADS * (j + 1) + 3 + ((0, 1, 3, 6, 7) if j < NT // 4 - 1 else (0, 0, 1, 2, 3))[k]:
            return j
    return None


def fills_of(u):
    out = [("stack", u // HEADS + 1, u % HEADS)] if u // HEADS + 1 < NT else []
    out += [("ln", 1, s) for s in (0, 1) if u == LN_STEP + 2 * s]
    return out + [("att", j, f) for j in range(NT // 4) for f in range(GC) if att_stage(u, 3 + f) == j]


FILLS = [("stack", 0, f) for f in range(4)] + [x for u in range(STEPS) for x in fills_of(u)]
FILL_NO = {x: n for n, x in enumerate(FILLS)}


def fills_at(u):
    return [FILL_NO[x] for x in fills_of(u)]


def splits_at(u):
    return [(n, a) for n in range(1, NT) for a in range(2) if u == max(0, 4 * n - 6 + 2 * a)]


def sc_chunks(i):
    n = (i + 1) * P
    return [(c0, min(BLK, n - c0)) for c0 in range(0, n, BLK)]


def at_groups(u):
    n = u // HEADS + 1
    return [(k0, min(4, n - k0)) for k0 in range(0, n, 4)]


def running(counts):
    out = [0]
    for n in counts:
        out.append(out[-1] + n)
    return out


SC_NO = running(2 * len(sc_chunks(u // HEADS)) for u in range(UNITS))
AT_NO = running(len(at_groups(u)) for u in range(UNITS))


def trunk(nc, x, c, w_ada, b_ada, norm1_g, norm2_g, w_in, w_out, q_norm_g, k_norm_g, lam_params,
          attn_sub_g, conf_dw_w, conf_dw_b, conf_ln_g, conf_ln_b, short_conv_w, pool_w, pool_scale,
          w_ff1, w_ff2, out):
    ctx = ExitStack()
    with ctx:
        KB = 1024
        base = 16512

        def sb(name, kb, shape, dt=F32):
            return nc.alloc_sbuf_tensor_at("sb_" + name, shape, dt, offset=base + int(kb * KB))

        def sem(name):
            return ctx.enter_context(nc.semaphore(name))

        qkv_d = nc.dram_tensor("qkv_scratch", (SEQ, 3 * GW), F32).ap()
        mix_d = nc.dram_tensor("mix_scratch", (D, SEQ), F32).ap()

        ident = sb("ident", 0, [P, P])
        ident_r = sb("ident_r", 0.5, [P, P], F32R)
        mask_r = sb("mask_r", 1, [P, P], F32R)
        ones_mean = sb("ones_mean", 1.5, [P, P])
        pool_blk = sb("pool_blk", 2, [P, GC, P])
        col1 = sb("col1", 3, [P, R_END1])
        col2 = sb("col2", 3.375, [P, R_END2])
        gain_qk = sb("gain_qk", 3.75, [P, 2, QKD])
        gain_sub = sb("gain_sub", 4, [P, VD])
        lam_in = sb("lam_in", 4.25, [P, 4, QKD])
        small = sb("small", 4.75, [P, 96])
        silu_c = sb("silu_c", 5.125, [P, DC])
        gain1 = sb("gain1", 5.1875, [P, DC])
        shift1 = sb("shift1", 5.25, [P, DC])
        gain2 = sb("gain2", 5.3125, [P, DC])
        shift2 = sb("shift2", 5.375, [P, DC])
        inv_win = sb("inv_win", 5.4375, [P, GC])
        inv_first = sb("inv_first", 5.5, [P, GC, POOL_HALO])
        bn = sb("bn", 5.6875, [P, 2, 6])
        stat = sb("stat", 5.75, [P, 16])
        diag_sum = sb("diag_sum", 5.8125, [P, 2 * DC])
        eps_col, lam_neg = small[:, 0:1], small[:, 1:2]
        gate_row = sb("gate_row", 6, [P, 2, D])
        h_hi = sb("h_hi", 14, [P, DC, HALF], F32R)
        h_lo = sb("h_lo", 46, [P, DC, HALF], F32R)
        w_hi = [sb(f"w_hi{s}", 78 + 16 * s, [P, ITEM], F32R) for s in range(4)]
        w_lo = [sb(f"w_lo{s}", 86 + 16 * s, [P, ITEM], F32R) for s in range(4)]
        w_raw = sb("w_raw", 142, [P, ITEM])
        gated = sb("gated", 126, [P, GC, HALF])
        acc = sb("acc", 134, [P, GC, HALF])
        h_tmp = sb("h_tmp", 150, [P, DC, P])
        conf = sb("conf", 154, [P, GC, TAPS - 1 + HALF])
        halo2 = sb("halo2", 162.25, [P, GC, 2])
        x_in = [sb(f"x_in{s}", 162.5 + 4 * s, [P, D]) for s in range(2)]
        prod = sb("prod", 170.5, [P, GC, 2 + HALF])
        pool_in = sb("pool_in", 170.5, [P, GC, HALF])
        ln_sq = [sb(f"ln_sq{h}", k, [P, GC, BLK]) for h, k in enumerate((170.5, 142))]
        ln_sig = [[sb(f"ln_sig{h}{cc}", k, [P, BLK]) for cc, k in enumerate(ks)]
                  for h, ks in enumerate(((174.5, 170.5), (146, 142)))]
        ln_rs = [sb(f"ln_rs{h}", k, [P, BLK]) for h, k in enumerate((176.5, 148))]
        stage = [sb(f"stage{s}", 179 + 2 * s, [P, BLK]) for s in range(2)]
        ud = sb("ud", 183, [P, GC, POOL_HALO + BLK])
        win_a = sb("win_a", 187.25, [P, POOL_HALO + BLK])
        win_b = sb("win_b", 189.5, [P, POOL_HALO + BLK])
        ada = sb("ada", 191.75, [P, 2 * D])
        qk_sq = sb("qk_sq", 199.75, [P, BLK])
        qkv_out = [sb(f"qkv_out{s}", 201.75 + 2 * s, [P, BLK]) for s in range(2)]
        norm_acc = sb("norm_acc", 187.25, [P, D])
        ada_first = [sb(f"ada_first{s}", k, [P, 2 * D]) for s, k in enumerate((126, 134, 154, 171))]
        table1 = sb("table1", 183, [R_END1, P])
        table2 = sb("table2", 183.5, [R_END2, P])
        k_stack = sb("k_stack", 14, [P, MAPS, SEQ], F32R)
        scores = [sb(f"scores{s}", 94 + 16 * s, [P, 2, SEQ]) for s in range(3)]
        att = sb("att", 150, [P, NT, GW])
        v_sb = sb("v_sb", 166, [P, NT, GW])
        q_stack = [sb(f"q_stack{s}", 183 + 4 * s, [P, MAPS, P], F32R) for s in range(2)]
        q_split = sb("q_split", 191, [P, MAPS, 4, QKD], F32R)
        k_split = sb("k_split", 195, [P, MAPS, 4, QKD], F32R)
        qk_in = [sb(f"qk_in{s}", 199 + 2 * s, [P, 2, GW]) for s in range(2)]
        a_t = [sb(f"a_t{s}", 203 + 2 * s, [P, BLK]) for s in range(2)]
        att_sq = sb("att_sq", 78, [P, 4, GW])
        att_t = [sb(f"att_t{s}", 82 + 4 * s, [P, GC, BLK]) for s in range(2)]
        bst = sb("bst", 90, [P, 3, 24])
        inv_s = sb("inv_s", 90.5, [P, 4])
        ams = sb("ams", 91, [P, 48])
        x_new = sb("x_new", 150, [P, HT, D])
        u_hi = sb("u_hi", 182, [P, 2, HALF], F32R)
        u_lo = sb("u_lo", 190, [P, 2, HALF], F32R)
        mix_in = [sb(f"mix_in{s}", 182 + 4 * s, [P, DC, P]) for s in range(2)]
        mix_early = [sb(f"mix_early{s}", 198 + 4 * s, [P, DC, P]) for s in range(2)]
        w_raw_x = [sb(f"w_raw_x{s}", 166 + 8 * s, [P, ITEM]) for s in range(2)]
        wo_gated = sb("wo_gated", 194, [P, BLK])
        relu_t = [sb(f"relu_t{s}", 198 + 2 * s, [P, BLK]) for s in range(4)]
        xn2 = sb("xn2", 198, [P, D])
        h_tmp2 = sb("h_tmp2", 202, [P, DC, P])

        psum = ctx.enter_context(nc.psum_tensor("ps", [P, 8, BLK], F32))
        ps_t = psum[:, 0:2, :].rearrange("p a b -> p (a b)").rearrange("p (k t) -> p k t", t=P)

        tab_ld, bc_ld, dve_chain, act_chain, pool_chain = [sem(n) for n in (
            "tab_ld", "bc_ld", "dve_chain", "act_chain", "pool_chain")]
        const_ready, tab_t, tab_col, sigc_ready, siluc_ready = [sem(n) for n in (
            "const_ready", "tab_t", "tab_col", "sigc_ready", "siluc_ready")]
        ada0_ld = [sem(f"ada0_ld{s}") for s in range(4)]
        ada0_used, mod1_mm, mod1_ready = sem("ada0_used"), sem("mod1_mm"), sem("mod1_ready")
        norm_read = sem("norm_read")
        ada_ld, ada_scaled, ada_used, mod2_mm, bias_ld = [sem(n) for n in (
            "ada_ld", "ada_scaled", "ada_used", "mod2_mm", "bias_ld")]
        lam_sums, lam_exp = sem("lam_sums"), sem("lam_exp")
        qk_ready = sem("qk_ready")
        x_ld = [sem(f"x_ld{s}") for s in range(2)]
        ms_ready, rms_ready, xn_ready, xt_ready = [sem(n) for n in (
            "ms_ready", "rms_ready", "xn_ready", "xt_ready")]
        hmod_ready, hhi_ready, h_ready = sem("hmod_ready"), sem("hhi_ready"), sem("h_ready")
        w_ld, w_folded, whi_ready, wlo_ready = [sem(n) for n in (
            "w_ld", "w_folded", "whi_ready", "wlo_ready")]
        proj_ready = sem("proj_ready")
        qsq_ready, qss_ready, qrms_ready, qn_ready = [sem(n) for n in (
            "qsq_ready", "qss_ready", "qrms_ready", "qn_ready")]
        qkv_st = [sem(f"qkv_st{s}") for s in range(2)]
        v_ready, gated_ready, conf_ready, conv_ready, prod_ready, short_ready = [sem(n) for n in (
            "v_ready", "gated_ready", "conf_ready", "conv_ready", "prod_ready", "short_ready")]
        lnd_ready, lnsq_ready, lnsd_ready, lnz_ready, lny_ready, lnsig_ready, lnout_ready = [sem(n) for n in (
            "lnd_ready", "lnsq_ready", "lnsd_ready", "lnz_ready", "lny_ready", "lnsig_ready", "lnout_ready")]
        ud_ready, win_ready, pool_y, halo_saved, poolout_ready = [sem(n) for n in (
            "ud_ready", "win_ready", "pool_y", "halo_saved", "poolout_ready")]
        stage_st, ln_st, mod2_ready = [[sem(f"{n}{s}") for s in range(2)] for n in ("stage_st", "ln_st")] + [sem("mod2_ready")]
        qk_ld, v_ld = [sem("qk_ld0"), sem("qk_ld1")], sem("v_ld")
        split_hi, split_lo, x_fill, x_read = [sem(n) for n in ("split_hi", "split_lo", "x_fill", "x_read")]
        sc_mm, sc_read, max_ready, exp_done, a_ready = [sem(n) for n in (
            "sc_mm", "sc_read", "max_ready", "exp_done", "a_ready")]
        at_mm, at_ready, pv_mm, o_read = [sem(n) for n in ("at_mm", "at_ready", "pv_mm", "o_read")]
        asq_ready, ams_ready, arms_ready, arcp_ready, att_ready = [sem(n) for n in (
            "asq_ready", "ams_ready", "arms_ready", "arcp_ready", "att_ready")]
        attt_st = [sem("attt_st0"), sem("attt_st1")]
        mix_ld = [sem("mix_ld0"), sem("mix_ld1")]
        wx_ld = [sem("wx_ld0"), sem("wx_ld1")]
        mixhi_ready, mix_ready, xr_ld, wo_mm, wo_read = [sem(n) for n in (
            "mixhi_ready", "mix_ready", "xr_ld", "wo_mm", "wo_read")]
        ff1_mm, relu_ready, sq_ready, uhi_ready, u_ready = [sem(n) for n in (
            "ff1_mm", "relu_ready", "sq_ready", "uhi_ready", "u_ready")]
        ff2_mm, ff2_read, out_st = [sem(n) for n in ("ff2_mm", "ff2_read", "out_st")]

        OUTS = projections()
        OUT_NO = {o: n for n, o in enumerate(OUTS)}

        def bank(o):
            return psum[:, 2 + o % RING, :]

        def chan_no(h, cc, b):
            return (h * NB + b) * GC + cc

        def prob(u, m, c0, n):
            s = u % 3
            if u // HEADS < NT // 2:
                return scores[s][:, 0, m * HALF + c0:m * HALF + c0 + n]
            return scores[s][:, m, c0:c0 + n]

        def att_scaling(j):
            return (att[:, 4 * j:4 * j + 4, :].rearrange("p i (a d) -> p (i a) d", d=VD),
                    ams[:, 32:48].rearrange("p (a o) -> p a o", o=1).to_broadcast([P, 16, VD]),
                    gain_sub[:, :].rearrange("p (o d) -> p o d", o=1).to_broadcast([P, 16, VD]))

        def mod_sums(h):
            return gate_row[:, h, :], norm_acc[:, :] if h else gate_row[:, 1, :]

        def ln_bank(h, b, s):
            return psum[:, 7, :] if (h, b) == (1, 1) else bank(OUT_NO["ln", h, b, s])

        def ln_summed(h, b, s):
            return (x_fill, FILL_NO["ln", 1, s] + 1) if (h, b) == (1, 1) else (proj_ready, OUT_NO["ln", h, b, s] + 1)

        def ln_read(h, b, s):
            if (h, b) == (1, 1):
                return x_read, FILL_NO["ln", 1, s] + 1
            return (lnsd_ready if s else lnd_ready), h * NB + b + 1

        def released(o):
            kind, h, a, b = OUTS[o]
            if kind == "qk":
                return qn_ready, h * HT + a + 1
            if kind == "v":
                return v_ready, h * HT // 2 + a // 2 + 1
            if kind == "ln":
                return ln_read(h, a, b)
            n = chan_no(h, a, b)
            if kind in ("gate", "cg"):
                return gated_ready, n + h * NB * GC + (NB * GC if kind == "cg" else 0) + 1
            return {"ud": ud_ready, "pool": poolout_ready, "val": conf_ready, "xc": prod_ready,
                    "bg": short_ready}[kind], n + 1

        w_in_v = w_in.rearrange("a (k p) n -> p (a k) n", p=P)
        w_out_v = w_out.rearrange("a (k p) n -> p (a k) n", p=P)
        w_ff1_v = w_ff1.rearrange("a (k p) n -> p (a k) n", p=P)
        w_ff2_v = w_ff2.rearrange("a (k p) n -> p (a k) n", p=P)
        w_ada_v = w_ada.rearrange("a (k p) n -> p (a k) n", p=P)
        x_v = x.rearrange("a (t p) d -> p (a t) d", p=P)
        out_v = out.rearrange("a (t p) d -> p (a t) d", p=P)
        qkv_v = qkv_d.rearrange("(t p) d -> p t d", p=P)
        mix_v = mix_d.rearrange("(k p) t -> p k t", p=P)

        def used(w):
            h, i = divmod(w, NI)
            if i < 3:
                last = ("v", h, HT - 2, 0) if i == 2 else ("qk", h, HT - 1, 0)
            else:
                last = (ITEMS[i][0], h, GC - 1, NB - 1)
            return proj_ready, OUT_NO[last] + 1

        def qk_turn(n):
            return n // 2 * 3 + n % 2

        def v_turn(h, t):
            return (h * HT + t) // 2 * 3 + 2

        def slot_of_qk(n):
            return qk_turn(n) % 2

        def slot_of_v(h, t):
            return v_turn(h, t) % 2

        def stores_before_qk(n):
            return qk_turn(n) // 2

        def stores_before_v(h, t):
            return v_turn(h, t) // 2

        def stores_of_stage(n, short):
            return (2 * NB * GC * (n // (NB * GC)) + NB * GC * short + n % (NB * GC)) // 2

        def heads_tails(a):
            if a == 0:
                return q_split[:, :, 0:2, :], q_split[:, :, 2:4, :]
            return k_split[:, :, 0:4:2, :], k_split[:, :, 1:4:2, :]

        def mix_buf(n):
            return mix_early[n % 2] if n in (HT, HT + 1) else mix_in[n % 2]

        def wo_slot(hc, i):
            return i if hc else (i + 1) % 4

        def wo_raw(hc, i):
            return w_raw_x[i - 1] if hc == 0 and i in (1, 2) else w_raw

        def loaded(w):
            return w_ld, (w - 1) * 16

        def wo_loaded(hc, i):
            if hc == 0 and i < 3:
                return (wx_ld[i - 1], 16) if i else (w_ld, (2 * NI + 1) * 16)
            return loaded(2 * NI + hc * C_ITEMS + i)

        def by_k8(a):
            return a.rearrange("p (k n) -> p k n", k=DC)

        def by_k2(a):
            return a.rearrange("p (k n) -> p k n", k=2)

        def f32(ap):
            return ap.bitcast(F32)

        block = ctx.enter_context(nc.Block())

        @block.sync
        def _(sp):
            def rows(src):
                return src.rearrange("o (a p) -> (o a) p", p=P)
            for r0, r1, src in ((R_C, R_B, c), (R_B, R_N1, b_ada), (R_N1, R_N2, norm1_g), (R_N2, R_DWB, norm2_g),
                                (R_DWB, R_LNG, conf_dw_b), (R_LNG, R_LNB, conf_ln_g),
                                (R_LNB, R_PSC, conf_ln_b), (R_PSC, R_END1, pool_scale)):
                sp.dma_start(table1[r0:r1, :], rows(src)).then_inc(tab_ld, 16)
            for r0, r1, src in ((R_DWW, R_SW, conf_dw_w), (R_SW, R_END2, short_conv_w)):
                sp.dma_start(table2[r0:r1, :], src.rearrange("o j (a p) -> (o j a) p", p=P)).then_inc(tab_ld, 16)
            def load_small():
                sp.wait_ge(const_ready, 1)
                for g in range(4):
                    r = 64 * (g % 2)
                    sp.dma_start(pool_blk[r:r + 64, g // 2, r:r + 64], pool_w[0, g, :, :]).then_inc(bc_ld, 16)
                for dst, src in ((gain_qk[:, 0, :], q_norm_g[0, :]), (gain_qk[:, 1, :], k_norm_g[0, :]),
                                 (gain_sub[:, :], attn_sub_g[0, :]), (lam_in[:, :, :], lam_params[0, :, :])):
                    sp.dma_start(dst, src.partition_broadcast(P)).then_inc(bc_ld, 16)

            def raw_free(w):
                sp.wait_ge(whi_ready, w)
                sp.wait_ge(wlo_ready, w)

            def load_w_in(w):
                if w:
                    raw_free(w)
                c0 = ITEMS[w % NI][1]
                sp.dma_start(by_k8(w_raw[:, :]), w_in_v[:, :, c0:c0 + GW]).then_inc(w_ld, 16)

            for k in range(DC):
                if k >= 4:
                    sp.wait_ge(ada0_used, k - 3)
                sp.dma_start(ada_first[k % 4][:, :], w_ada_v[:, k, 0:2 * D]).then_inc(ada0_ld[k % 4], 16)
                if k in (4, 5):
                    sp.dma_start(x_in[k - 4][:, :], x_v[:, k - 4, :]).then_inc(x_ld[k - 4], 16)
                if k == 5:
                    load_small()
                if k == 6:
                    load_w_in(0)

            def load_x(n):
                if n >= 2:
                    sp.wait_ge(xt_ready, n - 1)
                sp.dma_start(x_in[n % 2][:, :], x_v[:, n, :]).then_inc(x_ld[n % 2], 16)

            def load_ada(h, k):
                if h * DC + k:
                    sp.wait_ge(ada_used, h * DC + k)
                if h and k == 0:
                    sp.wait_ge(mod2_ready, 1)
                gate0, norm0 = (2 + 3 * h) * D, (3 + h) * D
                sp.dma_start(ada[:, 0:D], w_ada_v[:, k, gate0:gate0 + D]).then_inc(ada_ld, 16)
                sp.dma_start(ada[:, D:2 * D], w_ada_v[:, k, norm0:norm0 + D]).then_inc(ada_ld, 16)

            def load_bias(h):
                sp.wait_ge(ada_used, (h + 1) * DC)
                gate0 = (2 + 3 * h) * D
                sp.dma_start(ada[:, 0:D], b_ada[0, gate0:gate0 + D].partition_broadcast(P)).then_inc(bias_ld, 16)

            def store_qk(n):
                sp.wait_ge(qk_ready, n + 1)
                s = slot_of_qk(n)
                sp.dma_start(qkv_v[:, n, 0:2 * GW], qkv_out[s][:, :]).then_inc(qkv_st[s], 16)

            def store_v(h, t):
                s = slot_of_v(h, t)
                sp.wait_ge(v_ready, h * HT // 2 + t // 2 + 1)
                sp.dma_start(qkv_v[:, h * HT + t:h * HT + t + 2, 2 * GW:3 * GW],
                             qkv_out[s][:, :].rearrange("p (t d) -> p t d", t=2)).then_inc(qkv_st[s], 16)

            def store_mixer(h, chunk, ready):
                for b in range(NB):
                    for cc in range(GC):
                        n = chan_no(h, cc, b)
                        t0 = h * HALF + b * BLK
                        sp.wait_ge(ready, n + 1)
                        sp.dma_start(mix_v[:, chunk + cc, t0:t0 + BLK], stage[n % 2][:, :]).then_inc(stage_st[n % 2], 16)

            def store_ln(h, b):
                blk = slice(b * BLK, (b + 1) * BLK)
                sp.wait_ge(lnout_ready, GC * (NB * h + b + 1))
                sp.dma_start(mix_v[:, 2:4, h * HALF + b * BLK:h * HALF + (b + 1) * BLK], acc[:, :, blk]).then_inc(ln_st[b], 16)

            def load_qk(i):
                if i >= 2:
                    sp.wait_ge(split_lo, 2 * (i - 1))
                sp.dma_start(qk_in[i % 2][:, :, :],
                             qkv_v[:, i, 0:2 * GW].rearrange("p (a d) -> p a d", a=2)).then_inc(qk_ld[i % 2], 16)

            def store_turn(n):
                store_qk(n)
                if n % 2:
                    store_v(n // HT, n % HT - 1)

            load_w_in(1)
            for h in range(2):
                w0 = h * NI
                for t in range(HT):
                    n = h * HT + t
                    if t == 0:
                        load_w_in(w0 + 2)
                    if n + 2 < NT:
                        load_x(n + 2)
                    if t >= 2:
                        store_turn(n - 2)
                    if t == 2:
                        load_w_in(w0 + 3)
                    if t % 2 == 0:
                        load_ada(h, t // 2)
                store_turn(h * HT + HT - 2)
                load_ada(h, 4)
                load_w_in(w0 + 4)
                store_turn(h * HT + HT - 1)
                load_w_in(w0 + 5)
                load_w_in(w0 + 6)
                load_ada(h, 5)
                load_ada(h, 6)
                if h:
                    store_ln(0, 0)
                load_w_in(w0 + 7)
                load_ada(h, 7)
                if h:
                    store_ln(0, 1)
                load_bias(h)
                load_w_in(w0 + 8)
                if h == 0:
                    load_w_in(NI)
                store_mixer(h, 6, poolout_ready)
                if h == 0:
                    load_w_in(NI + 1)
                if h:
                    for s in range(2):
                        sp.wait_ge(qkv_st[s], 16 * (NT + NT // 2) // 2)
                    sp.wait_ge(ada_used, 2 * DC)
                    load_qk(0)
                    load_qk(1)
                store_mixer(h, 4, short_ready)
            store_ln(1, 0)

            for s in range(2):
                sp.wait_ge(stage_st[s], 16 * 4 * NB * GC // 2)
            sp.wait_ge(proj_ready, len(OUTS))
            sp.wait_ge(mod2_ready, 2)
            sp.wait_ge(h_ready, NT)
            def load_w_out(hc, i):
                w = 2 * NI + hc * C_ITEMS + i
                raw = wo_raw(hc, i)
                if raw is w_raw:
                    raw_free(w if hc or i == 0 else w - 2)
                sp.dma_start(by_k2(raw[:, :]), w_out_v[:, 2 * i:2 * i + 2, :]).then_inc(wo_loaded(hc, i)[0], 16)

            def load_mix(n):
                if n % HT >= 2:
                    sp.wait_ge(mix_ready, n - 1)
                sp.dma_start(mix_buf(n)[:, :, :], mix_v[:, :, n * P:(n + 1) * P]).then_inc(mix_ld[n % 2], 16)

            sp.dma_start(v_sb[:, :, :], qkv_v[:, :, 2 * GW:3 * GW]).then_inc(v_ld, 16)
            for i in range(2, NT):
                load_qk(i)
                if i == 5:
                    store_ln(1, 1)
                if i == 7:
                    load_w_out(0, 0)
            def store_out(hc, t):
                sp.wait_ge(ff2_read, (hc + 1) * FG * 2 * HT - 2 * (HT - 1 - t))
                sp.dma_start(out_v[:, hc * HT + t, :], x_new[:, t, :]).then_inc(out_st, 16)

            def store_att(j):
                sp.wait_ge(x_read, FILL_NO["att", j, 1] + 1)
                sp.dma_start(mix_v[:, 0:2, j * BLK:(j + 1) * BLK], att_t[j % 2][:, :, :]).then_inc(attt_st[j % 2], 16)

            for j in range(NT // 4 - 1):
                store_att(j)

            for s in range(2):
                sp.wait_ge(attt_st[s], 16)
                sp.wait_ge(ln_st[s], 32)
            sp.wait_ge(sc_mm, SC_NO[UNITS])
            for n in (0, 1):
                load_mix(n)
            sp.wait_ge(pv_mm, AT_NO[UNITS])
            load_w_out(0, 1)
            load_w_out(0, 2)
            store_att(NT // 4 - 1)
            load_w_out(0, 3)
            for hc in range(2):
                w0 = 2 * NI + hc * C_ITEMS
                if hc:
                    for s in range(2):
                        sp.wait_ge(attt_st[s], 32)
                    load_w_out(1, 0)
                    load_w_out(1, 1)
                    sp.wait_ge(u_ready, 4 * FG)
                    for n in (0, 1):
                        load_mix(HT + n)
                    load_w_out(1, 2)
                    load_w_out(1, 3)
                    for t in range(HT):
                        store_out(0, t)
                    sp.wait_ge(ff2_mm, 16 * FG)
                    sp.wait_ge(out_st, 16 * HT)
                for t in range(HT):
                    n = hc * HT + t
                    if n:
                        sp.wait_ge(xr_ld, 16 * n)
                    if n == HT // 2:
                        sp.wait_ge(wlo_ready, w0 + 3)
                    sp.dma_start(x_new[:, t, :], x_v[:, n, :]).then_inc(xr_ld, 16)
                    if t + 2 < HT:
                        load_mix(n + 2)

                def load_ff(g):
                    w = 2 * g + (w0 + KC_OUT)
                    raw_free(w)
                    sp.dma_start(by_k8(w_raw[:, :]), w_ff1_v[:, :, bass.ds(g * GW, GW)]).then_inc(w_ld, 16)
                    raw_free(w + 1)
                    sp.dma_start(by_k2(w_raw[:, :]), w_ff2_v[:, bass.ds(g * 2, 2), :]).then_inc(w_ld, 16)

                load_ff(0)
                load_ff(1)
                with sp.Fori(0, FG // 2 - 1) as it:
                    for q in range(2):
                        load_ff(it * 2 + (2 + q))
            for t in range(HT):
                store_out(1, t)
            sp.wait_ge(out_st, 16 * NT)

        @block.gpsimd
        def _(pool):
            links = [0]

            def link(ins):
                links[0] += 1
                ins.then_inc(pool_chain, 1)
                pool.wait_ge(pool_chain, links[0])

            link(pool.memset(pool_blk[:, :, :], 0.0))
            link(pool.memset(ident[:, :], 0.0))
            pool.affine_select(out=ident[:, :], in_=ident[:, :], compare_op=ALU.not_equal, fill=1.0,
                               base=0, pattern=[[-1, P]], channel_multiplier=1)
            link(pool.memset(h_tmp[:, 0, :], 0.0))
            pool.affine_select(out=h_tmp[:, 0, :], in_=h_tmp[:, 0, :], compare_op=ALU.is_ge, fill=NEG,
                               base=0, pattern=[[-1, P]], channel_multiplier=1)
            pool.memset(ones_mean[:, :], 1.0 / GW)
            pool.memset(eps_col, EPS).then_inc(const_ready, 1)

            def norm_gain(n):
                pool.wait_ge(qn_ready, n + 1)
                v = qkv_out[slot_of_qk(n)][:, :].rearrange("p (a m d) -> p a m d", a=2, d=QKD)
                if n == 0:
                    pool.wait_ge(bc_ld, 16 * BROADCASTS)
                pool.tensor_tensor(out=v[:, 0], in0=v[:, 0], op=ALU.mult,
                                   in1=gain_qk[:, 0:1, :].to_broadcast([P, MAPS, QKD]))
                pool.tensor_tensor(out=v[:, 1], in0=v[:, 1], op=ALU.mult,
                                   in1=gain_qk[:, 1:2, :].to_broadcast([P, MAPS, QKD])).then_inc(qk_ready, 1)

            def windows(n, cc):
                pool.wait_ge(ud_ready, n + 1)
                if n:
                    pool.wait_ge(pool_y, n)
                end = POOL_HALO + BLK
                u = ud[:, cc, :]
                link(pool.tensor_tensor(out=win_a[:, 1:end], in0=u[:, 1:end], in1=u[:, 0:end - 1], op=ALU.add))
                last = pool.tensor_tensor(out=win_b[:, 3:end], in0=win_a[:, 3:end], in1=win_a[:, 1:end - 2], op=ALU.add)
                if cc:
                    link(last)
                    link(pool.tensor_tensor(out=win_a[:, 7:end], in0=win_b[:, 7:end], in1=win_b[:, 3:end - 4], op=ALU.add))
                    last = pool.tensor_tensor(out=win_b[:, 15:end], in0=win_a[:, 15:end], in1=win_a[:, 7:end - 8], op=ALU.add)
                last.then_inc(win_ready, 1)

            def ln_out(h, b):
                for cc in range(GC):
                    pool.wait_ge(lnsig_ready, chan_no(h, cc, b) + 1)
                    y = acc[:, cc, b * BLK:(b + 1) * BLK]
                    pool.tensor_tensor(out=y, in0=y, in1=ln_sig[h][cc][:, :], op=ALU.mult).then_inc(lnout_ready, 1)

            def modulation(h, k):
                if k:
                    pool.wait_ge(ada_scaled, 2 * (h * (DC - 1) + k))
                    if k == 1:
                        pool.wait_ge(ada_used, h * DC + 1)
                    for n, acc_k in enumerate(mod_sums(h)):
                        last = pool.tensor_tensor(out=acc_k, in0=acc_k, in1=ada[:, n * D:(n + 1) * D], op=ALU.add)
                    last.then_inc(ada_used, 1)
                    pool.wait_ge(ada_used, h * DC + k + 1)

            for h in range(2):
                for t in range(HT):
                    norm_gain(h * HT + t)
                    if t % 2 == 0:
                        modulation(h, t // 2)
                modulation(h, 4)
                modulation(h, 5)
                if h:
                    ln_out(0, 0)
                modulation(h, 6)
                if h:
                    ln_out(0, 1)
                modulation(h, 7)
                if h:
                    pool.wait_ge(mod2_mm, 3)
                for b in range(NB):
                    for cc in range(GC):
                        windows(chan_no(h, cc, b), cc)
            ln_out(1, 0)

            def split_tail(n, a):
                pool.wait_ge(split_hi, 2 * n + a + 1)
                hi, lo = heads_tails(a)
                src = qk_in[n % 2][:, a, :].rearrange("p (m o d) -> p m o d", o=1, d=QKD).to_broadcast([P, MAPS, 2, QKD])
                pool.tensor_tensor(out=lo, in0=src, in1=f32(hi), op=ALU.subtract).then_inc(split_lo, 1)

            split_tail(0, 0)
            split_tail(0, 1)
            for u in range(STEPS):
                if u == LN_STEP + 4:
                    ln_out(1, 1)
                for n, a in splits_at(u):
                    split_tail(n, a)
                j = att_stage(u, 2)
                if j is not None and j < NT // 4 - 1:
                    pool.wait_ge(arcp_ready, j + 1)
                    y, root, gain = att_scaling(j)
                    link(pool.tensor_tensor(out=y, in0=y, in1=root, op=ALU.mult))
                    pool.tensor_tensor(out=y, in0=y, in1=gain, op=ALU.mult).then_inc(att_ready, 1)
                j = att_stage(u, 0)
                if j is not None:
                    pool.wait_ge(o_read, 16 * (j + 1))
                    y = att[:, 4 * j:4 * j + 4, :]
                    pool.tensor_tensor(out=att_sq[:, :, :], in0=y, in1=y, op=ALU.mult).then_inc(asq_ready, 1)

        @block.scalar
        def _(act):
            A = nc.scalar.activation

            def w_head(w, s, ready, before, raw=w_raw):
                act.wait_ge(*ready)
                if before is not None:
                    act.wait_ge(*before)
                A(w_hi[s][:, :], raw[:, :], ACT.Copy).then_inc(whi_ready, 1)

            def w_in_head(w):
                w_head(w, w % 3, (w_ld, 16 * (w + 1)), used(w - 3) if w >= 3 else None)

            def rms_root(n):
                act.wait_ge(ms_ready, n + 1)
                A(stat[:, 4 * (n % 2) + 3:4 * (n % 2) + 4], stat[:, 4 * (n % 2) + 2:4 * (n % 2) + 3],
                  ACT.Sqrt, bias=eps_col).then_inc(rms_ready, 1)

            def modulate(n, tmp, gain, shift):
                act.wait_ge(xt_ready, n + 1)
                if n:
                    act.wait_ge(h_ready, n)
                for k in range(DC):
                    last = A(tmp[:, k, :], ps_t[:, k, :], ACT.Identity, scale=gain[:, k:k + 1], bias=shift[:, k:k + 1])
                last.then_inc(hmod_ready, 1)

            def h_head(n, tmp):
                act.wait_ge(hmod_ready, n + 1)
                t = n % HT
                A(h_hi[:, :, t * P:(t + 1) * P], tmp[:, :, :], ACT.Copy).then_inc(hhi_ready, 1)

            act.wait_ge(const_ready, 1)
            A(ident_r[:, :], ident[:, :], ACT.Copy)
            A(mask_r[:, :], h_tmp[:, 0, :], ACT.Copy).then_inc(act_chain, 1)
            act.wait_ge(tab_t, 1)
            A(col1[:, :], psum[:, 0, 0:R_END1], ACT.Copy).then_inc(tab_col, 1)
            A(col2[:, :], psum[:, 1, 0:R_END2], ACT.Copy).then_inc(tab_col, 1)
            act.wait_ge(tab_col, 2)
            A(silu_c[:, :], col1[:, R_C:R_B], ACT.Sigmoid).then_inc(sigc_ready, 1)
            act.wait_ge(lam_sums, 1)
            A(small[:, 6:8], small[:, 4:6], ACT.Exp).then_inc(lam_exp, 1)
            act.wait_ge(act_chain, 1)
            rms_root(0)
            rms_root(1)
            w_in_head(0)
            w_in_head(1)
            act.wait_ge(mod1_ready, 1)
            modulate(0, h_tmp, gain1, shift1)
            h_head(0, h_tmp)

            def qk_square(n):
                o = OUT_NO["qk", n // HT, n % HT, 0]
                act.wait_ge(proj_ready, o + 1)
                if n:
                    act.wait_ge(qss_ready, n)
                A(qk_sq[:, :], bank(o), ACT.Square).then_inc(qsq_ready, 1)
                act.wait_ge(qss_ready, n + 1)
                if n:
                    act.wait_ge(qn_ready, n)
                A(small[:, 48:64], small[:, 32:48], ACT.Sqrt, bias=eps_col, scale=1.0 / QKD).then_inc(qrms_ready, 1)

            def ln_square(h, b):
                act.wait_ge(*ln_read(h, b, 0))
                if h or b:
                    act.wait_ge(lnout_ready, GC * (h * NB + b))
                A(ln_sq[h][:, :, :], acc[:, :, b * BLK:(b + 1) * BLK], ACT.Square).then_inc(lnsq_ready, 1)

            def ln_root(h, b):
                act.wait_ge(*ln_summed(h, b, 1))
                A(ln_rs[h][:, :], ln_bank(h, b, 1), ACT.Sqrt, bias=eps_col).then_inc(ln_read(h, b, 1)[0], 1)

            def ln_silu(h, b):
                m, blk = h * NB + b, slice(b * BLK, (b + 1) * BLK)
                act.wait_ge(lnz_ready, m + 1)
                for cc in range(GC):
                    y, n = acc[:, cc, blk], GC * m + cc
                    A(y, y, ACT.Identity, scale=col1[:, R_LNG + cc:R_LNG + cc + 1],
                      bias=col1[:, R_LNB + cc:R_LNB + cc + 1]).then_inc(lny_ready, 1)
                for cc in range(GC):
                    act.wait_ge(lny_ready, GC * m + cc + 1)
                    A(ln_sig[h][cc][:, :], acc[:, cc, blk], ACT.Sigmoid).then_inc(lnsig_ready, 1)

            def each_block(kind, h, evacuate, middle=lambda: None):
                for b in range(NB):
                    if b:
                        middle()
                    for cc in range(GC):
                        o = OUT_NO[kind, h, cc, b]
                        act.wait_ge(proj_ready, o + 1)
                        evacuate(o, cc, b, chan_no(h, cc, b))

            def to_ud(o, cc, b, n):
                if n >= GC:
                    act.wait_ge(halo_saved, n - GC + 1)
                A(ud[:, cc, POOL_HALO:], bank(o), ACT.Copy).then_inc(ud_ready, 1)

            def to_gated(func):
                def evacuate(o, cc, b, n):
                    A(gated[:, cc, b * BLK:(b + 1) * BLK], bank(o), func).then_inc(gated_ready, 1)
                return evacuate

            def to_pool_stage(o, cc, b, n):
                if n >= 2:
                    act.wait_ge(stage_st[n % 2], 16 * stores_of_stage(n, False))
                A(stage[n % 2][:, :], bank(o), ACT.Copy, scale=col1[:, R_PSC + cc:R_PSC + cc + 1]).then_inc(poolout_ready, 1)

            def scale_ada(h, k):
                act.wait_ge(ada_ld, 32 * (h * DC + k + 1))
                if h and k == 0:
                    act.wait_ge(mod2_ready, 1)
                    act.wait_ge(halo_saved, NB * GC)
                for n, acc_k in enumerate(mod_sums(h)):
                    w = ada[:, n * D:(n + 1) * D]
                    ins = A(w if k else acc_k, w, ACT.Copy, scale=silu_c[:, k:k + 1])
                    if k:
                        ins.then_inc(ada_scaled, 1)
                if k == 0:
                    ins.then_inc(ada_used, 1)

            def copy_v(h, t):
                o, s = OUT_NO["v", h, t, 0], slot_of_v(h, t)
                act.wait_ge(proj_ready, o + 1)
                if stores_before_v(h, t):
                    act.wait_ge(qkv_st[s], 16 * stores_before_v(h, t))
                A(qkv_out[s][:, :], bank(o), ACT.Copy).then_inc(v_ready, 1)

            for h in range(2):
                w0 = h * NI
                for t in range(HT):
                    n = h * HT + t
                    if t + 1 < HT:
                        modulate(n + 1, h_tmp, gain1, shift1)
                        h_head(n + 1, h_tmp)
                    if n + 2 < NT:
                        rms_root(n + 2)
                    if t:
                        qk_square(n - 1)
                    if t >= 2 and t % 2 == 0:
                        copy_v(h, t - 2)
                    if t == 0:
                        w_in_head(w0 + 2)
                    if t == HT - 1:
                        w_in_head(w0 + 3)
                    if t % 2:
                        scale_ada(h, t // 2)
                qk_square(h * HT + HT - 1)
                copy_v(h, HT - 2)
                w_in_head(w0 + 4)
                if h:
                    ln_square(0, 0)
                w_in_head(w0 + 5)
                scale_ada(h, 4)
                if h:
                    act.wait_ge(prod_ready, NB * GC * h)

                def middle():
                    scale_ada(h, 5)
                    if h:
                        ln_root(0, 0)

                each_block("gate", h, to_gated(ACT.Sigmoid), middle)
                w_in_head(w0 + 6)
                if h:
                    ln_silu(0, 0)
                    ln_square(0, 1)
                scale_ada(h, 6)
                if h:
                    ln_root(0, 1)
                    ln_silu(0, 1)
                scale_ada(h, 7)
                w_in_head(w0 + 7)
                each_block("ud", h, to_ud)
                w_in_head(w0 + 8)
                act.wait_ge(conf_ready, NB * GC * (h + 1))
                each_block("cg", h, to_gated(ACT.Copy))
                each_block("pool", h, to_pool_stage)
                if h == 0:
                    w_in_head(NI)
                    w_in_head(NI + 1)
                    modulate(HT, h_tmp, gain1, shift1)
                    act.wait_ge(*used(NI - 1))
                    h_head(HT, h_tmp)
                else:
                    ln_square(1, 0)
                    ln_root(1, 0)
                    ln_silu(1, 0)

            def split_head(n, a):
                hi, lo = heads_tails(a)
                if a == 0:
                    act.wait_ge(qk_ld[n % 2], 16 * (n // 2 + 1))
                if n:
                    act.wait_ge(x_fill, FILL_NO["stack", n - 1, 2 * a + 1] + 1)
                src = qk_in[n % 2][:, a, :].rearrange("p (m o d) -> p m o d", o=1, d=QKD).to_broadcast([P, MAPS, 2, QKD])
                A(hi, src, ACT.Copy).then_inc(split_hi, 1)

            def read_fill(x):
                kind, i, f = FILLS[x]
                if kind == "ln":
                    if f:
                        ln_root(1, 1)
                    return
                act.wait_ge(x_fill, x + 1)
                if kind == "stack":
                    m0, src = 4 * (f % 2), psum[:, 7, :].rearrange("p (m t) -> p m t", m=4)
                    dst = q_stack[i % 2][:, m0:m0 + 4, :] if f < 2 else k_stack[:, m0:m0 + 4, i * P:(i + 1) * P]
                else:
                    if i >= 2 and f == 0:
                        act.wait_ge(attt_st[i % 2], 16)
                    src, dst = psum[:, 7, :], att_t[i % 2][:, f, :]
                A(dst, src, ACT.Copy).then_inc(x_read, 1)

            def exps(u):
                i, s = u // HEADS, u % 3
                n = (i + 1) * P
                act.wait_ge(max_ready, u + 1)
                for m in range(2):
                    A(prob(u, m, 0, n), prob(u, m, 0, n), ACT.Exp, scale=SCALE, bias=bst[:, s, 10 + m:11 + m],
                      accum_out=bst[:, s, 12 + m:13 + m]).then_inc(exp_done, 1)

            def read_at(u, part):
                if not 0 <= u < UNITS:
                    return
                for g, (k0, nk) in list(enumerate(at_groups(u)))[part]:
                    gn = AT_NO[u] + g
                    act.wait_ge(at_mm, gn + 1)
                    if gn >= 2:
                        act.wait_ge(pv_mm, gn - 1)
                    A(a_t[gn % 2][:, 0:nk * P], psum[:, 4 + gn % 2, 0:nk * P], ACT.Copy).then_inc(at_ready, 1)

            def wo_head(hc, i, before):
                w_head(2 * NI + hc * C_ITEMS + i, wo_slot(hc, i), wo_loaded(hc, i), before, wo_raw(hc, i))

            def mix_head(n):
                act.wait_ge(mix_ld[n % 2], 16 * (n // 2 + 1))
                t = n % HT
                A(h_hi[:, :, t * P:(t + 1) * P], mix_buf(n)[:, :, :], ACT.Copy).then_inc(mixhi_ready, 1)

            act.wait_ge(mod2_ready, 2)
            split_head(0, 0)
            split_head(0, 1)
            act.wait_ge(proj_ready, len(OUTS))
            for x in range(4):
                read_fill(x)
            for u in range(STEPS):
                for n, a in splits_at(u):
                    split_head(n, a)
                if u == LN_STEP + 1:
                    ln_square(1, 1)
                if u == LN_STEP + 4:
                    ln_silu(1, 1)
                for x in fills_at(u):
                    read_fill(x)
                read_at(u - 2, slice(0, 2))
                if 0 <= u - 1 < UNITS:
                    exps(u - 1)
                read_at(u - 2, slice(2, 4))
                j = att_stage(u, 1)
                if j is not None:
                    act.wait_ge(ams_ready, j + 1)
                    A(ams[:, 16:32], ams[:, 0:16], ACT.Sqrt, bias=eps_col, scale=1.0 / VD).then_inc(arms_ready, 1)
                if u == UNITS + 1:
                    act.wait_ge(sc_mm, SC_NO[UNITS])
                    mix_head(0)
                    mix_head(1)
                if u == UNITS + 4:
                    wo_head(0, 0, (at_mm, AT_NO[UNITS]))

            for hc in range(2):
                w0 = 2 * NI + hc * C_ITEMS
                n0 = hc * HT
                if hc == 0:
                    for i in (1, 2):
                        wo_head(0, i, (at_mm, AT_NO[UNITS]))
                    for q in range(2):
                        act.wait_ge(attt_st[q], 32)
                    wo_head(0, 3, None)
                else:
                    wo_head(1, 2, (ff1_mm, 4 * FG))
                    act.wait_ge(ff1_mm, 4 * FG)
                    mix_head(HT)
                    mix_head(HT + 1)
                    wo_head(1, 3, (ff2_mm, 16 * FG))
                for t in range(HT):
                    n = NT + n0 + t
                    if 2 <= t + 1 < HT:
                        mix_head(n0 + t + 1)
                    if t:
                        modulate(n - 1, h_tmp2, gain2, shift2)
                        h_head(n - 1, h_tmp2)
                    if t + 1 < HT:
                        rms_root(n)

                all_w_out = (wo_mm, 2 * (n0 + HT))

                def ff1_head(g, q, first=False):
                    w = 2 * g + (w0 + KC_OUT)
                    w_head(w, 2 * q, loaded(w),
                           all_w_out if first else (ff1_mm, 4 * g + (4 * FG * hc - 4)))

                def ff2_head(g, q, first=False):
                    w = 2 * g + (w0 + KC_OUT + 1)
                    w_head(w, 2 * q + 1, (w_folded, g + (hc * FG + 1)),
                           all_w_out if first else (ff2_mm, 16 * g + (16 * FG * hc - 16)))

                ff1_head(0, 0, True)
                rms_root(NT + n0 + HT - 1)
                modulate(NT + n0 + HT - 1, h_tmp2, gain2, shift2)
                h_head(NT + n0 + HT - 1, h_tmp2)
                ff2_head(0, 0, True)
                act.wait_ge(h_ready, NT + n0 + HT)

                def group(g, q, first=False, ahead=None):
                    if ahead is None:
                        ahead = (lambda: ff1_head(g + 1, 1 - q, first), lambda: ff2_head(g + 1, 1 - q, first))

                    def relu(f):
                        F = 4 * g + (4 * FG * hc + f)
                        act.wait_ge(ff1_mm, F + 1)
                        if not first:
                            act.wait_ge(u_ready, F - 3)
                        A(relu_t[f][:, :], psum[:, 2 + f % 2, :], ACT.Relu).then_inc(relu_ready, 1)

                    def u_head(f):
                        F = 4 * g + (4 * FG * hc + f)
                        b, j = f // 2, f % 2
                        act.wait_ge(sq_ready, F + 1)
                        if not first:
                            act.wait_ge(ff2_mm, 16 * g + (16 * FG * hc - 16 + 8 * b + 8))
                        A(u_hi[:, j, b * BLK:(b + 1) * BLK], relu_t[f][:, :], ACT.Copy).then_inc(uhi_ready, 1)

                    relu(0)
                    if not first:
                        ahead[0]()
                    u_head(0)
                    relu(1)
                    u_head(1)
                    relu(2)
                    u_head(2)
                    if not first:
                        ahead[1]()
                    relu(3)
                    u_head(3)
                    if first:
                        ahead[0]()
                        ahead[1]()

                group(0, 0, first=True)
                group(1, 1)
                with act.Fori(1, FG // 2 - 1) as it:
                    for q in range(2):
                        group(it * 2 + q, q)
                group(FG - 2, 0)
                before = (ff1_mm, 4 * FG - 4), (ff2_mm, 16 * FG - 16)
                group(FG - 1, 1, ahead=(lambda: hc or wo_head(1, 0, before[0]), lambda: hc or wo_head(1, 1, before[1])))

        @block.vector
        def _(dve):
            V = nc.vector
            links = [0]

            def mark(ins):
                links[0] += 1
                ins.then_inc(dve_chain, 1)
                return links[0]

            def link(ins):
                dve.wait_ge(dve_chain, mark(ins))

            def mean_square(n, src):
                s = 4 * (n % 2)
                V.bn_stats(bn[:, 0, :], src[:, 0:BLK])
                link(V.bn_stats(bn[:, 1, :], src[:, BLK:D]))
                link(V.bn_aggr(stat[:, s:s + 2], bn[:, :, :].rearrange("p a b -> p (a b)")))
                V.scalar_tensor_tensor(out=stat[:, s + 2:s + 3], in0=stat[:, s:s + 1], scalar=stat[:, s:s + 1],
                                       in1=stat[:, s + 1:s + 2], op0=ALU.mult, op1=ALU.add).then_inc(ms_ready, 1)

            def normalise(n, src, dst):
                s = 4 * (n % 2)
                dve.wait_ge(rms_ready, n + 1)
                link(V.reciprocal(stat[:, 8:9], stat[:, s + 3:s + 4]))
                V.tensor_scalar(dst, src, stat[:, 8:9], None, ALU.mult).then_inc(xn_ready, 1)

            def h_tail(n, tmp):
                t = n % HT
                dve.wait_ge(hhi_ready, n + 1)
                tok = slice(t * P, (t + 1) * P)
                V.tensor_tensor(out=h_lo[:, :, tok], in0=tmp[:, :, :], in1=f32(h_hi[:, :, tok]),
                                op=ALU.subtract).then_inc(h_ready, 1)

            def w_tail(w, s, raw=w_raw):
                dve.wait_ge(whi_ready, w + 1)
                V.tensor_tensor(out=w_lo[s][:, :], in0=raw[:, :], in1=f32(w_hi[s][:, :]),
                                op=ALU.subtract).then_inc(wlo_ready, 1)

            def w_in_tail(w):
                w_tail(w, w % 3)

            def w_fold(w):
                dve.wait_ge(*loaded(w))
                V.tensor_tensor(out=by_k2(w_raw[:, :]), in0=by_k2(w_raw[:, :]), op=ALU.mult,
                                in1=gate_row[:, 1:2, :].to_broadcast([P, 2, D])).then_inc(w_folded, 1)

            def columns(rows, n, tmp):
                blocks = tmp.rearrange("p (m c) -> p m c", c=P)
                link(V.tensor_tensor(out=blocks, in0=rows.rearrange("p a n -> p (a n)").rearrange("p (m c) -> p m c", c=P),
                                     in1=ident[:, :].rearrange("p (o c) -> p o c", o=1).to_broadcast([P, n, P]), op=ALU.mult))
                link(V.tensor_reduce(out=diag_sum[:, 0:n], in_=blocks, axis=AX.X, op=ALU.add))

            groups = [(cc, slice(64 * s, 64 * s + 64), 2 << (2 * cc + s)) for cc in range(GC) for s in range(2)]
            for cc, part, win in groups:
                V.memset(inv_win[part, cc:cc + 1], 1.0 / win)
                ins = V.memset(inv_first[part, cc, :], 1.0 / win)
            link(ins)
            for cc, part, win in groups:
                for t in range(win - 1):
                    V.memset(inv_first[part, cc, t:t + 1], 1.0 / (t + 1))

            dve.wait_ge(sigc_ready, 1)
            V.tensor_tensor(out=silu_c[:, :], in0=silu_c[:, :], in1=col1[:, R_C:R_B], op=ALU.mult).then_inc(siluc_ready, 1)
            dve.wait_ge(bc_ld, 16 * BROADCASTS)
            pairs = small[:, 32:96].rearrange("p (a d) -> p a d", d=QKD)
            link(V.tensor_tensor(out=pairs, in0=lam_in[:, 0:4:2, :], in1=lam_in[:, 1:4:2, :], op=ALU.mult))
            V.tensor_reduce(out=small[:, 4:6], in_=pairs, axis=AX.X, op=ALU.add).then_inc(lam_sums, 1)
            dve.wait_ge(lam_exp, 1)
            V.scalar_tensor_tensor(out=lam_neg, in0=small[:, 7:8], scalar=-LAM_INIT, in1=small[:, 6:7],
                                   op0=ALU.add, op1=ALU.subtract)
            V.tensor_scalar(gain_sub[:, :], gain_sub[:, :], 1.0 - LAM_INIT, None, ALU.mult)
            for n in range(2):
                dve.wait_ge(x_ld[n], 16)
                mean_square(n, x_in[n])
                normalise(n, x_in[n][:, :], x_in[n][:, :])
            w_in_tail(0)
            dve.wait_ge(mod1_mm, 1)
            columns(psum[:, 2:6, :], 2 * DC, ada_first[0][:, :])
            V.tensor_tensor(out=shift1[:, :], in0=diag_sum[:, 0:DC], in1=col1[:, R_B:R_B + 8], op=ALU.add)
            link(V.tensor_tensor(out=gain1[:, :], in0=diag_sum[:, DC:2 * DC], in1=col1[:, R_B + 8:R_B + 16], op=ALU.add))
            V.scalar_tensor_tensor(out=gain1[:, :], in0=gain1[:, :], scalar=1.0, in1=col1[:, R_N1:R_N2],
                                   op0=ALU.add, op1=ALU.mult).then_inc(mod1_ready, 1)
            V.memset(conf[:, :, 0:TAPS - 1], 0.0)
            V.memset(ud[:, :, 0:POOL_HALO], 0.0)
            link(V.memset(halo2[:, :, :], 0.0))
            h_tail(0, h_tmp)
            w_in_tail(1)

            def qk_sums(n):
                dve.wait_ge(qsq_ready, n + 1)
                V.tensor_reduce(out=small[:, 32:48], in_=qk_sq[:, :].rearrange("p (a d) -> p a d", d=QKD),
                                axis=AX.X, op=ALU.add).then_inc(qss_ready, 1)

            def qk_normalise(n):
                s = slot_of_qk(n)
                dve.wait_ge(qrms_ready, n + 1)
                link(V.reciprocal(small[:, 64:80], small[:, 48:64]))
                if stores_before_qk(n):
                    dve.wait_ge(qkv_st[s], 16 * stores_before_qk(n))
                r = small[:, 64:80].rearrange("p (a o) -> p a o", o=1).to_broadcast([P, 2 * MAPS, QKD])
                V.tensor_tensor(out=qkv_out[s][:, :].rearrange("p (a d) -> p a d", d=QKD),
                                in0=bank(OUT_NO["qk", n // HT, n % HT, 0]).rearrange("p (a d) -> p a d", d=QKD),
                                in1=r, op=ALU.mult).then_inc(qn_ready, 1)

            def conv_taps(h):
                for b in range(NB):
                    marks = []
                    dve.wait_ge(conf_ready, NB * GC * h + GC * (b + 1))
                    for j in range(TAPS):
                        for cc in range(GC):
                            w = col2[:, R_DWW + GC * j + cc:R_DWW + GC * j + cc + 1]
                            src, dst = conf[:, cc, b * BLK + j:b * BLK + j + BLK], acc[:, cc, b * BLK:(b + 1) * BLK]
                            if j == 0:
                                if h and cc == 0:
                                    dve.wait_ge(ln_st[b], 16)
                                ins = V.tensor_scalar(dst, src, w, col1[:, R_DWB + cc:R_DWB + cc + 1], ALU.mult, ALU.add)
                            else:
                                dve.wait_ge(dve_chain, marks[-GC])
                                ins = V.scalar_tensor_tensor(out=dst, in0=src, scalar=w, in1=dst, op0=ALU.mult, op1=ALU.add)
                            if j == TAPS - 1 and cc == GC - 1:
                                ins.then_inc(conv_ready, 1)
                            else:
                                marks.append(mark(ins))
                            yield
                dve.wait_ge(conv_ready, NB * (h + 1))
                link(V.tensor_copy(conf[:, :, 0:TAPS - 1], conf[:, :, HALF:HALF + TAPS - 1]))

            def pump(taps, n):
                for _ in range(n):
                    next(taps, None)

            def ln_sub(h, b):
                blk, mean = slice(b * BLK, (b + 1) * BLK), ln_bank(h, b, 0)
                dve.wait_ge(*ln_summed(h, b, 0))
                V.tensor_tensor(out=acc[:, 0, blk], in0=acc[:, 0, blk], in1=mean, op=ALU.subtract)
                V.tensor_tensor(out=acc[:, 1, blk], in0=acc[:, 1, blk], in1=mean,
                                op=ALU.subtract).then_inc(ln_read(h, b, 0)[0], 1)

            def ln_scale(h, b):
                blk, rs = slice(b * BLK, (b + 1) * BLK), ln_rs[h][:, :]
                dve.wait_ge(*ln_read(h, b, 1))
                link(V.reciprocal(rs, rs))
                V.tensor_tensor(out=acc[:, 0, blk], in0=acc[:, 0, blk], in1=rs, op=ALU.mult)
                V.tensor_tensor(out=acc[:, 1, blk], in0=acc[:, 1, blk], in1=rs, op=ALU.mult).then_inc(lnz_ready, 1)

            def pooled(h, cc, b):
                n = chan_no(h, cc, b)
                dve.wait_ge(win_ready, n + 1)
                y = pool_in[:, cc, b * BLK:(b + 1) * BLK]
                first = POOL_HALO if h == b == 0 else 0
                for part, win in ((slice(0, 64), win_a), (slice(64, P), win_b)):
                    if first:
                        link(V.tensor_tensor(out=win[part, POOL_HALO:2 * POOL_HALO], in0=win[part, POOL_HALO:2 * POOL_HALO],
                                             in1=inv_first[part, cc, :], op=ALU.mult))
                        V.tensor_tensor(out=y[part, 0:first], in0=win[part, POOL_HALO:2 * POOL_HALO],
                                        in1=ud[part, cc, POOL_HALO:2 * POOL_HALO], op=ALU.subtract)
                    last = V.scalar_tensor_tensor(out=y[part, first:BLK], in0=win[part, POOL_HALO + first:],
                                                  scalar=inv_win[part, cc:cc + 1], in1=ud[part, cc, POOL_HALO + first:],
                                                  op0=ALU.mult, op1=ALU.subtract)
                last.then_inc(pool_y, 1)
                dve.wait_ge(pool_y, n + 1)
                V.tensor_copy(ud[:, cc, 0:POOL_HALO], ud[:, cc, BLK:BLK + POOL_HALO]).then_inc(halo_saved, 1)

            def in_prod(h, cc, b):
                o = OUT_NO["xc", h, cc, b]
                dve.wait_ge(proj_ready, o + 1)
                dve.wait_ge(gated_ready, (2 * h + 1) * NB * GC + GC * b + cc + 1)
                V.tensor_tensor(out=prod[:, cc, STAPS - 1 + b * BLK:STAPS - 1 + (b + 1) * BLK], in0=bank(o),
                                in1=gated[:, cc, b * BLK:(b + 1) * BLK], op=ALU.mult).then_inc(prod_ready, 1)

            def short(h, cc, b):
                n = chan_no(h, cc, b)
                y = stage[n % 2][:, :]
                dve.wait_ge(stage_st[n % 2], 16 * stores_of_stage(n, True))
                for j in range(STAPS):
                    w = col2[:, R_SW + GC * j + cc:R_SW + GC * j + cc + 1]
                    src = prod[:, cc, b * BLK + j:b * BLK + j + BLK]
                    if j == 0:
                        link(V.tensor_scalar(y, src, w, None, ALU.mult))
                    else:
                        link(V.scalar_tensor_tensor(out=y, in0=src, scalar=w, in1=y, op0=ALU.mult, op1=ALU.add))
                o = OUT_NO["bg", h, cc, b]
                dve.wait_ge(proj_ready, o + 1)
                V.tensor_tensor(out=y, in0=y, in1=bank(o), op=ALU.mult).then_inc(short_ready, 1)

            def read_norm_vector(h):
                dve.wait_ge(mod2_mm, 2 * h + 1)
                columns(psum[:, 0:2, :], DC, h_tmp[:, :, :].rearrange("p k t -> p (k t)"))
                r = R_B + (3 + h) * DC
                vector = V.scalar_tensor_tensor(out=(gain2 if h else shift2)[:, :], in0=diag_sum[:, 0:DC], scalar=float(GW),
                                                in1=col1[:, r:r + DC], op0=ALU.mult, op1=ALU.add)
                if h:
                    link(vector)
                    vector = V.scalar_tensor_tensor(out=gain2[:, :], in0=gain2[:, :], scalar=1.0, in1=col1[:, R_N2:R_DWB],
                                                    op0=ALU.add, op1=ALU.mult)
                vector.then_inc(norm_read, 1)

            def read_gate(h):
                dve.wait_ge(mod2_mm, 2 * h + 2)
                dve.wait_ge(bias_ld, 16 * (h + 1))
                V.scalar_tensor_tensor(out=gate_row[:, h, :], in0=psum[:, 0:2, :].rearrange("p a n -> p (a n)"),
                                       scalar=float(GW), in1=ada[:, 0:D], op0=ALU.mult, op1=ALU.add).then_inc(mod2_ready, 1)

            taps = iter(())
            blocks = [(cc, b) for b in range(NB) for cc in range(GC)]
            for h in range(2):
                w0 = h * NI
                for t in range(HT):
                    n = h * HT + t
                    if n + 2 < NT:
                        dve.wait_ge(x_ld[n % 2], 16 * ((n + 2) // 2 + 1))
                        mean_square(n + 2, x_in[n % 2])
                    if t + 1 < HT:
                        h_tail(n + 1, h_tmp)
                    if n + 2 < NT:
                        normalise(n + 2, x_in[n % 2][:, :], x_in[n % 2][:, :])
                    if t:
                        qk_sums(n - 1)
                        qk_normalise(n - 1)
                    if t == 0:
                        w_in_tail(w0 + 2)
                    pump(taps, 4)
                w_in_tail(w0 + 3)
                qk_sums(h * HT + HT - 1)
                qk_normalise(h * HT + HT - 1)
                w_in_tail(w0 + 4)
                pump(taps, 9 * TAPS)
                if h:
                    ln_sub(0, 0)
                w_in_tail(w0 + 5)
                if h:
                    ln_scale(0, 0)
                w_in_tail(w0 + 6)
                if h:
                    ln_sub(0, 1)
                for cc, b in blocks:
                    blk = slice(b * BLK, (b + 1) * BLK)
                    o = OUT_NO["val", h, cc, b]
                    dve.wait_ge(proj_ready, o + 1)
                    dve.wait_ge(gated_ready, 2 * h * NB * GC + GC * b + cc + 1)
                    V.tensor_tensor(out=conf[:, cc, TAPS - 1 + b * BLK:TAPS - 1 + (b + 1) * BLK], in0=bank(o),
                                    in1=gated[:, cc, blk], op=ALU.mult).then_inc(conf_ready, 1)
                    if (cc, b) == (GC - 1, 0):
                        taps = conv_taps(h)
                    if b or cc == GC - 1:
                        pump(taps, 6)
                    if h and (cc, b) == (GC - 1, 0):
                        ln_scale(0, 1)
                w_in_tail(w0 + 7)
                pump(taps, 16)
                read_norm_vector(h)
                for cc, b in blocks:
                    if (cc, b) == (0, 1):
                        w_in_tail(w0 + 8)
                    pooled(h, cc, b)
                    pump(taps, 4)
                read_gate(h)
                dve.wait_ge(proj_ready, OUT_NO["pool", h, GC - 1, NB - 1] + 1)
                link(V.tensor_copy(prod[:, :, 0:STAPS - 1], halo2[:, :, :]))
                for cc, b in blocks:
                    in_prod(h, cc, b)
                    if h == 0 and cc == b == 0:
                        w_in_tail(NI)
                    pump(taps, 7)
                dve.wait_ge(prod_ready, NB * GC * (h + 1))
                if h:
                    ln_sub(1, 0)
                for cc, b in blocks:
                    short(h, cc, b)
                    if h == 0 and cc == b == 0:
                        w_in_tail(NI + 1)
                    if h or (cc, b) != blocks[-1]:
                        pump(taps, 3)
                    if h and (cc, b) == (GC - 1, 0):
                        ln_scale(1, 0)
                if h == 0:
                    h_tail(HT, h_tmp)
                    link(V.tensor_copy(halo2[:, :, :], prod[:, :, HALF:HALF + STAPS - 1]))

            dve.wait_ge(proj_ready, len(OUTS))

            def read_scores(u):
                i, s = u // HEADS, u % 3
                nch = len(sc_chunks(i))
                if u >= 3:
                    dve.wait_ge(at_mm, AT_NO[u - 2])
                for m in range(2):
                    for ch, (c0, n) in enumerate(sc_chunks(i)):
                        r = SC_NO[u] + m * nch + ch
                        dve.wait_ge(sc_mm, r + 1)
                        V.tensor_scalar(prob(u, m, c0, n), psum[:, r % 4, 0:n], 1.0, None, ALU.mult, ALU.max,
                                        accum_out=bst[:, s, 4 * m + ch:4 * m + ch + 1]).then_inc(sc_read, 1)
                dve.wait_ge(sc_read, SC_NO[u + 1])
                link(V.tensor_reduce(out=bst[:, s, 8:10], axis=AX.X, op=ALU.max,
                                     in_=bst[:, s, 0:8].rearrange("p (m c) -> p m c", m=2)[:, :, 0:nch]))
                V.tensor_scalar(bst[:, s, 10:12], bst[:, s, 8:10], -SCALE, None, ALU.mult).then_inc(max_ready, 1)

            def combine(u):
                i, s = u // HEADS, u % 3
                n = (i + 1) * P
                dve.wait_ge(exp_done, 2 * (u + 1))
                link(V.reciprocal(bst[:, s, 14:16], bst[:, s, 12:14]))
                link(V.scalar_tensor_tensor(out=bst[:, s, 16:17], in0=bst[:, s, 12:13], scalar=bst[:, s, 15:16],
                                            in1=lam_neg, op0=ALU.mult, op1=ALU.mult))
                V.scalar_tensor_tensor(out=prob(u, 0, 0, n), in0=prob(u, 1, 0, n), scalar=bst[:, s, 16:17],
                                       in1=prob(u, 0, 0, n), op0=ALU.mult, op1=ALU.add).then_inc(a_ready, 1)
                link(V.tensor_copy(inv_s[:, u % 4:u % 4 + 1], bst[:, s, 14:15]))

            def read_o(u):
                i, hd = u // HEADS, u % HEADS
                dve.wait_ge(pv_mm, AT_NO[u + 1])
                V.tensor_scalar(att[:, i, hd * VD:(hd + 1) * VD], psum[:, 6, 0:VD],
                                inv_s[:, u % 4:u % 4 + 1], None, ALU.mult).then_inc(o_read, 1)

            def mix_tail(n):
                tok = slice(n % HT * P, (n % HT + 1) * P)
                dve.wait_ge(mixhi_ready, n + 1)
                V.tensor_tensor(out=h_lo[:, :, tok], in0=mix_buf(n)[:, :, :], in1=f32(h_hi[:, :, tok]),
                                op=ALU.subtract).then_inc(mix_ready, 1)

            def wo_tail(hc, i):
                w_tail(2 * NI + hc * C_ITEMS + i, wo_slot(hc, i), wo_raw(hc, i))

            for u in range(STEPS):
                if u == NT // 2 * HEADS:
                    for b in range(NB):
                        dve.wait_ge(ln_st[b], 32)
                if 0 <= u - 3 < UNITS:
                    read_o(u - 3)
                if u < UNITS:
                    read_scores(u)
                if 0 <= u - 1 < UNITS:
                    combine(u - 1)
                pump(taps, 4 if u < 6 else 9 * TAPS)
                if u == LN_STEP:
                    ln_sub(1, 1)
                if u == LN_STEP + 3:
                    ln_scale(1, 1)
                j = att_stage(u, 1)
                if j is not None:
                    dve.wait_ge(asq_ready, j + 1)
                    V.tensor_reduce(out=ams[:, 0:16], in_=att_sq[:, :, :].rearrange("p i (a d) -> p (i a) d", d=VD),
                                    axis=AX.X, op=ALU.add).then_inc(ams_ready, 1)
                j = att_stage(u, 2)
                if j is not None:
                    dve.wait_ge(arms_ready, j + 1)
                    V.reciprocal(ams[:, 32:48], ams[:, 16:32]).then_inc(arcp_ready, 1)
                    if j == NT // 4 - 1:
                        dve.wait_ge(arcp_ready, j + 1)
                        y, root, gain = att_scaling(j)
                        link(V.tensor_tensor(out=y, in0=y, in1=root, op=ALU.mult))
                        V.tensor_tensor(out=y, in0=y, in1=gain, op=ALU.mult).then_inc(att_ready, 1)
                if u == UNITS + 1:
                    mix_tail(0)
                    mix_tail(1)
                if u == UNITS + 4:
                    wo_tail(0, 0)

            for hc in range(2):
                w0 = 2 * NI + hc * C_ITEMS
                n0 = hc * HT

                if hc == 0:
                    for i in (1, 2, 3):
                        wo_tail(0, i)
                for t in range(HT):
                    n = n0 + t
                    if 2 <= t + 1 < HT:
                        mix_tail(n + 1)
                    dve.wait_ge(xr_ld, 16 * (n + 1))
                    for cb in range(2):
                        o, col = 2 * n + cb, slice(cb * BLK, (cb + 1) * BLK)
                        y = x_new[:, t, col]
                        dve.wait_ge(wo_mm, o + 1)
                        V.tensor_tensor(out=wo_gated[:, :], in0=psum[:, 4 + o % 4, :], in1=gate_row[:, 0, col],
                                        op=ALU.mult).then_inc(wo_read, 1)
                        dve.wait_ge(wo_read, o + 1)
                        link(V.tensor_tensor(out=y, in0=y, in1=wo_gated[:, :], op=ALU.add))
                        if t and cb == 0:
                            h_tail(NT + n - 1, h_tmp2)
                    if t == HT - 1:
                        w_tail(w0 + KC_OUT, 0)
                    mean_square(NT + n, x_new[:, t, :])
                    if t:
                        dve.wait_ge(xt_ready, NT + n)
                    normalise(NT + n, x_new[:, t, :], xn2[:, :])

                def ff1_tail(g, q):
                    w_tail(2 * g + (w0 + KC_OUT), 2 * q)

                def ff2_fold(g):
                    w_fold(2 * g + (w0 + KC_OUT + 1))

                def ff2_tail(g, q):
                    w_tail(2 * g + (w0 + KC_OUT + 1), 2 * q + 1)

                ff2_fold(0)
                h_tail(NT + n0 + HT - 1, h_tmp2)
                ff2_tail(0, 0)

                def group(g, q, first=False, last=False):
                    def square(f):
                        dve.wait_ge(relu_ready, 4 * g + (4 * FG * hc + f + 1))
                        V.tensor_tensor(out=relu_t[f][:, :], in0=relu_t[f][:, :], in1=relu_t[f][:, :],
                                        op=ALU.mult).then_inc(sq_ready, 1)

                    def u_tail(f):
                        b, j = f // 2, f % 2
                        blk = slice(b * BLK, (b + 1) * BLK)
                        dve.wait_ge(uhi_ready, 4 * g + (4 * FG * hc + f + 1))
                        V.tensor_tensor(out=u_lo[:, j, blk], in0=relu_t[f][:, :], in1=f32(u_hi[:, j, blk]),
                                        op=ALU.subtract).then_inc(u_ready, 1)

                    def accumulate(q0):
                        for o in range(q0, q0 + 8):
                            t, cb = o // 2, o % 2
                            y = x_new[:, t, cb * BLK:(cb + 1) * BLK]
                            dve.wait_ge(ff2_mm, 16 * g + (16 * FG * hc + o + 1))
                            V.tensor_tensor(out=y, in0=y, in1=psum[:, 4 + o % 4, :], op=ALU.add).then_inc(ff2_read, 1)

                    square(0)
                    if not last and not first:
                        ff1_tail(g + 1, 1 - q)
                    elif last and hc == 0:
                        wo_tail(1, 0)
                    u_tail(0)
                    square(1)
                    u_tail(1)
                    square(2)
                    if not last and not first:
                        ff2_fold(g + 1)
                    u_tail(2)
                    square(3)
                    u_tail(3)
                    if first:
                        ff1_tail(g + 1, 1 - q)
                    if last and hc == 0:
                        wo_tail(1, 1)
                    accumulate(0)
                    if first:
                        ff2_fold(g + 1)
                    if not last:
                        ff2_tail(g + 1, 1 - q)
                    elif hc == 0:
                        wo_tail(1, 2)
                        mix_tail(HT)
                        mix_tail(HT + 1)
                    accumulate(8)
                    if last and hc == 0:
                        wo_tail(1, 3)

                group(0, 0, first=True)
                group(1, 1)
                with dve.Fori(1, FG // 2 - 1) as it:
                    for q in range(2):
                        group(it * 2 + q, q)
                group(FG - 2, 0)
                group(FG - 1, 1, last=True)

        @block.tensor
        def _(pe):
            M = nc.tensor.matmul

            def mm3(dst, terms):
                last = len(terms) - 1
                for n, (ah, al, bh, bl) in enumerate(terms):
                    M(dst, ah, bh, start=(n == 0), stop=False)
                    M(dst, ah, bl, start=False, stop=False)
                    ins = M(dst, al, bh, start=False, stop=(n == last))
                return ins

            def transposes(n, src):
                pe.wait_ge(xn_ready, n + 1)
                if n:
                    pe.wait_ge(hmod_ready, n)
                for k in range(DC):
                    ins = nc.tensor.transpose(ps_t[:, k, :], src[:, k * P:(k + 1) * P], ident[:, :])
                ins.then_inc(xt_ready, 1)

            pe.wait_ge(const_ready, 1)
            pe.wait_ge(tab_ld, 16 * 10)
            nc.tensor.transpose(psum[:, 0, 0:R_END1], table1[:, :], ident[0:R_END1, 0:R_END1])
            nc.tensor.transpose(psum[:, 1, 0:R_END2], table2[:, :], ident[0:R_END2, 0:R_END2]).then_inc(tab_t, 1)
            pe.wait_ge(siluc_ready, 1)
            for k in range(DC):
                pe.wait_ge(ada0_ld[k % 4], 16 * (k // 4 + 1))
                for m in range(4):
                    ins = M(psum[:, 2 + m, :], silu_c[:, k:k + 1].to_broadcast([P, P]), ada_first[k % 4][:, m * BLK:(m + 1) * BLK],
                            start=(k == 0), stop=(k == DC - 1), skip_group_check=True)
                ins.then_inc(ada0_used if k < DC - 1 else mod1_mm, 1)
            pe.wait_ge(tab_col, 2)
            transposes(0, x_in[0])

            def free(o):
                if o >= RING:
                    pe.wait_ge(*released(o - RING))

            def item_ready(w):
                pe.wait_ge(wlo_ready, w + 1)

            def w8(w, part):
                return by_k8(part[w % 3][:, :])

            def project_rows(h, t, w, dst):
                tok = slice(t * P, (t + 1) * P)
                wh, wl = w8(w, w_hi), w8(w, w_lo)
                return mm3(dst, [(h_hi[:, k, tok], h_lo[:, k, tok], wh[:, k, :], wl[:, k, :]) for k in range(DC)])

            def project_cols(kind, h, w, middle=lambda: None):
                layer_norm(kind, h, 0)
                item_ready(w)
                wh, wl = w8(w, w_hi), w8(w, w_lo)
                for b in range(NB):
                    if b:
                        middle()
                        layer_norm(kind, h, 1)
                    for cc in range(GC):
                        o = OUT_NO[kind, h, cc, b]
                        free(o)
                        col, tok = slice(cc * P, (cc + 1) * P), slice(b * BLK, (b + 1) * BLK)
                        ins = mm3(bank(o), [(wh[:, k, col], wl[:, k, col], h_hi[:, k, tok], h_lo[:, k, tok])
                                            for k in range(DC)])
                        ins.then_inc(proj_ready, 1)

            def modulation(h, s):
                if s:
                    pe.wait_ge(norm_read, h + 1)
                else:
                    pe.wait_ge(ada_used, (h + 1) * DC)
                for n in range(2):
                    ins = M(psum[:, n, :], ones_mean[:, :], mod_sums(h)[1 - s][:, n * BLK:(n + 1) * BLK], start=True, stop=True)
                ins.then_inc(mod2_mm, 1)

            def ln_sum(h, b, s):
                if s:
                    pe.wait_ge(lnsq_ready, h * NB + b + 1)
                else:
                    pe.wait_ge(conv_ready, h * NB + b + 1)
                for cc in range(GC):
                    src = ln_sq[h][:, cc, :] if s else acc[:, cc, b * BLK:(b + 1) * BLK]
                    ins = M(ln_bank(h, b, s), ones_mean[:, :], src, start=(cc == 0), stop=(cc == GC - 1))
                return ins

            def layer_norm(kind, h, s):
                if h and kind in LN_AT:
                    free(OUT_NO[("ln",) + LN_AT[kind] + (s,)])
                    ln_sum(*LN_AT[kind], s).then_inc(proj_ready, 1)

            def project_v(h, t):
                o = OUT_NO["v", h, t // 2 * 2, 0]
                if t % 2 == 0:
                    free(o)
                return project_rows(h, t, h * NI + 2, bank(o)[:, t % 2 * GW:(t % 2 + 1) * GW])

            def next_tile():
                pe.wait_ge(mod2_ready, 1)
                transposes(HT, x_in[HT % 2])

            for h in range(2):
                w0 = h * NI
                for t in range(HT):
                    n = h * HT + t
                    if t + 1 < HT:
                        transposes(n + 1, x_in[(n + 1) % 2])
                    o = OUT_NO["qk", h, t, 0]
                    pe.wait_ge(h_ready, n + 1)
                    free(o)
                    item_ready(w0)
                    project_rows(h, t, w0, bank(o)[:, 0:GW])
                    item_ready(w0 + 1)
                    project_rows(h, t, w0 + 1, bank(o)[:, GW:2 * GW]).then_inc(proj_ready, 1)
                    if t == 1:
                        item_ready(w0 + 2)
                    if t in (1, HT - 1):
                        project_v(h, t - 1)
                    if t and t != HT - 2:
                        ins = project_v(h, t)
                        if t % 2:
                            ins.then_inc(proj_ready, 1)
                for i, kind in enumerate(("gate", "val", "ud", "cg")):
                    project_cols(kind, h, w0 + 3 + i, (lambda: modulation(h, 1)) if kind == "cg" else (lambda: None))
                    if kind == "ud":
                        modulation(h, 0)
                for b in range(NB):
                    for cc in range(GC):
                        o = OUT_NO["pool", h, cc, b]
                        free(o)
                        pe.wait_ge(pool_y, chan_no(h, cc, b) + 1)
                        if h == 0 and b == 0 and cc == 0:
                            pe.wait_ge(bc_ld, 16 * BROADCASTS)
                        M(bank(o), pool_blk[:, cc, :], pool_in[:, cc, b * BLK:(b + 1) * BLK],
                          start=True, stop=True).then_inc(proj_ready, 1)
                project_cols("xc", h, w0 + 7)
                project_cols("bg", h, w0 + 8, (lambda: None) if h else next_tile)

            pe.wait_ge(*released(max(o for o in range(len(OUTS)) if o % RING == 5)))
            pe.wait_ge(mod2_ready, 2)
            pe.wait_ge(hmod_ready, NT)

            def fill(x):
                kind, i, f = FILLS[x]
                if x:
                    pe.wait_ge(x_read, x)
                if kind == "ln":
                    ln_sum(1, 1, f).then_inc(x_fill, 1)
                    return
                if kind == "stack":
                    a = f // 2
                    pe.wait_ge(split_lo, 2 * i + a + 1)
                    src = f32((k_split if a else q_split)[:, :, :, :]).rearrange("p m s d -> p m (s d)")
                    srcs = [src[:, 4 * (f % 2) + m, :] for m in range(4)]
                else:
                    pe.wait_ge(att_ready, i + 1)
                    srcs = [att[:, 4 * i + t, f * P:(f + 1) * P] for t in range(4)]
                for m, s in enumerate(srcs):
                    ins = nc.tensor.transpose(psum[:, 7, m * P:(m + 1) * P], s, ident[:, :])
                ins.then_inc(x_fill, 1)

            def score(u, between):
                i, hd = u // HEADS, u % HEADS
                if hd == 0:
                    pe.wait_ge(x_read, FILL_NO["stack", i, 3] + 1)
                r = SC_NO[u]
                for m in range(2):
                    for c0, n in sc_chunks(i):
                        if r == SC_NO[u] + 1:
                            next(between, None)
                        if r >= 4:
                            pe.wait_ge(sc_read, r - 3)
                        diag = c0 + n == (i + 1) * P
                        ins = M(psum[:, r % 4, 0:n], q_stack[i % 2][:, 2 * hd + m, :], k_stack[:, 2 * hd + m, c0:c0 + n],
                                start=True, stop=not diag, skip_group_check=diag)
                        if diag:
                            ins = M(psum[:, r % 4, n - P:n], ident_r[:, :], mask_r[:, :], start=False, stop=True,
                                    skip_group_check=True)
                        ins.then_inc(sc_mm, 1)
                        r += 1

            def attend(u):
                if not 0 <= u < UNITS:
                    return
                i, hd = u // HEADS, u % HEADS
                s = u % 3
                pe.wait_ge(a_ready, u + 1)
                groups = at_groups(u)
                if u == 0:
                    pe.wait_ge(v_ld, 16)

                def turn(g):
                    gn, (k0, nk) = AT_NO[u] + g, groups[g]
                    if gn >= 2:
                        pe.wait_ge(at_ready, gn - 1)
                    for k in range(nk):
                        ins = nc.tensor.transpose(psum[:, 4 + gn % 2, k * P:(k + 1) * P],
                                                  prob(u, 0, (k0 + k) * P, P), ident[:, :])
                    ins.then_inc(at_mm, 1)

                def product(g):
                    gn, (k0, nk) = AT_NO[u] + g, groups[g]
                    pe.wait_ge(at_ready, gn + 1)
                    if g == 0 and u:
                        pe.wait_ge(o_read, u)
                    for k in range(nk):
                        ins = M(psum[:, 6, 0:VD], a_t[gn % 2][:, k * P:(k + 1) * P],
                                v_sb[:, k0 + k, hd * VD:(hd + 1) * VD], start=(k0 + k == 0), stop=(k0 + k == i))
                    ins.then_inc(pv_mm, 1)

                last = len(groups) - 1
                turn(0)
                if last:
                    turn(1)
                yield
                for g in range(last + 1):
                    product(g)
                    if g + 2 <= last:
                        turn(g + 2)
                    yield

            for x in range(4):
                fill(x)
            for o in range(len(OUTS) - RING, len(OUTS)):
                pe.wait_ge(*released(o))
            for u in range(STEPS):
                for x in fills_at(u):
                    fill(x)
                pieces = attend(u - 2)
                if u < UNITS:
                    score(u, pieces)
                for _ in pieces:
                    pass

            pe.wait_ge(x_read, len(FILLS))
            pe.wait_ge(o_read, UNITS)
            pe.wait_ge(sc_read, SC_NO[UNITS])
            pe.wait_ge(at_ready, AT_NO[UNITS])
            for hc in range(2):
                w0 = 2 * NI + hc * C_ITEMS
                n0 = hc * HT
                for t in range(HT):
                    n, tok = n0 + t, slice(t * P, (t + 1) * P)
                    pe.wait_ge(mix_ready, n + 1)
                    for cb in range(2):
                        if cb and t:
                            transposes(NT + n - 1, xn2)
                        o, col = 2 * n + cb, slice(cb * BLK, (cb + 1) * BLK)
                        if t >= 2:
                            pe.wait_ge(wo_read, o - 3)
                        elif hc:
                            pe.wait_ge(ff2_read, FG * 2 * HT - 3 + 2 * t + cb)
                        for i in range(KC_OUT):
                            if t == 0 and cb == 0:
                                item_ready(w0 + i)
                            slot = wo_slot(hc, i)
                            for kk in range(2):
                                k = 2 * i + kk
                                wh, wl = by_k2(w_hi[slot][:, :])[:, kk, col], by_k2(w_lo[slot][:, :])[:, kk, col]
                                M(psum[:, 4 + o % 4, :], h_hi[:, k, tok], wh, start=(k == 0), stop=False)
                                M(psum[:, 4 + o % 4, :], h_hi[:, k, tok], wl, start=False, stop=False)
                                ins = M(psum[:, 4 + o % 4, :], h_lo[:, k, tok], wh, start=False, stop=(k == DC - 1))
                        ins.then_inc(wo_mm, 1)

                def group(g, q, first=False):
                    w = 2 * g + (w0 + KC_OUT)
                    s1, s2 = 2 * q, 2 * q + 1
                    pe.wait_ge(wlo_ready, w + 1)
                    for b in range(NB):
                        for j in range(2):
                            f = 2 * b + j
                            if first and f == 1:
                                transposes(NT + n0 + HT - 1, xn2)
                            if not (first and b == 0):
                                pe.wait_ge(relu_ready, 4 * g + (4 * FG * hc + f - 1))
                            if first:
                                pe.wait_ge(h_ready, NT + n0 + 4 * (b + 1))
                            col, tok = slice(j * P, (j + 1) * P), slice(b * BLK, (b + 1) * BLK)
                            wh, wl = by_k8(w_hi[s1][:, :]), by_k8(w_lo[s1][:, :])
                            ins = mm3(psum[:, 2 + f % 2, :], [(wh[:, k, col], wl[:, k, col], h_hi[:, k, tok], h_lo[:, k, tok])
                                                              for k in range(DC)])
                            ins.then_inc(ff1_mm, 1)
                    pe.wait_ge(wlo_ready, w + 2)
                    wh, wl = by_k2(w_hi[s2][:, :]), by_k2(w_lo[s2][:, :])
                    for o in range(2 * HT):
                        t, cb = o // 2, o % 2
                        tok, col = slice(t * P, (t + 1) * P), slice(cb * BLK, (cb + 1) * BLK)
                        if o % 8 == 0:
                            pe.wait_ge(u_ready, 4 * g + (4 * FG * hc + o // 4 + 2))
                        if first and o < 4:
                            pe.wait_ge(wo_read, 2 * (n0 + HT) - 3 + o)
                        else:
                            pe.wait_ge(ff2_read, 16 * g + (16 * FG * hc + o - 3))
                        ins = mm3(psum[:, 4 + o % 4, :], [(u_hi[:, j, tok], u_lo[:, j, tok], wh[:, j, col], wl[:, j, col])
                                                          for j in range(2)])
                        ins.then_inc(ff2_mm, 1)

                group(0, 0, first=True)
                group(1, 1)
                with pe.Fori(1, FG // 2) as it:
                    for q in range(2):
                        group(it * 2 + q, q)


INPUTS = ["x", "c", "w_ada", "b_ada", "norm1_g", "norm2_g", "w_in", "w_out", "q_norm_g", "k_norm_g",
          "lam_params", "attn_sub_g", "conf_dw_w", "conf_dw_b", "conf_ln_g", "conf_ln_b", "short_conv_w",
          "pool_w", "pool_scale", "w_ff1", "w_ff2"]


def kernel(**inputs):
    import numpy as np
    import concourse.bacc as bacc
    from concourse.bass_utils import run_bass_kernel_spmd

    nc = bacc.Bacc("TRN2", target_bir_lowering=False, num_devices=1)
    arrays, args = {}, []
    for name in INPUTS:
        a = np.ascontiguousarray(inputs[name])
        arrays["in_" + name] = a
        args.append(nc.dram_tensor("in_" + name, a.shape, mybir.dt.from_np(a.dtype), kind="ExternalInput").ap())
    out = nc.dram_tensor("out", (1, SEQ, D), F32, kind="ExternalOutput").ap()
    trunk(nc, *args, out)
    r = run_bass_kernel_spmd(nc, [arrays], core_ids=[0])
    return r.results[0]["out"]
```
